# Optimizing a Trainium2 kernel written in Bass

```python
import math
import jax, jax.numpy as jnp
from jax import lax
import numpy as np

D_MODEL = 1024
BATCH = 1
SEQ = 256
DEPTH = 2

PL_DIM = 256
N_EVEN = (DEPTH + 1) // 2
N_ODD = DEPTH // 2
CONV_A_WIDTH = D_MODEL
CONV_A_KERNEL = 3
GDN_HEADS = 8
GDN_HEAD_DIM = 128
GDN_WIDTH = GDN_HEADS * GDN_HEAD_DIM
GDN_CONV_KERNEL = 4
GDN_CHUNK = 64
HGRN_HEAD_DIM = 128
HGRN_WIDTH = 2 * D_MODEL
HGRN_HEADS = HGRN_WIDTH // HGRN_HEAD_DIM
HGRN_CHUNK = 32
EVEN_IN = 4 * CONV_A_WIDTH + 4 * GDN_WIDTH + 2 * GDN_HEADS
EVEN_MIX = CONV_A_WIDTH + GDN_WIDTH
ODD_IN = 4 * HGRN_WIDTH
ODD_MIX = HGRN_WIDTH
DEEPNORM_ALPHA = (2.0 * DEPTH) ** 0.25
DEEPNORM_BETA = (8.0 * DEPTH) ** -0.25
NORM_EPS = 1e-5


def layer_norm(x, g, b):
    xf = x.astype(jnp.float32)
    mu = jnp.mean(xf, axis=-1, keepdims=True)
    var = jnp.mean(jnp.square(xf - mu), axis=-1, keepdims=True)
    return ((xf - mu) * lax.rsqrt(var + NORM_EPS) * g.astype(jnp.float32) + b.astype(jnp.float32)).astype(x.dtype)

def rms_norm(x, g):
    xf = x.astype(jnp.float32)
    y = xf * lax.rsqrt(jnp.mean(jnp.square(xf), axis=-1, keepdims=True) + NORM_EPS)
    return (y * g.astype(jnp.float32)).astype(x.dtype)

def l2_normalize(x):
    xf = x.astype(jnp.float32)
    return (xf * lax.rsqrt(jnp.sum(jnp.square(xf), axis=-1, keepdims=True) + 1e-6)).astype(x.dtype)

def causal_depthwise_conv(x, w):
    k, c = w.shape
    return lax.conv_general_dilated(
        x, w[:, None, :].astype(x.dtype), window_strides=(1,), padding=[(k - 1, 0)],
        dimension_numbers=("NWC", "WIO", "NWC"), feature_group_count=c)

def _to_chunks(t, c):
    b, s, h, d = t.shape
    return t.reshape(b, s // c, c, h, d).transpose(0, 3, 1, 2, 4)

def _from_chunks(t):
    b, h, n, c, d = t.shape
    return t.transpose(0, 2, 3, 1, 4).reshape(b, n * c, h, d)

def gated_delta_rule(q, k, v, g, beta):
    dtype = v.dtype
    c = GDN_CHUNK
    dk, dv = q.shape[-1], v.shape[-1]
    q = _to_chunks(q.astype(jnp.float32) * (dk ** -0.5), c)
    k = _to_chunks(k.astype(jnp.float32), c)
    v = _to_chunks(v.astype(jnp.float32), c)
    g = _to_chunks(g.astype(jnp.float32)[..., None], c)[..., 0]
    beta = _to_chunks(beta.astype(jnp.float32)[..., None], c)
    gc = jnp.cumsum(g, axis=-1)
    incl = jnp.tril(jnp.ones((c, c), bool))
    strict = jnp.tril(jnp.ones((c, c), bool), -1)
    decay = jnp.exp(jnp.where(incl, gc[..., :, None] - gc[..., None, :], -jnp.inf))
    kb = k * beta
    low = jnp.where(strict, jnp.einsum("bhnid,bhnjd->bhnij", kb, k) * decay, 0.0)
    rhs = jnp.concatenate([v * beta, kb * jnp.exp(gc)[..., None]], axis=-1)
    sol = lax.linalg.triangular_solve(low + jnp.eye(c, dtype=jnp.float32), rhs,
                                      left_side=True, lower=True, unit_diagonal=True)
    u, w = sol[..., :dv], sol[..., dv:]
    attn = jnp.einsum("bhnid,bhnjd->bhnij", q, k) * decay
    q_dec = q * jnp.exp(gc)[..., None]
    g_last = gc[..., -1]
    k_dec = k * jnp.exp(g_last[..., None] - gc)[..., None]

    def step(state, xs):
        q_i, k_i, u_i, w_i, a_i, gl_i = xs
        v_new = u_i - jnp.einsum("bhcd,bhde->bhce", w_i, state)
        o_i = jnp.einsum("bhcd,bhde->bhce", q_i, state) + jnp.einsum("bhij,bhje->bhie", a_i, v_new)
        state = state * jnp.exp(gl_i)[..., None, None] + jnp.einsum("bhcd,bhce->bhde", k_i, v_new)
        return state, o_i

    mv = lambda t: jnp.moveaxis(t, 2, 0)
    s0 = jnp.zeros(q.shape[:2] + (dk, dv), jnp.float32)
    _, o = lax.scan(step, s0, (mv(q_dec), mv(k_dec), mv(u), mv(w), mv(attn), mv(g_last)))
    return _from_chunks(jnp.moveaxis(o, 0, 2)).astype(dtype)

def hgrn2_recurrence(q, k, v, logf):
    dtype = v.dtype
    c = HGRN_CHUNK
    q, k, v, logf = (jnp.moveaxis(_to_chunks(t.astype(jnp.float32), c), 2, 0) for t in (q, k, v, logf))
    b = jnp.cumsum(logf, axis=-2)
    incl = jnp.tril(jnp.ones((c, c), bool))[:, :, None]

    def step(state, xs):
        q_i, k_i, v_i, b_i = xs
        b_last = b_i[..., -1:, :]
        decay = jnp.exp(jnp.where(incl, b_i[..., :, None, :] - b_i[..., None, :, :], -jnp.inf))
        attn = jnp.einsum("bhtd,bhsd,bhtsd->bhts", q_i, k_i, decay)
        o_i = (jnp.einsum("bhtd,bhde->bhte", q_i * jnp.exp(b_i), state)
               + jnp.einsum("bhts,bhse->bhte", attn, v_i))
        state = (state * jnp.exp(b_last)[..., 0, :, None]
                 + jnp.einsum("bhsd,bhse->bhde", k_i * jnp.exp(b_last - b_i), v_i))
        return state, o_i

    s0 = jnp.zeros(q.shape[1:3] + (q.shape[-1], v.shape[-1]), jnp.float32)
    _, o = lax.scan(step, s0, (q, k, v, b))
    return _from_chunks(jnp.moveaxis(o, 0, 2)).astype(dtype)

def conv_gdn_mixer(x, w_in, conv_a_w, conv_b_w, a_log, dt_bias, gdn_norm_g, w_out):
    bsz, s, _ = x.shape
    wa, wg, h = CONV_A_WIDTH, GDN_WIDTH, GDN_HEADS
    proj = x @ w_in
    cuts = [wa, 2 * wa, 3 * wa, 4 * wa, 4 * wa + 3 * wg, 4 * wa + 4 * wg, 4 * wa + 4 * wg + h]
    h_a, c_a, b_a, z_a, qkv, z_b, beta_raw, a_raw = jnp.split(proj, cuts, axis=-1)
    y_a = b_a * causal_depthwise_conv(c_a * h_a, conv_a_w) * jax.nn.silu(z_a)
    qkv = jax.nn.silu(causal_depthwise_conv(qkv, conv_b_w))
    q, k, v = (t.reshape(bsz, s, h, GDN_HEAD_DIM) for t in jnp.split(qkv, 3, axis=-1))
    q, k = l2_normalize(q), l2_normalize(k)
    beta = jax.nn.sigmoid(beta_raw.astype(jnp.float32))
    g = -jnp.exp(a_log.astype(jnp.float32)) * jax.nn.softplus(a_raw.astype(jnp.float32) + dt_bias.astype(jnp.float32))
    o = gated_delta_rule(q, k, v, g, beta)
    o = rms_norm(o, gdn_norm_g) * jax.nn.silu(z_b.reshape(bsz, s, h, GDN_HEAD_DIM))
    y = jnp.concatenate([y_a, o.reshape(bsz, s, wg)], axis=-1)
    return y @ w_out

def hgrn2_mixer(x, w_in, lower_bound, hgrn_norm_g, w_out):
    bsz, s, _ = x.shape
    q_raw, f_raw, i_in, z = jnp.split(x @ w_in, 4, axis=-1)
    f = lower_bound + (1.0 - lower_bound) * jax.nn.sigmoid(f_raw.astype(jnp.float32))
    q = jax.nn.silu(q_raw)
    k = (1.0 - f).astype(x.dtype)
    logf = jnp.log(f)
    heads = lambda t: t.reshape(bsz, s, HGRN_HEADS, HGRN_HEAD_DIM)
    o = hgrn2_recurrence(heads(q), heads(k), heads(i_in), heads(logf))
    o = rms_norm(o, hgrn_norm_g) * jax.nn.silu(heads(z))
    return o.reshape(bsz, s, HGRN_WIDTH) @ w_out

def first_inputs(seed: int = 0) -> dict:
    key = jax.random.key(seed)
    ks = jax.random.split(key, 20)
    nrm = lambda k, shape, scale: jax.random.normal(k, shape, jnp.float32) * scale
    dt = jnp.exp(jax.random.uniform(ks[6], (N_EVEN, GDN_HEADS), jnp.float32)
                 * (math.log(0.1) - math.log(0.001)) + math.log(0.001))
    return {
        "x": nrm(ks[0], (BATCH, SEQ, D_MODEL), 1.0),
        "p": nrm(ks[1], (DEPTH, BATCH, SEQ, PL_DIM), 1.0),
        "w_in_even": nrm(ks[2], (N_EVEN, D_MODEL, EVEN_IN), D_MODEL ** -0.5),
        "conv_a_w": nrm(ks[3], (N_EVEN, CONV_A_KERNEL, CONV_A_WIDTH), CONV_A_KERNEL ** -0.5),
        "conv_b_w": nrm(ks[4], (N_EVEN, GDN_CONV_KERNEL, 3 * GDN_WIDTH), GDN_CONV_KERNEL ** -0.5),
        "a_log": jnp.log(jax.random.uniform(ks[5], (N_EVEN, GDN_HEADS), jnp.float32, 1.0, 16.0)),
        "dt_bias": dt + jnp.log(-jnp.expm1(-dt)),
        "gdn_norm_g": 1.0 + nrm(ks[7], (N_EVEN, GDN_HEAD_DIM), 0.02),
        "w_out_even": nrm(ks[8], (N_EVEN, EVEN_MIX, D_MODEL), EVEN_MIX ** -0.5 * DEEPNORM_BETA),
        "w_in_odd": nrm(ks[9], (N_ODD, D_MODEL, ODD_IN), D_MODEL ** -0.5),
        "lower_bounds": nrm(ks[10], (DEPTH, HGRN_WIDTH), 0.1),
        "hgrn_norm_g": 1.0 + nrm(ks[11], (N_ODD, HGRN_HEAD_DIM), 0.02),
        "w_out_odd": nrm(ks[12], (N_ODD, ODD_MIX, D_MODEL), ODD_MIX ** -0.5 * DEEPNORM_BETA),
        "ln_g": 1.0 + nrm(ks[13], (DEPTH, D_MODEL), 0.02),
        "ln_b": nrm(ks[14], (DEPTH, D_MODEL), 0.02),
        "w_pl": nrm(ks[15], (DEPTH, PL_DIM, D_MODEL), PL_DIM ** -0.5),
        "w_pl_gate": nrm(ks[16], (DEPTH, D_MODEL, D_MODEL), D_MODEL ** -0.5),
    }

def first_block(x, p, w_in_even, conv_a_w, conv_b_w, a_log, dt_bias, gdn_norm_g, w_out_even,
              w_in_odd, lower_bounds, hgrn_norm_g, w_out_odd, ln_g, ln_b, w_pl, w_pl_gate):
    lbs = jnp.cumsum(jax.nn.softmax(lower_bounds.astype(jnp.float32), axis=0), axis=0)
    lbs = lbs - lbs[0]
    for i in range(DEPTH):
        j = i // 2
        if i % 2 == 0:
            s = conv_gdn_mixer(x, w_in_even[j], conv_a_w[j], conv_b_w[j], a_log[j], dt_bias[j],
                               gdn_norm_g[j], w_out_even[j])
        else:
            s = hgrn2_mixer(x, w_in_odd[j], lbs[i], hgrn_norm_g[j], w_out_odd[j])
        x = layer_norm(DEEPNORM_ALPHA * x + s, ln_g[i], ln_b[i])
        gate = jax.nn.sigmoid((x @ w_pl_gate[i]).astype(jnp.float32))
        x = x + ((p[i] @ w_pl[i]).astype(jnp.float32) * gate).astype(x.dtype)
    return x


DEPTH_2 = 1

HEAD_DIM = 64
N_HEADS = D_MODEL // HEAD_DIM
ML_HEADS = N_HEADS // 4
FOX_HEADS = (N_HEADS - ML_HEADS) // 2
MOBA_HEADS = N_HEADS - ML_HEADS - FOX_HEADS
FOX_W = FOX_HEADS * HEAD_DIM
ML_W = ML_HEADS * HEAD_DIM
MOBA_W = MOBA_HEADS * HEAD_DIM
Q_BLOCK = 128
ML_CHUNK = 64
ML_CONV = 4
MOBA_BLOCK = 256
MOBA_TOPK = 3
ALIBI_MAX = 8.0
D_FF = ((8 * D_MODEL // 3 + 255) // 256) * 256
EPS = 1e-6
SPLIT_SIZES = (FOX_W, FOX_W, FOX_W, FOX_HEADS,
               ML_W, ML_W, ML_W, ML_HEADS, ML_HEADS, ML_W,
               MOBA_W, MOBA_W, MOBA_W)
IN_COLS = sum(SPLIT_SIZES)


def _rms(x, g=None):
    xf = x.astype(jnp.float32)
    y = xf * lax.rsqrt(jnp.mean(xf * xf, axis=-1, keepdims=True) + EPS)
    return y if g is None else y * g.astype(jnp.float32)

def _to_heads(x, h):
    b, t, _ = x.shape
    return x.reshape(b, t, h, HEAD_DIM).transpose(0, 2, 1, 3)

def _from_heads(x):
    b, h, t, d = x.shape
    return x.transpose(0, 2, 1, 3).reshape(b, t, h * d)

def _alibi_slopes(h):
    return jnp.exp2(-ALIBI_MAX * jnp.arange(1, h + 1, dtype=jnp.float32) / h)

def _causal_conv(x, w, bias):
    ch = x.shape[-1]
    y = lax.conv_general_dilated(x, w.astype(x.dtype)[:, None, :], window_strides=(1,),
                                 padding=((ML_CONV - 1, 0),),
                                 dimension_numbers=('NWC', 'WIO', 'NWC'),
                                 feature_group_count=ch)
    return y + bias.astype(x.dtype)

def _fox_attention(q, k, v, f_pre):
    b, h, t, d = q.shape
    nq = t // Q_BLOCK
    logf = jax.nn.log_sigmoid(f_pre).transpose(0, 2, 1)
    cum = jnp.cumsum(logf, axis=-1)
    kpos = jnp.arange(t)
    qb = q.reshape(b, h, nq, Q_BLOCK, d).transpose(2, 0, 1, 3, 4)
    cq = cum.reshape(b, h, nq, Q_BLOCK).transpose(2, 0, 1, 3)
    starts = jnp.arange(nq) * Q_BLOCK
    scale = HEAD_DIM ** -0.5

    def block(args):
        qc, cqc, st = args
        qpos = st + jnp.arange(Q_BLOCK)
        s = jnp.einsum('bhqd,bhkd->bhqk', qc, k) * scale
        s = s + (cqc[..., None] - cum[:, :, None, :])
        s = jnp.where(kpos[None, :] <= qpos[:, None], s, -jnp.inf)
        p = jax.nn.softmax(s, axis=-1)
        return jnp.einsum('bhqk,bhkd->bhqd', p, v)

    out = lax.map(block, (qb, cq, starts))
    return out.transpose(1, 2, 0, 3, 4).reshape(b, h, t, d)

def _mlstm(q, k, v, i_pre, f_pre):
    b, h, t, d = q.shape
    nc = t // ML_CHUNK
    k = k * (d ** -0.5)
    itil = i_pre.transpose(0, 2, 1).reshape(b, h, nc, ML_CHUNK)
    logf = jax.nn.log_sigmoid(f_pre).transpose(0, 2, 1).reshape(b, h, nc, ML_CHUNK)
    bcum = jnp.cumsum(logf, axis=-1)
    bend = bcum[..., -1]
    wlog = bend[..., None] - bcum + itil
    qc = q.reshape(b, h, nc, ML_CHUNK, d)
    kc = k.reshape(b, h, nc, ML_CHUNK, d)
    vc = v.reshape(b, h, nc, ML_CHUNK, d)

    def step(carry, xs):
        cmat, nvec, m = carry
        kx, vx, wx, bx = xs
        m_new = jnp.maximum(bx + m, wx.max(-1))
        decay = jnp.exp(bx + m - m_new)
        ws = jnp.exp(wx - m_new[..., None])
        c_new = decay[..., None, None] * cmat + jnp.einsum('bhs,bhsd,bhse->bhde', ws, vx, kx)
        n_new = decay[..., None] * nvec + jnp.einsum('bhs,bhse->bhe', ws, kx)
        return (c_new, n_new, m_new), (cmat, nvec, m)

    init = (jnp.zeros((b, h, d, d), jnp.float32), jnp.zeros((b, h, d), jnp.float32),
            jnp.zeros((b, h), jnp.float32))
    xs = (kc.transpose(2, 0, 1, 3, 4), vc.transpose(2, 0, 1, 3, 4),
          wlog.transpose(2, 0, 1, 3), bend.transpose(2, 0, 1))
    _, (cs, ns, ms) = lax.scan(step, init, xs)
    cs = cs.transpose(1, 2, 0, 3, 4)
    ns = ns.transpose(1, 2, 0, 3)
    ms = ms.transpose(1, 2, 0)

    causal = jnp.tril(jnp.ones((ML_CHUNK, ML_CHUNK), dtype=bool))
    logd = bcum[..., :, None] - bcum[..., None, :] + itil[..., None, :]
    logd = jnp.where(causal, logd, -jnp.inf)
    m_inter = bcum + ms[..., None]
    m_j = jnp.maximum(m_inter, logd.max(-1))
    smat = jnp.einsum('bhcjd,bhcsd->bhcjs', qc, kc) * jnp.exp(logd - m_j[..., None])
    inter = jnp.exp(m_inter - m_j)
    num = (inter[..., None] * jnp.einsum('bhcde,bhcje->bhcjd', cs, qc)
           + jnp.einsum('bhcjs,bhcsd->bhcjd', smat, vc))
    den = inter * jnp.einsum('bhce,bhcje->bhcj', ns, qc) + smat.sum(-1)
    hout = num / jnp.maximum(jnp.abs(den), jnp.exp(-m_j))[..., None]
    return hout.reshape(b, h, t, d)

def _moba_attention(q, k, v, slopes):
    b, h, t, d = q.shape
    nb = -(-t // MOBA_BLOCK)
    pad = nb * MOBA_BLOCK - t
    kb = jnp.pad(k, ((0, 0), (0, 0), (0, pad), (0, 0))).reshape(b, h, nb, MOBA_BLOCK, d)
    vb = jnp.pad(v, ((0, 0), (0, 0), (0, pad), (0, 0))).reshape(b, h, nb, MOBA_BLOCK, d)
    kmean = kb.mean(axis=3)
    qblk = jnp.arange(t) // MOBA_BLOCK
    gate = jnp.einsum('bhtd,bhnd->bhtn', q, kmean)
    gate = jnp.where(jnp.arange(nb)[None, :] < qblk[:, None], gate, -jnp.inf)
    topk = min(MOBA_TOPK, nb)
    _, sel = lax.top_k(gate, topk)
    valid = sel < qblk[:, None]
    nq = t // Q_BLOCK
    xs = (q.reshape(b, h, nq, Q_BLOCK, d).transpose(2, 0, 1, 3, 4),
          sel.reshape(b, h, nq, Q_BLOCK, topk).transpose(2, 0, 1, 3, 4),
          valid.reshape(b, h, nq, Q_BLOCK, topk).transpose(2, 0, 1, 3, 4),
          jnp.arange(nq))
    bi = jnp.arange(b)[:, None, None, None]
    hi = jnp.arange(h)[None, :, None, None]
    scale = HEAD_DIM ** -0.5
    offs = jnp.arange(MOBA_BLOCK)

    def block(args):
        qc, selc, validc, ci = args
        qpos = ci * Q_BLOCK + jnp.arange(Q_BLOCK)
        ks = kb[bi, hi, selc]
        vs = vb[bi, hi, selc]
        kpos_sel = selc[..., None] * MOBA_BLOCK + offs
        dist_sel = (qpos[:, None, None] - kpos_sel).astype(jnp.float32)
        s_sel = (jnp.einsum('bhqd,bhqkld->bhqkl', qc, ks) * scale
                 - slopes[:, None, None, None] * dist_sel)
        s_sel = jnp.where(validc[..., None], s_sel, -jnp.inf)
        own = (ci * Q_BLOCK) // MOBA_BLOCK
        ko = lax.dynamic_index_in_dim(kb, own, axis=2, keepdims=False)
        vo = lax.dynamic_index_in_dim(vb, own, axis=2, keepdims=False)
        dist_own = qpos[:, None] - (own * MOBA_BLOCK + offs)[None, :]
        s_own = (jnp.einsum('bhqd,bhld->bhql', qc, ko) * scale
                 - slopes[:, None, None] * dist_own.astype(jnp.float32))
        s_own = jnp.where(dist_own >= 0, s_own, -jnp.inf)
        s_all = jnp.concatenate([s_sel.reshape(b, h, Q_BLOCK, topk * MOBA_BLOCK), s_own], axis=-1)
        p = jax.nn.softmax(s_all, axis=-1)
        p_sel = p[..., :topk * MOBA_BLOCK].reshape(b, h, Q_BLOCK, topk, MOBA_BLOCK)
        p_own = p[..., topk * MOBA_BLOCK:]
        return (jnp.einsum('bhqkl,bhqkld->bhqd', p_sel, vs)
                + jnp.einsum('bhql,bhld->bhqd', p_own, vo))

    out = lax.map(block, xs)
    return out.transpose(1, 2, 0, 3, 4).reshape(b, h, t, d)

def _mixer(hn, w_in, fox_f_bias, fox_q_g, fox_k_g, ml_conv_w, ml_conv_b, ml_i_bias,
           ml_f_bias, ml_h_g, moba_q_g, moba_k_g):
    proj = (hn @ w_in).astype(jnp.float32)
    idx = [int(i) for i in np.cumsum(SPLIT_SIZES)[:-1]]
    fq, fk, fv, ff, mq, mk, mv, mi, mf, mo, bq, bk, bv = jnp.split(proj, idx, axis=-1)
    y_fox = _fox_attention(_rms(_to_heads(fq, FOX_HEADS), fox_q_g),
                           _rms(_to_heads(fk, FOX_HEADS), fox_k_g),
                           _to_heads(fv, FOX_HEADS),
                           ff + fox_f_bias.astype(jnp.float32))
    qk = jax.nn.silu(_causal_conv(jnp.concatenate([mq, mk], axis=-1), ml_conv_w, ml_conv_b))
    mq, mk = jnp.split(qk, 2, axis=-1)
    h_ml = _mlstm(_to_heads(mq, ML_HEADS), _to_heads(mk, ML_HEADS), _to_heads(mv, ML_HEADS),
                  mi + ml_i_bias.astype(jnp.float32), mf + ml_f_bias.astype(jnp.float32))
    y_ml = _from_heads(_rms(h_ml)) * ml_h_g.astype(jnp.float32) * jax.nn.sigmoid(mo)
    y_moba = _moba_attention(_rms(_to_heads(bq, MOBA_HEADS), moba_q_g),
                             _rms(_to_heads(bk, MOBA_HEADS), moba_k_g),
                             _to_heads(bv, MOBA_HEADS), _alibi_slopes(MOBA_HEADS))
    return jnp.concatenate([_from_heads(y_fox), y_ml, _from_heads(y_moba)], axis=-1)

def second_inputs(seed: int = 0) -> dict:
    key = jax.random.key(seed)
    ks = jax.random.split(key, 22)
    n = jax.random.normal
    f32 = jnp.float32
    return {
        'x': n(ks[0], (BATCH, SEQ, D_MODEL), f32),
        'c': n(ks[1], (BATCH, D_MODEL), f32),
        'w_ada': n(ks[2], (DEPTH_2, D_MODEL, 6 * D_MODEL), f32) * (0.5 * D_MODEL ** -0.5),
        'b_ada': n(ks[3], (DEPTH_2, 6 * D_MODEL), f32) * 0.01,
        'norm1_g': 1.0 + 0.02 * n(ks[4], (DEPTH_2, D_MODEL), f32),
        'norm2_g': 1.0 + 0.02 * n(ks[5], (DEPTH_2, D_MODEL), f32),
        'w_in': n(ks[6], (DEPTH_2, D_MODEL, IN_COLS), f32) * D_MODEL ** -0.5,
        'fox_f_bias': 2.0 + 0.1 * n(ks[7], (DEPTH_2, FOX_HEADS), f32),
        'fox_q_g': 1.0 + 0.02 * n(ks[8], (DEPTH_2, HEAD_DIM), f32),
        'fox_k_g': 1.0 + 0.02 * n(ks[9], (DEPTH_2, HEAD_DIM), f32),
        'ml_conv_w': n(ks[10], (DEPTH_2, ML_CONV, 2 * ML_W), f32) * ML_CONV ** -0.5,
        'ml_conv_b': 0.01 * n(ks[11], (DEPTH_2, 2 * ML_W), f32),
        'ml_i_bias': 0.1 * n(ks[12], (DEPTH_2, ML_HEADS), f32),
        'ml_f_bias': 3.0 + 0.1 * n(ks[13], (DEPTH_2, ML_HEADS), f32),
        'ml_h_g': 1.0 + 0.02 * n(ks[14], (DEPTH_2, ML_W), f32),
        'moba_q_g': 1.0 + 0.02 * n(ks[15], (DEPTH_2, HEAD_DIM), f32),
        'moba_k_g': 1.0 + 0.02 * n(ks[16], (DEPTH_2, HEAD_DIM), f32),
        'w_out': n(ks[17], (DEPTH_2, D_MODEL, D_MODEL), f32) * D_MODEL ** -0.5,
        'w_gate_up': n(ks[18], (DEPTH_2, D_MODEL, 2 * D_FF), f32) * D_MODEL ** -0.5,
        'w_down': n(ks[19], (DEPTH_2, D_FF, D_MODEL), f32) * D_FF ** -0.5,
    }

def second_block(x, c, w_ada, b_ada, norm1_g, norm2_g, w_in, fox_f_bias, fox_q_g, fox_k_g,
              ml_conv_w, ml_conv_b, ml_i_bias, ml_f_bias, ml_h_g, moba_q_g, moba_k_g,
              w_out, w_gate_up, w_down):
    for l in range(DEPTH_2):
        mod = jax.nn.silu(c) @ w_ada[l] + b_ada[l]
        sh1, sc1, g1, sh2, sc2, g2 = jnp.split(mod[:, None, :], 6, axis=-1)
        hn = (_rms(x, norm1_g[l]) * (1 + sc1) + sh1).astype(x.dtype)
        y = _mixer(hn, w_in[l], fox_f_bias[l], fox_q_g[l], fox_k_g[l], ml_conv_w[l],
                   ml_conv_b[l], ml_i_bias[l], ml_f_bias[l], ml_h_g[l], moba_q_g[l], moba_k_g[l])
        x = x + g1 * (y.astype(x.dtype) @ w_out[l])
        hn = (_rms(x, norm2_g[l]) * (1 + sc2) + sh2).astype(x.dtype)
        gate, up = jnp.split(hn @ w_gate_up[l], 2, axis=-1)
        x = x + g2 * ((jax.nn.silu(gate) * up) @ w_down[l])
    return x


def setup_inputs(seed=0):
    out = dict(first_inputs(seed))
    for name, value in second_inputs(seed + 1).items():
        if name != "x":
            out[name + "_2"] = value
    return out


def reference(
    x, p, w_in_even, conv_a_w, conv_b_w, a_log, dt_bias, gdn_norm_g, w_out_even, w_in_odd,
    lower_bounds, hgrn_norm_g, w_out_odd, ln_g, ln_b, w_pl, w_pl_gate, c_2, w_ada_2, b_ada_2,
    norm1_g_2, norm2_g_2, w_in_2, fox_f_bias_2, fox_q_g_2, fox_k_g_2, ml_conv_w_2, ml_conv_b_2,
    ml_i_bias_2, ml_f_bias_2, ml_h_g_2, moba_q_g_2, moba_k_g_2, w_out_2, w_gate_up_2, w_down_2,
):
    x = first_block(
        x, p, w_in_even, conv_a_w, conv_b_w, a_log, dt_bias, gdn_norm_g, w_out_even, w_in_odd,
        lower_bounds, hgrn_norm_g, w_out_odd, ln_g, ln_b, w_pl, w_pl_gate,
    )
    return second_block(
        x, c_2, w_ada_2, b_ada_2, norm1_g_2, norm2_g_2, w_in_2, fox_f_bias_2, fox_q_g_2,
        fox_k_g_2, ml_conv_w_2, ml_conv_b_2, ml_i_bias_2, ml_f_bias_2, ml_h_g_2, moba_q_g_2,
        moba_k_g_2, w_out_2, w_gate_up_2, w_down_2,
    )


_drawn_inputs = setup_inputs


def setup_inputs(seed=0):
    import zlib

    import numpy as np

    out = dict(_drawn_inputs(seed))
    spreads = {}
    factors = {'a_log': 2.791,
     'gdn_norm_g': 8.0,
     'lower_bounds': 8.0,
     'hgrn_norm_g': 8.0,
     'b_ada_2': 6.011,
     'norm1_g_2': 8.0,
     'norm2_g_2': 8.0,
     'fox_f_bias_2': 8.0,
     'fox_q_g_2': 8.0,
     'fox_k_g_2': 8.0,
     'ml_conv_b_2': 189.711,
     'ml_i_bias_2': 200.0,
     'ml_f_bias_2': 64.0,
     'ml_h_g_2': 58.32,
     'moba_q_g_2': 8.0,
     'moba_k_g_2': 8.0}
    for name, (base, spread) in spreads.items():
        noise = np.random.default_rng([zlib.crc32(name.encode()), seed]).standard_normal(out[name].shape)
        drawn = base * np.exp(spread * noise) if base else spread * noise
        out[name] = __import__('jax').numpy.asarray(drawn.astype(out[name].dtype))
    for name, factor in factors.items():
        out[name] = (out[name] * factor).astype(out[name].dtype)
    return out
```

```python
import math
from contextlib import ExitStack

import numpy as np

import concourse.bass as bass
from concourse import mybir

F32 = mybir.dt.float32
U32 = mybir.dt.uint32
ALU = mybir.AluOpType
ACT = mybir.ActivationFunctionType
AX = mybir.AxisListType

P = 128
T = 256
NT = T // P
D = 1024
KC = D // P
SLAB = 512
RING = 4
LEVELS = [1, 2, 4, 8, 16, 32, 64]
NL = len(LEVELS)
HG = 4
GDN_HEADS = 8
HGRN_GROUPS = 4
ALPHA = math.sqrt(2.0)
LN_EPS = 1e-5
L2_EPS = 1e-6
RMS_EPS = 1e-6
D_FF = 2816
FF = D_FF // P
FOX, ML, MOBA = 6, 4, 6
HD = 64
NEG = -1e30
SCALE64 = HD ** -0.5
SCALE128 = 128 ** -0.5

C_ID, C_TRIU, C_BD = 0, P, 2 * P
C_LVL = 3 * P
C_MASK = C_LVL + NL * P
C_DIST = C_MASK + 3 * P
C_N = C_DIST + 3 * P
NORM_AT = 12288

_SIZES = [("conv_b", 96), ("conv_a", 24), ("gdn_g", 1), ("hgrn_g", 1), ("lb", 32), ("n1", 8), ("n2", 8),
          ("mlw", 16), ("mlb", 4), ("mlg", 2), ("bada", 32), ("c", 8), ("foxq", 1), ("foxk", 1),
          ("mobaq", 1), ("mobak", 1), ("a_log", 8), ("dt", 8), ("gate_bias", 14)]
VC = {}
_at = 0
for _n, _s in _SIZES:
    VC[_n] = _at
    _at += _s
V_N = _at

QT = {"fq": 0, "fk": 3, "mq": 6, "mk": 8, "mo": 10, "bq": 12, "bk": 15}
N_QT = 18
HEADS = FOX + ML + MOBA
MOD_ROW = [0, 0, 1, 1, None, None, 2, 2, 3, 3, None, None]
SQ_SLOTS = [(0, 1, 2), (0, 1, 3)]
NG = FOX + 2 * ML


class Step:

    def __init__(self, kind, args, engines, banks, slabs, readers, opens):
        self.kind, self.args, self.engines, self.banks = kind, args, engines, banks
        self.slabs, self.readers, self.opens = slabs, readers, opens
        self.name = (kind,) + args


def plan(stage):
    script, slabs = [], []
    ring = [0]

    def step(kind, *args, on, banks=(), slab=(), readers=None, opens=True):
        at = []
        for s in slab:
            if s not in slabs:
                slabs.append(s)
            at.append(slabs.index(s))
        if readers is None:
            readers = "".join(e for e in on if e in "SV")
        script.append(Step(kind, args, on, tuple(banks), at, readers, opens))

    def unit(kind, *args, on, slab=None, readers=None):
        step(kind, *args, on=on, banks=(4 + ring[0] % 4,), slab=(slab,) if slab else (), readers=readers)
        ring[0] += 1

    def later(f, *args, **kw):
        return lambda: f(*args, **kw)

    def pair(name, g, on, readers=None):
        return [later(unit, name, g, p, on=on, slab=(name, g), readers=readers) for p in range(2)]

    def ada(i):
        if MOD_ROW[i] is None:
            unit("ada", i, on="TV", slab=("ada", i))
        else:
            unit("ada", i, on="TS", slab=("ada", i))
            unit("adat", i, on="TV")

    def interleave(chain, fill):
        fill = list(fill)
        rate, owed = len(fill) / len(chain), 0.0
        for c in chain:
            c()
            owed += rate
            while owed >= 1 and fill:
                fill.pop(0)()
                owed -= 1
        for f in fill:
            f()

    def tail(layer):
        for n in range(2):
            step("out", layer, n, on="TV", banks=(4 + 2 * n, 5 + 2 * n), slab=[("out", layer, n, k) for k in range(2)])
        for n in range(2):
            step("pl", layer, n, on="TS", banks=(2 * n, 2 * n + 1), slab=[("pl", layer)])
        step("lna", layer, on="VS")
        step("lnb", layer, on="V")
        step("xt", 2 * layer, on="TSV", banks=(0, 1, 2, 3))
        for n in range(2):
            step("gate", layer, n, on="TSV", banks=(4 + 2 * n, 5 + 2 * n), slab=[("gate", layer, n)], readers="S")
        step("xt", 2 * layer + 1, on="TSV", banks=(0, 1, 2, 3))

    step("setup", on="SG")
    step("ba", on="TV", banks=(0,))
    step("ba1", on="SV")
    step("ba2", on="SV")
    step("c1", on="SV")
    step("c2", on="S")

    def conv(name, g):
        return pair(name, g, on="TVS", readers="V")

    def gdn(g):
        out = [later(step, "gt", g, on="G"),
               later(step, "gc", g, on="TVS", banks=(0, 1, 2)),
               later(step, "gc2", g, on="VG"),
               later(step, "norm", g, on="TSV", banks=(0, 1, 2, 3), readers="S"),
               later(step, "norm2", g, on="G"),
               later(step, "vtr", g, on="TV", banks=(0, 1)),
               later(step, "gk", g, on="TV", banks=(2,)),
               later(step, "gkk", g, on="TV", banks=(0, 1, 2, 3))]
        for i in range(NL):
            out.append(later(step, "gp", g, i, on="TV", banks=(0, 1)))
            out.append(later(step, "gu", g, i, on="TV", banks=(2, 3) if i == NL - 1 else (0, 1, 2, 3)))
        out += [later(step, "gv", g, 0, on="TS", banks=(0,)),
                later(step, "gs", g, on="TS", banks=(1,)),
                later(step, "gks", g, on="TV", banks=(2,)),
                later(step, "gv", g, 1, on="TS", banks=(3,)),
                later(step, "go", g, on="TS", banks=(0, 1)),
                later(step, "gr", g, on="TSV", banks=(2, 3), readers="S")]
        return out

    for name in "kqv":
        for u in conv(name, 0):
            u()
    fill = pair("zb", 0, "TS")
    for name in "kqv":
        fill += conv(name, 1)
    fill += pair("zb", 1, "TS")
    for hf in range(2):
        fill += pair("ah", hf, "TS") + pair("ac", hf, "TV") + pair("az", hf, "TS") + pair("ab", hf, "TV")
    interleave(gdn(0), fill[:14])
    interleave(gdn(1), fill[14:] + [later(ada, i) for i in range(4)])
    step("mod", 0, on="V")
    tail(0)
    if stage == 0:
        return script, slabs

    def project(g):
        return (pair("f", g, "TSV", readers="S") + pair("q1", g, "TS")
                + [later(unit, "i", g, c, on="TS", slab=("i", g)) for c in range(NT)] + pair("z1", g, "TS"))

    def hgrn(g):
        out = [later(step, "hf", g, on="SV"),
               later(step, "hd", g, on="TV", banks=(0, 1)),
               later(step, "hx", g, 0, on="VS"),
               later(step, "hy", g, 0, on="VG"),
               later(step, "hx", g, 1, on="VS")]
        for i in range(NL):
            out.append(later(step, "hy", g, i + 1, on="VG"))
            out.append(later(step, "hm", g, i, on="TV", banks=(0, 1) if i % 2 else (2, 3)))
            if i + 2 <= NL:
                out.append(later(step, "hx", g, i + 2, on="VS"))
        out += [later(step, "hc", g, on="TS", banks=(2,)),
                later(step, "ho", g, on="TS", banks=(0, 1)),
                later(step, "hr", g, on="TSV", banks=(2, 3), readers="S")]
        return out

    step("lb", on="VS")
    step("lb2", on="V")
    for u in project(0):
        u()
    for g in range(HGRN_GROUPS):
        interleave(hgrn(g), project(g + 1) if g + 1 < HGRN_GROUPS else [])
    tail(1)
    if stage == 1:
        return script, slabs

    def feat(j):
        if j in (3, 4):
            unit("feat", j, on="TVS", slab=("feat", j // 2), readers="V")
        else:
            unit("feat", j, on="TS", slab=("feat", j // 2))

    step("rms", 0, on="S")
    step("rmsb", 0, on="V")
    step("xt", 4, on="TSV", banks=(0, 1, 2, 3))
    for c in range(NT):
        unit("gates", c, on="TV", slab=("feat", 4))
    feat(8)
    step("ga", on="VS")
    feat(0)
    step("gb", on="VS")
    feat(1)
    step("gd", on="V")
    step("gsp", on="GV")
    feat(2)
    step("qn", 0, on="TSV", banks=(0, 1, 2), readers="S")
    step("gcol", on="TV", banks=(3,))
    feat(3)
    step("grow", 0, on="TV", banks=(0, 1, 2))
    feat(4)
    step("grow", 1, on="TV", banks=(0, 1))
    feat(5)
    step("gm", on="VS")
    feat(6)
    feat(7)
    step("qn", 1, on="TSV", banks=(0, 1, 2), readers="S")
    step("mb", on="V")
    for n in range(2):
        for c in range(NT):
            unit("val", n, c, on="TS", slab=("val", n))
    fill = [later(ada, i) for i in range(4, 12)]
    for n in range(HEADS + 2):
        if n < HEADS:
            step("score", n, on="TV" if FOX <= n < FOX + ML else "TVS", banks=(n % 2,), readers="V")
        if n % 2 and fill:
            fill.pop(0)()
        if 1 <= n <= HEADS:
            step("turn", n - 1, on="VTS", banks=(2,), readers="S")
        if n >= 2:
            if n % 2 == 0:
                step("pv", n - 2, on="T", banks=(3,))
            else:
                step("pv", n - 2, on="TS", banks=(3,), opens=False)
        if n == 14:
            step("mln", on="TSV", banks=(0,), readers="S")
    for n in range(2):
        step("out2", n, on="TV", banks=(4 + 2 * n, 5 + 2 * n), slab=[("out2", n)])
    step("mod", 1, on="V")
    step("rms", 1, on="S")
    step("rmsb", 1, on="V")
    step("xt", 5, on="TSV", banks=(0, 1, 2, 3))
    for j in range(FF):
        unit("ff", j, on="TSV", slab=("ff", j // 2))
    for n in range(2):
        step("down", n, on="TV", banks=(2 * n, 2 * n + 1), slab=[("down", n, k) for k in range(3)])
    return script, slabs


STAGE = 2


def build(nc, wst, x_in, xt_in, pt_in, wba, cst_in, vec_in, lnrow, out):
    script, slabs = plan(STAGE)
    where = {s.name: n for n, s in enumerate(script)}
    assert len(where) == len(script)
    counts = {}
    for e in "TSVG":
        n, counts[e] = 0, []
        for s in script:
            n += e in s.engines
            counts[e].append(n)
    last_use = {}
    for n, s in enumerate(script):
        for b in s.slabs:
            last_use[b] = n

    ctx = ExitStack()
    with ctx:
        def sem(name):
            return ctx.enter_context(nc.semaphore(name))

        tensor_done, scalar_done, vector_done = sem("tensor_done"), sem("scalar_done"), sem("vector_done")
        gpsimd_done = sem("gpsimd_done")
        done = {"T": tensor_done, "S": scalar_done, "V": vector_done, "G": gpsimd_done}
        vector_link, scalar_link, gpsimd_link = sem("vector_link"), sem("scalar_link"), sem("gpsimd_link")
        slab_loaded = [sem(f"slab_loaded{i}") for i in range(RING)]
        x_loaded, small_loaded, cst_loaded = sem("x_loaded"), sem("small_loaded"), sem("cst_loaded")
        ln_loaded, g_loaded, out_stored = sem("ln_loaded"), sem("g_loaded"), sem("out_stored")

        def count(engine, name):
            assert engine in script[where[name]].engines, name
            return counts[engine][where[name]]

        def tensor_at(*name):
            return count("T", name)

        def scalar_at(*name):
            return count("S", name)

        def vector_at(*name):
            return count("V", name)

        def gpsimd_at(*name):
            return count("G", name)

        def sb(name, shape):
            return ctx.enter_context(nc.sbuf_tensor(name, shape, F32))

        ring = sb("ring", [P, RING, KC * SLAB])
        X = sb("X", [P, NT, D])
        XT = sb("XT", [P, KC, T])
        PT = sb("PT", [P, 2, 2, T])
        CST = sb("CST", [P, C_N])
        VEC = sb("VEC", [P, V_N])
        ONES = sb("ONES", [P, P])
        EPS = sb("EPS", [P, 4])
        LNW = sb("LNW", [P, 2, D])
        YT = sb("YT", [P, FF, T])
        WBA = sb("WBA", [P, KC, 16])
        SCT = sb("SCT", [P, KC, P])
        SC8 = sb("SC8", [P, KC])
        MROW = sb("MROW", [1, SLAB])
        MODT = sb("MODT", [P, 4, KC])
        MODG = sb("MODG", [P, 2, KC])
        STAT = sb("STAT", [P, NT, 2, 6])
        AGG = sb("AGG", [P, NT, 2])
        RSTD = sb("RSTD", [P, NT])
        SUMSQ = sb("SUMSQ", [P, NT])
        ident = CST[:, C_ID:C_ID + P]
        triu = CST[:, C_TRIU:C_TRIU + P]
        bd64 = CST[:, C_BD:C_BD + P]
        lvl = [CST[:, C_LVL + i * P:C_LVL + (i + 1) * P] for i in range(NL)]
        mask3 = CST[:, C_MASK:C_MASK + 3 * P]
        dist3 = CST[:, C_DIST:C_DIST + 3 * P]

        free = nc.sbuf_usable_end - nc.sbuf_base
        ARENA_WORDS = (free - 64) // 4
        arena = sb("arena", [P, ARENA_WORDS])

        class Arena:
            def __init__(self):
                self.at = 0

            def take(self, *shape):
                n = 1
                for s in shape:
                    n *= s
                assert self.at + n <= ARENA_WORDS, (self.at, n, ARENA_WORDS)
                ap = arena[:, self.at:self.at + n]
                self.at += n
                if len(shape) == 2:
                    return ap.rearrange("p (a b) -> p a b", a=shape[0])
                if len(shape) == 3:
                    return ap.rearrange("p (a b c) -> p a b c", a=shape[0], b=shape[1])
                return ap

        PS = ctx.enter_context(nc.psum_tensor("PS", [P, 8, SLAB], F32))

        A0 = Arena()
        KT, QT0 = A0.take(2 * HG, T), A0.take(2 * HG, T)
        VT = A0.take(HG, T)
        ZB = A0.take(2 * HG, T)
        CV = A0.take(2, 2 * T)
        SQ = A0.take(4, 2 * T)
        AC, AZ = A0.take(2, 2 * T), A0.take(2, 2 * T)
        assert A0.at == NORM_AT
        AH = YT[:, 16:20, :].rearrange("p (a b) t -> p a (b t)", a=2)
        DL, DU = A0.take(8, P), A0.take(8, P)
        U, XI, PM = A0.take(8, P), A0.take(8, P), A0.take(8, P)
        BV, VN = (LNW[:, i, :].rearrange("p (m j) -> p m j", m=8) for i in range(2))
        KD, ST, ER = A0.take(4, P), A0.take(4, P), A0.take(4, P)
        TA, TB, TC, TD = A0.take(16), A0.take(16), A0.take(16), A0.take(16)
        BE, GG = A0.take(2, 8), A0.take(2, 8)
        GCOL, EGC, BEG = A0.take(8), A0.take(8), A0.take(8)
        KDF = A0.take(4)
        OT = U.rearrange("p (h c) t -> p h (c t)", h=HG)
        SQO = PM.rearrange("p (h c) t -> p h (c t)", h=HG)
        RO = XI.rearrange("p (h c) t -> p h (c t)", h=HG)

        AN = Arena()
        AN.take(NORM_AT)
        PLB = AN.take(NT, D)
        GT = AN.take(NT, SLAB)

        A1 = Arena()
        HB, HK, HQ = A1.take(2 * HG, T), A1.take(2 * HG, T), A1.take(2 * HG, T)
        HV = A1.take(2, NT, HG * P)
        HZ = A1.take(2 * HG, T)
        FS = A1.take(HG, T)
        HE, HX = A1.take(2 * HG, T), A1.take(2 * HG, T)
        HA, HC = A1.take(8, P), A1.take(HG, P)
        HS = A1.take(HG, T)
        LBV, OML, LT1, LT2 = A1.take(16), A1.take(16), A1.take(32), A1.take(16)
        HOT, HRN = HE[:, 0:HG, :], HE[:, HG:2 * HG, :]

        A2 = Arena()
        Q2 = A2.take(N_QT, T)
        V2 = A2.take(NT, D)
        B2 = A2.take(HEADS, 3 * P)
        SC, PTT = A2.take(2, 3 * P), A2.take(2, 3 * P)
        SQ2 = A2.take(4, 2 * T)
        CV2 = A2.take(2, 2 * T)
        GA, GB, NLS, GCC = A2.take(NT, NG), A2.take(NT, NG), A2.take(NT, NG), A2.take(NT, NG)
        MX, SM, RI, EM = A2.take(HEADS, 2), A2.take(HEADS, 2), A2.take(HEADS, 2), A2.take(ML, 2)
        XN = A2.take(NT, D)
        GSP = [YT[:, 8 + 5 * c:13 + 5 * c, :].rearrange("p a (b k) -> p (a b) k", b=2) for c in range(NT)]

        def v(name, i=0, n=1):
            return VEC[:, VC[name] + i:VC[name] + i + n]

        def bc(ap, n):
            return ap.unsqueeze(2).to_broadcast([ap.shape[0], ap.shape[1], n])

        def rep(ap, n):
            return ap.unsqueeze(1).to_broadcast([ap.shape[0], n, ap.shape[1]])

        def flat(ap):
            return ap.rearrange("p a b -> p (a b)")

        def tiles(ap, a, n):
            return flat(ap[:, a:a + n, :])

        def bank_of(*name):
            return script[where[name]].banks[0]

        def gate_of(j):
            return j if j < FOX else j + ML

        def head(h):
            fam, i = ("f", h) if h < FOX else ("m", h - FOX) if h < FOX + ML else ("b", h - FOX - ML)
            return QT[fam + "q"] + i // 2, QT[fam + "k"] + i // 2, (h % 2) * HD, h * HD, h // 2

        def rows(c):
            return slice(0, P) if c == 0 else slice(P, 3 * P)

        conv_units = [s.name for s in script if s.kind in ("k", "q", "v")]
        block = ctx.enter_context(nc.Block())

        @block.sync
        def _(sp):
            def slab(i):
                if i >= RING:
                    sp.wait_ge(tensor_done, counts["T"][last_use[i - RING]])
                n = _width(slabs[i])
                sp.dma_start(ring[:, i % RING, 0:n], wst[i, :, 0:n]).then_inc(slab_loaded[i % RING], 16)

            sp.dma_start(XT[:], xt_in).then_inc(x_loaded, 16)
            for i in range(len(slabs)):
                slab(i)
            if STAGE == 2:
                for n in range(2):
                    sp.wait_ge(vector_done, vector_at("down", n))
                    sp.dma_start(out[:, :, n * SLAB:(n + 1) * SLAB], X[:, :, n * SLAB:(n + 1) * SLAB]).then_inc(out_stored, 16)
                sp.wait_ge(out_stored, 32)
            else:
                sp.wait_ge(vector_done, vector_at("gate", STAGE, 1))
                sp.dma_start(out, X[:]).then_inc(out_stored, 16)
                sp.wait_ge(out_stored, 16)
                sp.wait_ge(ln_loaded, 32 + 16 * STAGE)

        @block.tensor
        def _(pe):
            def mm(o, lhsT, rhs, start=True, stop=True):
                return pe.matmul(o, lhsT, rhs, start=start, stop=stop)

            def claim(step):
                n = where[step.name]
                for b in step.banks if step.opens else ():
                    before = [s for s in script[:n] if b in s.banks]
                    if before:
                        for r in before[-1].readers or "":
                            pe.wait_ge(done[r], count(r, before[-1].name))

            def loaded(step):
                for i in step.slabs:
                    pe.wait_ge(slab_loaded[i % RING], 16 * (i // RING + 1))

            def w(step, k=0):
                return ring[:, step.slabs[k] % RING, :].rearrange("p (k n) -> p k n", k=KC)

            def features(step, col):
                wt = w(step)
                for a in range(2):
                    for k in range(KC):
                        last = mm(PS[:, step.banks[0], a * T:(a + 1) * T], wt[:, k, col + a * P:col + (a + 1) * P],
                                  XT[:, k, :], start=k == 0, stop=k == KC - 1)
                return last

            def tokens(step, c, act=None, cols=SLAB, first=0):
                wt = w(step)
                for k in range(KC):
                    last = mm(PS[:, step.banks[0], 0:cols], (act or XT)[:, k, c * P:(c + 1) * P],
                              wt[:, k, first:first + cols], start=k == 0, stop=k == KC - 1)
                return last

            def t_ba(step):
                pe.wait_ge(x_loaded, 16)
                pe.wait_ge(small_loaded, 16 * 4)
                for c in range(NT):
                    for k in range(KC):
                        last = mm(PS[:, 0, c * 16:(c + 1) * 16], XT[:, k, c * P:(c + 1) * P], WBA[:, k, :],
                                  start=k == 0, stop=k == KC - 1)
                last.then_inc(tensor_done, 1)

            def unit2(step, g, p):
                features(step, 2 * p * P).then_inc(tensor_done, 1)

            def t_gc(step, g):
                pe.wait_ge(vector_done, vector_at("ba2"))
                pe.wait_ge(gpsimd_done, gpsimd_at("gt", g))
                gt = flat(PM)
                for i in range(2):
                    mm(PS[:, i, :], ONES[:], gt[:, i * SLAB:(i + 1) * SLAB])
                mm(PS[:, 2, 0:8], triu, GG[:, g, :]).then_inc(tensor_done, 1)

            def t_norm(step, g):
                pe.wait_ge(scalar_done, scalar_at("q", g, 1))
                for i in range(4):
                    last = mm(PS[:, i, :], ONES[:], SQ[:, i, :])
                last.then_inc(tensor_done, 1)

            def t_vtr(step, g):
                pe.wait_ge(scalar_done, scalar_at("v", g, 1))
                for c in range(NT):
                    for h in range(HG):
                        last = pe.transpose(PS[:, c, h * P:(h + 1) * P], VT[:, h, c * P:(c + 1) * P], ident)
                last.then_inc(tensor_done, 1)

            def t_gk(step, g):
                pe.wait_ge(vector_done, vector_at("norm", g))
                for h in range(HG):
                    last = pe.transpose(PS[:, 2, h * P:(h + 1) * P], KT[:, g * HG + h, 0:P], ident)
                last.then_inc(tensor_done, 1)

            def t_gkk(step, g):
                pe.wait_ge(gpsimd_done, gpsimd_at("norm2", g))
                for c in range(NT):
                    for h in range(HG):
                        kt = KT[:, g * HG + h, c * P:(c + 1) * P]
                        mm(PS[:, c, h * P:(h + 1) * P], kt, kt)
                        last = mm(PS[:, 2 + c, h * P:(h + 1) * P], kt, QT0[:, g * HG + h, c * P:(c + 1) * P])
                last.then_inc(tensor_done, 1)

            def t_gp(step, g, i):
                if i == 0:
                    pe.wait_ge(vector_done, vector_at("gkk", g))
                    pe.wait_ge(gpsimd_done, gpsimd_at("gc2", g))
                else:
                    pe.wait_ge(vector_done, vector_at("gu", g, i - 1))
                for m in range(8):
                    last = mm(PS[:, m // HG, (m % HG) * P:(m % HG + 1) * P], DL[:, m, :], U[:, m, :])
                last.then_inc(tensor_done, 1)

            def t_gu(step, g, i):
                pe.wait_ge(vector_done, vector_at("gp", g, i))
                for m in range(8):
                    last = mm(PS[:, 2 + m // HG, (m % HG) * P:(m % HG + 1) * P], XI[:, m, :], PM[:, m, :])
                if i < NL - 1:
                    for m in range(8):
                        last = mm(PS[:, m // HG, (m % HG) * P:(m % HG + 1) * P], PM[:, m, :], XI[:, m, :])
                last.then_inc(tensor_done, 1)

            def t_gv(step, g, c):
                pe.wait_ge(vector_done, vector_at("gu", g, NL - 1))
                if c:
                    pe.wait_ge(vector_done, vector_at("gks", g))
                for h in range(HG):
                    m = c * HG + h
                    last = mm(PS[:, step.banks[0], h * P:(h + 1) * P], U[:, m, :], BV[:, m, :])
                last.then_inc(tensor_done, 1)

            def t_gs(step, g):
                pe.wait_ge(scalar_done, scalar_at("gv", g, 0))
                for h in range(HG):
                    last = mm(PS[:, 1, h * P:(h + 1) * P], KD[:, h, :], VN[:, h, :])
                last.then_inc(tensor_done, 1)

            def t_gks(step, g):
                pe.wait_ge(scalar_done, scalar_at("gs", g))
                for h in range(HG):
                    last = mm(PS[:, 2, h * P:(h + 1) * P], KT[:, g * HG + h, P:T], ST[:, h, :])
                last.then_inc(tensor_done, 1)

            def t_go(step, g):
                pe.wait_ge(scalar_done, scalar_at("gv", g, 1))
                for h in range(HG):
                    mm(PS[:, 0, h * P:(h + 1) * P], VN[:, h, :], DU[:, h, :])
                for h in range(HG):
                    mm(PS[:, 1, h * P:(h + 1) * P], VN[:, HG + h, :], DU[:, HG + h, :], stop=False)
                    last = mm(PS[:, 1, h * P:(h + 1) * P], ST[:, h, :], QT0[:, g * HG + h, P:T], start=False)
                last.then_inc(tensor_done, 1)

            def t_gr(step, g):
                pe.wait_ge(scalar_done, scalar_at("go", g))
                for i in range(2):
                    last = mm(PS[:, 2 + i, :], ONES[:], tiles(SQO, 2 * i, 2))
                last.then_inc(tensor_done, 1)

            def t_out(step, layer, n):
                if layer == 0:
                    pe.wait_ge(vector_done, vector_at("ab", 1, 1))
                    pe.wait_ge(vector_done, vector_at("gr", 1))
                else:
                    pe.wait_ge(vector_done, vector_at("hr", HGRN_GROUPS - 1))
                for k in range(2):
                    pe.wait_ge(slab_loaded[step.slabs[k] % RING], 16 * (step.slabs[k] // RING + 1))
                    for c in range(NT):
                        for j in range(KC):
                            last = mm(PS[:, step.banks[c], :], YT[:, k * KC + j, c * P:(c + 1) * P], w(step, k)[:, j, :],
                                      start=k == 0 and j == 0, stop=k == 1 and j == KC - 1)
                last.then_inc(tensor_done, 1)

            def t_pl(step, layer, n):
                wt = ring[:, step.slabs[0] % RING, 0:2 * D].rearrange("p (k n) -> p k n", k=2)
                for c in range(NT):
                    for k in range(2):
                        last = mm(PS[:, step.banks[c], :], PT[:, layer, k, c * P:(c + 1) * P],
                                  wt[:, k, n * SLAB:(n + 1) * SLAB], start=k == 0, stop=k == 1)
                last.then_inc(tensor_done, 1)

            def t_xt(step, i):
                src = X if i < 4 else XN
                if i in (0, 2):
                    pe.wait_ge(vector_done, vector_at("lnb", i // 2))
                elif i in (1, 3):
                    pe.wait_ge(vector_done, vector_at("gate", i // 2, 1))
                else:
                    pe.wait_ge(vector_done, vector_at("rmsb", i - 4))
                for k in range(KC):
                    for c in range(NT):
                        o = (k % 2) * T + c * P
                        last = pe.transpose(PS[:, k // 2, o:o + P], src[:, c, k * P:(k + 1) * P], ident)
                last.then_inc(tensor_done, 1)

            def xt_ready(i):
                pe.wait_ge(scalar_done, scalar_at("xt", i))
                pe.wait_ge(vector_done, vector_at("xt", i))

            def t_gate(step, layer, n):
                xt_ready(2 * layer)
                for c in range(NT):
                    for k in range(KC):
                        last = mm(PS[:, step.banks[c], :], XT[:, k, c * P:(c + 1) * P], w(step)[:, k, :],
                                  start=k == 0, stop=k == KC - 1)
                last.then_inc(tensor_done, 1)

            def unit1(step, g, p):
                xt_ready(1)
                features(step, 2 * p * P).then_inc(tensor_done, 1)

            def t_i(step, g, c):
                xt_ready(1)
                tokens(step, c).then_inc(tensor_done, 1)

            def t_ada(step, i):
                pe.wait_ge(scalar_done, scalar_at("c2"))
                wt = w(step)
                for k in range(KC):
                    last = mm(PS[:, step.banks[0], :], SCT[:, k, :], wt[:, k, :], start=k == 0, stop=k == KC - 1)
                last.then_inc(tensor_done, 1)

            def t_adat(step, i):
                pe.wait_ge(scalar_done, scalar_at("ada", i))
                for j in range(4):
                    last = mm(PS[:, step.banks[0], j:j + 1], MROW[0:1, j * P:(j + 1) * P], ONES[0:1, 0:1])
                last.then_inc(tensor_done, 1)

            def t_hd(step, g):
                pe.wait_ge(scalar_done, scalar_at("q1", g, 1))
                pe.wait_ge(vector_done, vector_at("hf", g))
                for c in range(NT):
                    for h in range(HG):
                        s = slice(c * P, (c + 1) * P)
                        last = mm(PS[:, c, h * P:(h + 1) * P], HK[:, g % 2 * HG + h, s], HQ[:, g % 2 * HG + h, s])
                last.then_inc(tensor_done, 1)

            def t_hm(step, g, i):
                pe.wait_ge(vector_done, vector_at("hy", g, i))
                pe.wait_ge(gpsimd_done, gpsimd_at("hy", g, i))
                for c in range(NT):
                    for h in range(HG):
                        x = HX[:, i % 2 * HG + h, c * P:(c + 1) * P]
                        last = mm(PS[:, step.banks[c], h * P:(h + 1) * P], x, x)
                last.then_inc(tensor_done, 1)

            def t_hc(step, g):
                pe.wait_ge(vector_done, vector_at("hy", g, NL))
                pe.wait_ge(gpsimd_done, gpsimd_at("hy", g, NL))
                for h in range(HG):
                    x = HX[:, NL % 2 * HG + h, :]
                    last = mm(PS[:, 2, h * P:(h + 1) * P], x[:, 0:P], x[:, P:T])
                last.then_inc(tensor_done, 1)

            def t_ho(step, g):
                pe.wait_ge(vector_done, vector_at("hm", g, NL - 1))
                pe.wait_ge(scalar_done, scalar_at("hc", g))
                pe.wait_ge(scalar_done, scalar_at("i", g, 1))
                vv = HV[:, g % 2]
                for h in range(HG):
                    s = slice(h * P, (h + 1) * P)
                    mm(PS[:, 0, s], vv[:, 0, s], HA[:, h, :])
                    mm(PS[:, 1, s], vv[:, 0, s], HC[:, h, :], stop=False)
                    last = mm(PS[:, 1, s], vv[:, 1, s], HA[:, HG + h, :], start=False)
                last.then_inc(tensor_done, 1)

            def t_hr(step, g):
                pe.wait_ge(scalar_done, scalar_at("ho", g))
                for i in range(2):
                    last = mm(PS[:, 2 + i, :], ONES[:], tiles(HS, 2 * i, 2))
                last.then_inc(tensor_done, 1)

            def t_gates(step, c):
                xt_ready(4)
                tokens(step, c, cols=NG, first=2 * P).then_inc(tensor_done, 1)

            def t_feat(step, j):
                xt_ready(4)
                features(step, (j % 2) * 2 * P).then_inc(tensor_done, 1)

            def t_val(step, n, c):
                xt_ready(4)
                tokens(step, c).then_inc(tensor_done, 1)

            def t_qn(step, i):
                pe.wait_ge(scalar_done, scalar_at("feat", 2 if i == 0 else 7))
                for b in range(3):
                    last = mm(PS[:, b, :], bd64, SQ2[:, SQ_SLOTS[i][b], :])
                last.then_inc(tensor_done, 1)

            def t_gcol(step):
                pe.wait_ge(vector_done, vector_at("gd"))
                mm(PS[:, 3, 0:NG], triu, NLS[:, 0, :])
                mm(PS[:, 3, NG:2 * NG], ONES[:], NLS[:, 0, :], stop=False)
                mm(PS[:, 3, NG:2 * NG], triu, NLS[:, 1, :], start=False).then_inc(tensor_done, 1)

            def t_grow(step, part):
                pe.wait_ge(vector_done, vector_at("gsp"))
                pe.wait_ge(gpsimd_done, gpsimd_at("gsp"))
                pairs = range(3) if part == 0 else range(3, 5)
                for b, pr in enumerate(pairs):
                    for a in range(2):
                        j = 2 * pr + a
                        o = a * T
                        mm(PS[:, b, o:o + P], ONES[:], GSP[0][:, j, :])
                        tot = NLS[:, 0, gate_of(j):gate_of(j) + 1].to_broadcast([P, P])
                        mm(PS[:, b, o + P:o + T], ONES[:], tot, stop=False)
                        last = mm(PS[:, b, o + P:o + T], ONES[:], GSP[1][:, j, :], start=False)
                last.then_inc(tensor_done, 1)

            def t_score(step, h):
                q, k, r, _, _ = head(h)
                pe.wait_ge(vector_done, vector_at("qn", 1))
                pe.wait_ge(scalar_done, scalar_at("feat", 5))
                o = PS[:, step.banks[0], :]
                mm(o[:, 0:P], Q2[r:r + HD, q, 0:P], Q2[r:r + HD, k, 0:P])
                mm(o[:, P:3 * P], Q2[r:r + HD, q, P:T], Q2[r:r + HD, k, :]).then_inc(tensor_done, 1)

            def t_turn(step, h):
                pe.wait_ge(vector_done, vector_at("turn", h))
                for j in range(3):
                    last = pe.transpose(PS[:, 2, j * P:(j + 1) * P], SC[:, h % 2, j * P:(j + 1) * P], ident)
                last.then_inc(tensor_done, 1)

            def t_pv(step, h):
                pe.wait_ge(scalar_done, scalar_at("turn", h))
                if h == 0:
                    pe.wait_ge(scalar_done, scalar_at("val", 1, 1))
                _, _, r, vcol, _ = head(h)
                o = PS[r:r + HD, 3, :]
                pt = PTT[:, h % 2, :]
                mm(o[:, 0:P], V2[:, 0, vcol:vcol + HD], pt[:, 0:P])
                mm(o[:, P:T], V2[:, 0, vcol:vcol + HD], pt[:, P:2 * P], stop=False)
                mm(o[:, P:T], V2[:, 1, vcol:vcol + HD], pt[:, 2 * P:3 * P], start=False).then_inc(tensor_done, 1)

            def t_mln(step):
                pe.wait_ge(scalar_done, scalar_at("pv", FOX + ML - 1))
                mm(PS[:, 0, :], bd64, SQ2[:, 0, :]).then_inc(tensor_done, 1)

            def t_out2(step, n):
                pe.wait_ge(vector_done, vector_at("mln"))
                pe.wait_ge(scalar_done, scalar_at("pv", HEADS - 1))
                for c in range(NT):
                    for k in range(KC):
                        last = mm(PS[:, step.banks[c], :], YT[:, k, c * P:(c + 1) * P], w(step)[:, k, :],
                                  start=k == 0, stop=k == KC - 1)
                last.then_inc(tensor_done, 1)

            def t_ff(step, j):
                xt_ready(5)
                features(step, (j % 2) * 2 * P).then_inc(tensor_done, 1)

            def t_down(step, n):
                pe.wait_ge(vector_done, vector_at("ff", FF - 1))
                for k in range(3):
                    pe.wait_ge(slab_loaded[step.slabs[k] % RING], 16 * (step.slabs[k] // RING + 1))
                    for c in range(NT):
                        for j in range(min(KC, FF - k * KC)):
                            kk = k * KC + j
                            last = mm(PS[:, step.banks[c], :], YT[:, kk, c * P:(c + 1) * P], w(step, k)[:, j, :],
                                      start=kk == 0, stop=kk == FF - 1)
                last.then_inc(tensor_done, 1)

            parts = {"ba": t_ba, "k": unit2, "q": unit2, "v": unit2, "zb": unit2, "ah": unit2, "ac": unit2,
                     "az": unit2, "ab": unit2, "gc": t_gc, "norm": t_norm, "vtr": t_vtr, "gk": t_gk, "gkk": t_gkk,
                     "gp": t_gp, "gu": t_gu, "gv": t_gv, "gs": t_gs, "gks": t_gks, "go": t_go, "gr": t_gr,
                     "out": t_out, "pl": t_pl, "xt": t_xt, "gate": t_gate, "f": unit1, "q1": unit1, "z1": unit1,
                     "i": t_i, "ada": t_ada, "adat": t_adat, "hd": t_hd, "hm": t_hm, "hc": t_hc, "ho": t_ho,
                     "hr": t_hr, "gates": t_gates, "feat": t_feat, "val": t_val, "qn": t_qn, "gcol": t_gcol,
                     "grow": t_grow, "score": t_score, "turn": t_turn, "pv": t_pv, "mln": t_mln, "out2": t_out2,
                     "ff": t_ff, "down": t_down}
            pe.wait_ge(cst_loaded, 16)
            pe.wait_ge(gpsimd_done, gpsimd_at("setup"))
            for step in script:
                if "T" in step.engines:
                    claim(step)
                    if len(step.slabs) == 1:
                        loaded(step)
                    parts[step.kind](step, *step.args)

        @block.scalar
        def _(act):
            links = [0]

            def link(ins):
                links[0] += 1
                ins.then_inc(scalar_link, 1)
                act.wait_ge(scalar_link, links[0])

            fn = act.activation

            def s_setup():
                act.dma_start(CST[:], cst_in).then_inc(cst_loaded, 16)
                act.dma_start(WBA[:], wba).then_inc(small_loaded, 16)
                act.dma_start(VEC[:], vec_in).then_inc(small_loaded, 16)
                act.dma_start(X[:], x_in).then_inc(small_loaded, 16)
                act.dma_start(PT[:], pt_in).then_inc(small_loaded, 16)
                act.wait_ge(small_loaded, 16 * 4)
                act.wait_ge(cst_loaded, 16)
                act.wait_ge(gpsimd_done, gpsimd_at("setup"))
                fn(SC8[:], v("c", 0, 8), ACT.Sigmoid).then_inc(scalar_done, 1)

            def s_c1():
                fn(SC8[:], v("c", 0, 8), ACT.Sigmoid).then_inc(scalar_done, 1)

            def s_c2():
                act.wait_ge(vector_done, vector_at("c1"))
                fn(SCT[:], bc(SC8[:], P), ACT.Copy).then_inc(scalar_done, 1)

            def s_ba1():
                act.wait_ge(vector_done, vector_at("ba"))
                fn(flat(BE), TA, ACT.Exp, scale=-1.0)
                fn(TB, TB, ACT.Exp)
                fn(TC[:, 0:8], v("a_log", 0, 8), ACT.Exp).then_inc(scalar_done, 1)

            def s_ba2():
                act.wait_ge(vector_done, vector_at("ba1"))
                fn(TB, TB, ACT.Ln).then_inc(scalar_done, 1)

            def s_conv(kind):
                def part(g, p):
                    act.wait_ge(vector_done, vector_at(kind, g, p))
                    i = conv_units.index((kind, g, p))
                    if kind == "v":
                        if g:
                            act.wait_ge(tensor_done, tensor_at("vtr", 0))
                        fn(tiles(VT, 2 * p, 2), CV[:, i % 2, :], ACT.Silu).then_inc(scalar_done, 1)
                        return
                    if g:
                        act.wait_ge(vector_done, vector_at("norm", 0))
                        act.wait_ge(gpsimd_done, gpsimd_at("norm2", 0))
                    dst = tiles(KT if kind == "k" else QT0, g * HG + 2 * p, 2)
                    link(fn(dst, CV[:, i % 2, :], ACT.Silu))
                    fn(SQ[:, (2 if kind == "q" else 0) + p, :], dst, ACT.Square).then_inc(scalar_done, 1)
                return part

            def s_gc(g):
                act.wait_ge(vector_done, vector_at("gc", g))
                fn(flat(ER), PS[:, 1, :], ACT.Exp)
                fn(EGC, GCOL, ACT.Exp)
                fn(KDF, KDF, ACT.Exp)
                fn(flat(DU), flat(DU), ACT.Exp)
                fn(flat(DL), flat(DL), ACT.Exp, scale=-1.0).then_inc(scalar_done, 1)

            def s_norm(g):
                act.wait_ge(tensor_done, tensor_at("norm", g))
                fn(flat(SQ), PS[:, 0:4, :].rearrange("p b n -> p (b n)"), ACT.Sqrt, bias=EPS[:, 1:2]).then_inc(scalar_done, 1)

            def s_gv(g, c):
                act.wait_ge(tensor_done, tensor_at("gv", g, c))
                fn(tiles(VN, c * HG, HG), PS[:, bank_of("gv", g, c), :], ACT.Copy).then_inc(scalar_done, 1)

            def s_gs(g):
                act.wait_ge(tensor_done, tensor_at("gs", g))
                fn(flat(ST), PS[:, 1, :], ACT.Copy).then_inc(scalar_done, 1)

            def outputs(dst, squares):
                for c in range(NT):
                    src = PS[:, c, :].rearrange("p (h t) -> p h t", h=HG)
                    fn(dst[:, :, c * P:(c + 1) * P], src, ACT.Copy)
                    last = fn(squares[:, :, c * P:(c + 1) * P], src, ACT.Square)
                return last

            def s_go(g):
                act.wait_ge(tensor_done, tensor_at("go", g))
                outputs(OT, SQO).then_inc(scalar_done, 1)

            def root(dst, banks):
                return fn(flat(dst), banks.rearrange("p b n -> p (b n)"), ACT.Sqrt, bias=EPS[:, 0:1], scale=1.0 / P)

            def s_gr(g):
                act.wait_ge(tensor_done, tensor_at("gr", g))
                root(RO, PS[:, 2:4, :]).then_inc(scalar_done, 1)

            def s_zb(g, p):
                act.wait_ge(tensor_done, tensor_at("zb", g, p))
                fn(tiles(ZB, g * HG + 2 * p, 2), PS[:, bank_of("zb", g, p), :], ACT.Silu).then_inc(scalar_done, 1)

            def s_ah(hf, p):
                act.wait_ge(tensor_done, tensor_at("ah", hf, p))
                if hf:
                    act.wait_ge(vector_done, vector_at("ac", hf - 1, p))
                fn(AH[:, p, :], PS[:, bank_of("ah", hf, p), :], ACT.Copy).then_inc(scalar_done, 1)

            def s_az(hf, p):
                act.wait_ge(tensor_done, tensor_at("az", hf, p))
                if hf:
                    act.wait_ge(vector_done, vector_at("ab", hf - 1, p))
                fn(AZ[:, p, :], PS[:, bank_of("az", hf, p), :], ACT.Silu).then_inc(scalar_done, 1)

            def s_pl(layer, n):
                act.wait_ge(tensor_done, tensor_at("pl", layer, n))
                act.wait_ge(vector_done, vector_at(*(("gr", 1) if layer == 0 else ("hr", HGRN_GROUPS - 1))))
                if layer == 0 and n == 0:
                    act.dma_start(LNW[:], lnrow[0].partition_broadcast(P)).then_inc(ln_loaded, 16)
                for c in range(NT):
                    last = fn(PLB[:, c, n * SLAB:(n + 1) * SLAB], PS[:, 2 * n + c, :], ACT.Copy)
                last.then_inc(scalar_done, 1)

            def s_lna(layer):
                act.wait_ge(vector_done, vector_at("lna", layer))
                fn(RSTD[:], AGG[:, :, 1], ACT.Sqrt, bias=EPS[:, 0:1]).then_inc(scalar_done, 1)

            def s_xt(i):
                act.wait_ge(tensor_done, tensor_at("xt", i))
                if i < 4:
                    fn(tiles(XT, 0, 4), PS[:, 0:2, :].rearrange("p b n -> p (b n)"), ACT.Copy).then_inc(scalar_done, 1)
                    return
                act.wait_ge(vector_done, vector_at("rmsb", i - 4))
                for k in range(4):
                    last = fn(XT[:, k, :], PS[:, k // 2, (k % 2) * T:(k % 2 + 1) * T], ACT.Identity,
                              scale=MODG[:, i - 4, k:k + 1], bias=MODT[:, 2 * (i - 4), k:k + 1])
                last.then_inc(scalar_done, 1)

            def s_gate(layer, n):
                if n == 0:
                    act.wait_ge(vector_done, vector_at("lnb", layer))
                    act.dma_start(LNW[:], lnrow[layer + 1].partition_broadcast(P)).then_inc(ln_loaded, 16)
                act.wait_ge(tensor_done, tensor_at("gate", layer, n))
                act.wait_ge(vector_done, vector_at(*(("lnb", layer) if n == 0 else ("gate", layer, 0))))
                for c in range(NT):
                    last = fn(GT[:, c, :], PS[:, bank_of("gate", layer, n) + c, :], ACT.Sigmoid)
                last.then_inc(scalar_done, 1)

            def s_ada(i):
                act.wait_ge(tensor_done, tensor_at("ada", i))
                before = [s for s in script[:where[("ada", i)]] if s.kind == "adat"]
                if before:
                    act.wait_ge(tensor_done, tensor_at(*before[-1].name))
                fn(MROW[:], PS[0:1, bank_of("ada", i), :], ACT.Copy).then_inc(scalar_done, 1)

            def s_lb():
                act.wait_ge(vector_done, vector_at("lb"))
                fn(LT1, LT1, ACT.Exp).then_inc(scalar_done, 1)

            def s_f(g, p):
                act.wait_ge(tensor_done, tensor_at("f", g, p))
                if g == 0:
                    act.wait_ge(vector_done, vector_at("gate", 0, 1))
                if g >= 1:
                    act.wait_ge(vector_done, vector_at("hf", g - 1))
                if g >= 2:
                    act.wait_ge(vector_done, vector_at("hr", g - 2))
                    act.wait_ge(gpsimd_done, gpsimd_at("hy", g - 2, NL))
                b = bank_of("f", g, p)
                fn(tiles(FS, 2 * p, 2), PS[:, b, :], ACT.Sigmoid)
                fn(tiles(HK, g % 2 * HG + 2 * p, 2), PS[:, b, :], ACT.Sigmoid, scale=-1.0).then_inc(scalar_done, 1)

            def s_silu(kind, dst):
                def part(g, p):
                    act.wait_ge(tensor_done, tensor_at(kind, g, p))
                    if g >= 2:
                        act.wait_ge(vector_done, vector_at("hr", g - 2))
                    fn(tiles(dst, g % 2 * HG + 2 * p, 2), PS[:, bank_of(kind, g, p), :], ACT.Silu).then_inc(scalar_done, 1)
                return part

            def s_i(g, c):
                act.wait_ge(tensor_done, tensor_at("i", g, c))
                fn(HV[:, g % 2, c, :], PS[:, bank_of("i", g, c), :], ACT.Copy).then_inc(scalar_done, 1)

            def s_hf(g):
                act.wait_ge(vector_done, vector_at("f", g, 1))
                fn(flat(FS), flat(FS), ACT.Ln).then_inc(scalar_done, 1)

            def s_hx(g, i):
                act.wait_ge(vector_done, vector_at("hx", g, i))
                e = HE[:, i % 2 * HG:(i % 2 + 1) * HG, :]
                if i < NL:
                    s = LEVELS[i]
                    blocks = flat(e).rearrange("p (b s) -> p b s", s=2 * s)
                    fn(blocks[:, :, 0:s], blocks[:, :, 0:s], ACT.Exp, scale=-1.0)
                    fn(blocks[:, :, s:2 * s], blocks[:, :, s:2 * s], ACT.Exp).then_inc(scalar_done, 1)
                    return
                fn(e[:, :, 0:P], e[:, :, 0:P], ACT.Exp, scale=-1.0)
                fn(e[:, :, P:T], HB[:, g % 2 * HG:(g % 2 + 1) * HG, P:T], ACT.Exp).then_inc(scalar_done, 1)

            def s_hc(g):
                act.wait_ge(tensor_done, tensor_at("hc", g))
                fn(flat(HC), PS[:, 2, :], ACT.Copy).then_inc(scalar_done, 1)

            def s_ho(g):
                act.wait_ge(tensor_done, tensor_at("ho", g))
                act.wait_ge(vector_done, vector_at("hy", g, NL))
                act.wait_ge(gpsimd_done, gpsimd_at("hy", g, NL))
                outputs(HOT, HS).then_inc(scalar_done, 1)

            def s_hr(g):
                act.wait_ge(tensor_done, tensor_at("hr", g))
                root(HRN, PS[:, 2:4, :]).then_inc(scalar_done, 1)

            def s_rms(i):
                act.wait_ge(vector_done, vector_at(*(("gate", 1, 1) if i == 0 else ("out2", 1))))
                for c in range(NT):
                    last = fn(XN[:, c, :], X[:, c, :], ACT.Square, accum_out=SUMSQ[:, c:c + 1])
                link(last)
                fn(RSTD[:], SUMSQ[:], ACT.Sqrt, scale=1.0 / D, bias=EPS[:, 1:2]).then_inc(scalar_done, 1)

            def s_feat(j):
                b = bank_of("feat", j)
                if j in (3, 4):
                    act.wait_ge(vector_done, vector_at("feat", j))
                    for a in range(2):
                        t = 2 * j + a
                        last = fn(Q2[:, t, :], CV2[:, j % 2, a * T:(a + 1) * T], ACT.Silu, bias=v("mlb", t - QT["mq"]))
                    last.then_inc(scalar_done, 1)
                    return
                act.wait_ge(tensor_done, tensor_at("feat", j))
                if j == 5:
                    fn(tiles(Q2, 2 * j, 2), PS[:, b, :], ACT.Sigmoid).then_inc(scalar_done, 1)
                    return
                if j in (6, 7):
                    act.wait_ge(vector_done, vector_at("qn", 0))
                slot = SQ_SLOTS[j // 6][j % 3]
                fn(tiles(Q2, 2 * j, 2), PS[:, b, :], ACT.Copy)
                fn(SQ2[:, slot, :], PS[:, b, :], ACT.Square).then_inc(scalar_done, 1)

            def s_qn(i):
                act.wait_ge(tensor_done, tensor_at("qn", i))
                for b in range(3):
                    last = fn(SQ2[:, SQ_SLOTS[i][b], :], PS[:, b, :], ACT.Sqrt, scale=1.0 / HD, bias=EPS[:, 1:2])
                last.then_inc(scalar_done, 1)

            def s_ga():
                act.wait_ge(vector_done, vector_at("ga"))
                fn(flat(GB), flat(GB), ACT.Exp).then_inc(scalar_done, 1)

            def s_gb():
                act.wait_ge(vector_done, vector_at("gb"))
                fn(flat(GB), flat(GB), ACT.Ln).then_inc(scalar_done, 1)

            def s_val(n, c):
                act.wait_ge(tensor_done, tensor_at("val", n, c))
                fn(V2[:, c, n * SLAB:(n + 1) * SLAB], PS[:, bank_of("val", n, c), :], ACT.Copy).then_inc(scalar_done, 1)

            def s_gm():
                act.wait_ge(vector_done, vector_at("gm"))
                for h in range(FOX, FOX + ML):
                    for c in range(NT):
                        fn(B2[:, h, rows(c)], B2[:, h, rows(c)], ACT.Exp, bias=MX[:, h, c:c + 1])
                fn(EM, MX[:, FOX:FOX + ML, :], ACT.Exp).then_inc(scalar_done, 1)

            def s_score(h):
                act.wait_ge(vector_done, vector_at("score", h))
                for c in range(NT):
                    last = fn(SC[:, h % 2, rows(c)], SC[:, h % 2, rows(c)], ACT.Exp, bias=MX[:, h, c:c + 1],
                              accum_out=SM[:, h, c:c + 1])
                last.then_inc(scalar_done, 1)

            def s_turn(h):
                act.wait_ge(tensor_done, tensor_at("turn", h))
                if h >= 2:
                    act.wait_ge(tensor_done, tensor_at("pv", h - 2))
                fn(PTT[:, h % 2, :], PS[:, 2, 0:3 * P], ACT.Copy).then_inc(scalar_done, 1)

            def s_pv(h):
                act.wait_ge(tensor_done, tensor_at("pv", h))
                t = h // 2
                if FOX // 2 <= t < (FOX + ML) // 2:
                    a = t - FOX // 2
                    fn(SQ2[:, 0, a * T:(a + 1) * T], PS[:, 3, 0:T], ACT.Square)
                fn(YT[:, t, :], PS[:, 3, 0:T], ACT.Copy).then_inc(scalar_done, 1)

            def s_mln():
                act.wait_ge(tensor_done, tensor_at("mln"))
                fn(SQ2[:, 1, :], PS[:, 0, :], ACT.Sqrt, scale=1.0 / HD, bias=EPS[:, 1:2]).then_inc(scalar_done, 1)

            def s_ff(j):
                act.wait_ge(tensor_done, tensor_at("ff", j))
                if j >= 2:
                    act.wait_ge(vector_done, vector_at("ff", j - 2))
                fn(CV2[:, j % 2, 0:T], PS[:, bank_of("ff", j), 0:T], ACT.Silu).then_inc(scalar_done, 1)

            parts = {"setup": s_setup, "c1": s_c1, "c2": s_c2, "ba1": s_ba1, "ba2": s_ba2, "k": s_conv("k"),
                     "q": s_conv("q"), "v": s_conv("v"), "gc": s_gc, "norm": s_norm, "gv": s_gv, "gs": s_gs,
                     "go": s_go, "gr": s_gr, "zb": s_zb, "ah": s_ah, "az": s_az, "pl": s_pl, "lna": s_lna,
                     "xt": s_xt, "gate": s_gate, "ada": s_ada, "lb": s_lb, "f": s_f, "q1": s_silu("q1", HQ),
                     "z1": s_silu("z1", HZ), "i": s_i, "hf": s_hf, "hx": s_hx, "hc": s_hc, "ho": s_ho,
                     "hr": s_hr, "rms": s_rms, "feat": s_feat, "qn": s_qn, "ga": s_ga, "gb": s_gb, "val": s_val,
                     "gm": s_gm, "score": s_score, "turn": s_turn, "pv": s_pv, "mln": s_mln, "ff": s_ff}
            mine = 0
            for step in script:
                if "S" in step.engines:
                    if mine:
                        act.wait_ge(scalar_done, mine)
                    parts[step.kind](*step.args)
                    mine += 1

        @block.vector
        def _(dve):
            links = [0]

            def link(ins):
                links[0] += 1
                ins.then_inc(vector_link, 1)
                dve.wait_ge(vector_link, links[0])

            tt, ts, stt = dve.tensor_tensor, dve.tensor_scalar, dve.scalar_tensor_tensor

            def conv(acc, src, weight, taps):
                for a in range(2):
                    last = ts(acc[:, a, :], src[:, a, :], weight(a, taps - 1), None, ALU.mult)
                for back in range(1, taps):
                    link(last)
                    for a in range(2):
                        last = stt(acc[:, a, back:T], src[:, a, 0:T - back], weight(a, taps - 1 - back),
                                   acc[:, a, back:T], ALU.mult, ALU.add)
                return last

            def two(ap):
                return ap.rearrange("p (a t) -> p a t", a=2)

            def v_ba():
                dve.wait_ge(tensor_done, tensor_at("ba"))
                dve.wait_ge(small_loaded, 16 * 4)
                for g in range(2):
                    for c in range(NT):
                        o = g * 8 + c * HG
                        dve.tensor_copy(TA[:, o:o + HG], PS[:, 0, c * 16 + g * HG:c * 16 + (g + 1) * HG])
                        last = tt(TD[:, o:o + HG], PS[:, 0, c * 16 + 8 + g * HG:c * 16 + 8 + (g + 1) * HG],
                                  v("dt", g * HG, HG), ALU.add)
                link(last)
                stt(TB, TD, -1.0, TD, ALU.mult, ALU.min).then_inc(vector_done, 1)

            def v_ba1():
                dve.wait_ge(scalar_done, scalar_at("ba1"))
                link(ts(flat(BE), flat(BE), 1.0, None, ALU.add))
                dve.reciprocal(flat(BE), flat(BE))
                ts(TB, TB, 1.0, None, ALU.add).then_inc(vector_done, 1)

            def v_ba2():
                dve.wait_ge(scalar_done, scalar_at("ba2"))
                link(stt(TB, TD, 0.0, TB, ALU.max, ALU.add))
                for g in range(2):
                    for c in range(NT):
                        o = g * 8 + c * HG
                        last = stt(GG[:, g, c * HG:(c + 1) * HG], TB[:, o:o + HG], -1.0, TC[:, g * HG:(g + 1) * HG],
                                   ALU.mult, ALU.mult)
                last.then_inc(vector_done, 1)

            def v_c1():
                dve.wait_ge(scalar_done, scalar_at("c1"))
                tt(SC8[:], SC8[:], v("c", 0, 8), ALU.mult).then_inc(vector_done, 1)

            def v_conv(kind, first):
                def part(g, p):
                    dve.wait_ge(tensor_done, tensor_at(kind, g, p))
                    i = conv_units.index((kind, g, p))
                    if i >= 2:
                        dve.wait_ge(scalar_done, scalar_at(*conv_units[i - 2]))
                    tile = first + g * HG + 2 * p
                    conv(two(CV[:, i % 2, :]), two(PS[:, bank_of(kind, g, p), :]),
                                lambda a, j: v("conv_b", (tile + a) * 4 + j), 4).then_inc(vector_done, 1)
                return part

            def v_gc(g):
                dve.wait_ge(tensor_done, tensor_at("gc", g))
                if g:
                    dve.wait_ge(tensor_done, tensor_at("go", 0))
                link(dve.tensor_copy(GCOL, PS[:, 2, 0:8]))
                r = PS[:, 0:2, :].rearrange("p b (h j) -> p (b h) j", h=HG)
                link(tt(DU, r, bc(GCOL, P), ALU.subtract))
                ts(flat(DL), flat(DU), 0.0, None, ALU.max)
                link(dve.tensor_copy(KDF, DU[:, 0:HG, P - 1]))
                ts(flat(DU), flat(DU), 0.0, None, ALU.min).then_inc(vector_done, 1)

            def v_gc2(g):
                dve.wait_ge(scalar_done, scalar_at("gc", g))
                tt(DL, DL, bc(BE[:, g, :], P), ALU.mult)
                stt(DU, DU, SCALE128, rep(triu, 8), ALU.mult, ALU.mult)
                tt(BEG, EGC, BE[:, g, :], ALU.mult).then_inc(vector_done, 1)

            def v_norm(g):
                dve.wait_ge(scalar_done, scalar_at("norm", g))
                link(dve.reciprocal(flat(SQ), flat(SQ)))
                tt(tiles(KT, g * HG, HG), tiles(KT, g * HG, HG), flat(SQ[:, 0:2, :]), ALU.mult).then_inc(vector_done, 1)

            def heads4(bank):
                return PS[:, bank, :].rearrange("p (h j) -> p h j", h=HG)

            def heads8(bank):
                return PS[:, bank:bank + 2, :].rearrange("p b (h j) -> p (b h) j", h=HG)

            def v_vtr(g):
                dve.wait_ge(tensor_done, tensor_at("vtr", g))
                tt(BV, heads8(0), bc(BE[:, g, :], P), ALU.mult).then_inc(vector_done, 1)

            def v_gk(g):
                dve.wait_ge(tensor_done, tensor_at("gk", g))
                dve.wait_ge(scalar_done, scalar_at("gc", g))
                tt(KD, heads4(2), bc(KDF, P), ALU.mult).then_inc(vector_done, 1)

            def v_gkk(g):
                dve.wait_ge(tensor_done, tensor_at("gkk", g))
                tt(DL, heads8(0), DL, ALU.mult)
                tt(DU, heads8(2), DU, ALU.mult)
                q = QT0[:, g * HG:(g + 1) * HG, P:T]
                stt(q, q, SCALE128, ER, ALU.mult, ALU.mult).then_inc(vector_done, 1)

            def v_gp(g, i):
                dve.wait_ge(tensor_done, tensor_at("gp", g, i))
                tt(PM, heads8(0), rep(lvl[i], 8), ALU.mult).then_inc(vector_done, 1)

            def v_gu(g, i):
                dve.wait_ge(tensor_done, tensor_at("gu", g, i))
                last = tt(U, U, heads8(2), ALU.subtract)
                if i < NL - 1:
                    last = tt(XI, XI, heads8(0), ALU.subtract)
                last.then_inc(vector_done, 1)

            def v_gks(g):
                dve.wait_ge(tensor_done, tensor_at("gks", g))
                link(tt(PM[:, 0:HG, :], heads4(2), bc(BEG[:, HG:2 * HG], P), ALU.mult))
                tt(BV[:, HG:2 * HG, :], BV[:, HG:2 * HG, :], PM[:, 0:HG, :], ALU.subtract).then_inc(vector_done, 1)

            def gated(o, r, gain, z, dst):
                link(dve.reciprocal(flat(r), flat(r)))
                link(tt(flat(o), flat(o), flat(r), ALU.mult))
                return stt(dst, flat(o), gain, z, ALU.mult, ALU.mult)

            def v_gr(g):
                dve.wait_ge(scalar_done, scalar_at("gr", g))
                dve.wait_ge(scalar_done, scalar_at("zb", g, 1))
                gated(OT, RO, v("gdn_g"), tiles(ZB, g * HG, HG), tiles(YT, KC + g * HG, HG)).then_inc(vector_done, 1)

            def v_ac(hf, p):
                dve.wait_ge(tensor_done, tensor_at("ac", hf, p))
                dve.wait_ge(scalar_done, scalar_at("ah", hf, p))
                link(tt(AH[:, p, :], AH[:, p, :], PS[:, bank_of("ac", hf, p), :], ALU.mult))
                conv(two(AC[:, p, :]), two(AH[:, p, :]),
                            lambda a, j: v("conv_a", (hf * HG + 2 * p + a) * 3 + j), 3).then_inc(vector_done, 1)

            def v_ab(hf, p):
                dve.wait_ge(tensor_done, tensor_at("ab", hf, p))
                dve.wait_ge(scalar_done, scalar_at("az", hf, p))
                link(tt(AC[:, p, :], AC[:, p, :], PS[:, bank_of("ab", hf, p), :], ALU.mult))
                tt(tiles(YT, hf * HG + 2 * p, 2), AC[:, p, :], AZ[:, p, :], ALU.mult).then_inc(vector_done, 1)

            def v_out(layer, n):
                dve.wait_ge(tensor_done, tensor_at("out", layer, n))
                for c in range(NT):
                    x = X[:, c, n * SLAB:(n + 1) * SLAB]
                    last = stt(x, x, ALPHA, PS[:, bank_of("out", layer, n) + c, :], ALU.mult, ALU.add)
                last.then_inc(vector_done, 1)

            def v_lna(layer):
                for c in range(NT):
                    for n in range(2):
                        last = dve.bn_stats(STAT[:, c, n, :], X[:, c, n * SLAB:(n + 1) * SLAB])
                link(last)
                for c in range(NT):
                    last = dve.bn_aggr(AGG[:, c, :], STAT[:, c, :, :])
                last.then_inc(vector_done, 1)

            def v_lnb(layer):
                dve.wait_ge(scalar_done, scalar_at("lna", layer))
                link(dve.reciprocal(RSTD[:], RSTD[:]))
                for c in range(NT):
                    last = ts(X[:, c, :], X[:, c, :], AGG[:, c, 0:1], RSTD[:, c:c + 1], ALU.subtract, ALU.mult)
                link(last)
                dve.wait_ge(ln_loaded, 16 * (layer + 1))
                for c in range(NT):
                    last = tt(X[:, c, :], X[:, c, :], LNW[:, 0, :], ALU.mult)
                link(last)
                for c in range(NT):
                    last = tt(X[:, c, :], X[:, c, :], LNW[:, 1, :], ALU.add)
                last.then_inc(vector_done, 1)

            def v_xt(i):
                dve.wait_ge(tensor_done, tensor_at("xt", i))
                if i < 4:
                    dve.tensor_copy(tiles(XT, 4, 4), PS[:, 2:4, :].rearrange("p b n -> p (b n)")).then_inc(vector_done, 1)
                    return
                for k in range(4, KC):
                    last = ts(XT[:, k, :], PS[:, k // 2, (k % 2) * T:(k % 2 + 1) * T], MODG[:, i - 4, k:k + 1],
                              MODT[:, 2 * (i - 4), k:k + 1], ALU.mult, ALU.add)
                last.then_inc(vector_done, 1)

            def v_gate(layer, n):
                dve.wait_ge(scalar_done, scalar_at("gate", layer, n))
                dve.wait_ge(scalar_done, scalar_at("pl", layer, n))
                s = slice(n * SLAB, (n + 1) * SLAB)
                link(tt(GT, GT, PLB[:, :, s], ALU.mult))
                tt(X[:, :, s], X[:, :, s], GT, ALU.add).then_inc(vector_done, 1)

            def v_ada(i):
                dve.wait_ge(tensor_done, tensor_at("ada", i))
                dve.wait_ge(ln_loaded, 48)
                g = LNW[:, i // 6, (i % 2) * SLAB:(i % 2 + 1) * SLAB]
                tt(g, g, PS[:, bank_of("ada", i), :], ALU.add).then_inc(vector_done, 1)

            def v_adat(i):
                dve.wait_ge(tensor_done, tensor_at("adat", i))
                r, o = MOD_ROW[i], (i % 2) * 4
                tt(MODT[:, r, o:o + 4], PS[:, bank_of("adat", i), 0:4], v("bada", r * KC + o, 4), ALU.add).then_inc(vector_done, 1)

            def v_mod(i):
                stt(MODG[:, i, :], MODT[:, 2 * i + 1, :], 1.0, v("n1" if i == 0 else "n2", 0, KC),
                           ALU.add, ALU.mult).then_inc(vector_done, 1)

            def v_lb():
                link(tt(LT2, v("lb", 0, 16), v("lb", 16, 16), ALU.max))
                tt(LT1[:, 0:16], v("lb", 0, 16), LT2, ALU.subtract)
                tt(LT1[:, 16:32], v("lb", 16, 16), LT2, ALU.subtract).then_inc(vector_done, 1)

            def v_lb2():
                dve.wait_ge(scalar_done, scalar_at("lb"))
                link(tt(LT2, LT1[:, 0:16], LT1[:, 16:32], ALU.add))
                link(dve.reciprocal(LT2, LT2))
                link(tt(LBV, LT1[:, 16:32], LT2, ALU.mult))
                ts(OML, LBV, -1.0, 1.0, ALU.mult, ALU.add).then_inc(vector_done, 1)

            def v_f(g, p):
                dve.wait_ge(scalar_done, scalar_at("f", g, p))
                for a in range(2):
                    t, h = g * HG + 2 * p + a, 2 * p + a
                    ts(FS[:, h, :], FS[:, h, :], OML[:, t:t + 1], LBV[:, t:t + 1], ALU.mult, ALU.add)
                    k = HK[:, g % 2 * HG + h, :]
                    last = ts(k, k, OML[:, t:t + 1], None, ALU.mult)
                last.then_inc(vector_done, 1)

            def v_hf(g):
                dve.wait_ge(scalar_done, scalar_at("hf", g))
                for h in range(HG):
                    for c in range(NT):
                        s = slice(c * P, (c + 1) * P)
                        last = dve.tensor_tensor_scan(HB[:, g % 2 * HG + h, s], ONES[:], FS[:, h, s], 0.0,
                                                      ALU.mult, ALU.add)
                last.then_inc(vector_done, 1)

            def v_hd(g):
                dve.wait_ge(tensor_done, tensor_at("hd", g))
                tt(HA, heads8(0), rep(ident, 8), ALU.mult).then_inc(vector_done, 1)

            def v_hx(g, i):
                if i >= 2:
                    dve.wait_ge(gpsimd_done, gpsimd_at("hy", g, i - 2))
                b = HB[:, g % 2 * HG:(g % 2 + 1) * HG, :]
                e = HE[:, i % 2 * HG:(i % 2 + 1) * HG, :]
                if i == NL:
                    tt(e[:, :, 0:P], b[:, :, 0:P], b[:, :, P - 1:P].to_broadcast([P, HG, P]), ALU.subtract).then_inc(vector_done, 1)
                    return
                s = LEVELS[i]
                n = HG * T // (2 * s)
                b3 = flat(b).rearrange("p (b s) -> p b s", s=2 * s)
                e3 = flat(e).rearrange("p (b s) -> p b s", s=2 * s)
                tt(e3, b3, b3[:, :, s - 1:s].to_broadcast([P, n, 2 * s]), ALU.subtract).then_inc(vector_done, 1)

            def v_hy(g, i):
                dve.wait_ge(scalar_done, scalar_at("hx", g, i))
                dve.wait_ge(scalar_done, scalar_at("q1", g, 1))
                if i >= 2:
                    dve.wait_ge(tensor_done, tensor_at("hm", g, i - 2))
                r = slice(i % 2 * HG, (i % 2 + 1) * HG)
                q = HQ[:, g % 2 * HG:(g % 2 + 1) * HG, :]
                if i == NL:
                    tt(HX[:, r, P:T], q[:, :, P:T], HE[:, r, P:T], ALU.mult).then_inc(vector_done, 1)
                    return
                s = LEVELS[i]
                x, e, y = (flat(a).rearrange("p (b s) -> p b s", s=2 * s)[:, :, s:2 * s]
                           for a in (HX[:, r, :], HE[:, r, :], q))
                tt(x, y, e, ALU.mult).then_inc(vector_done, 1)

            def v_hm(g, i):
                dve.wait_ge(tensor_done, tensor_at("hm", g, i))
                dve.copy_predicated(HA, rep(lvl[i].bitcast(U32), 8), heads8(script[where[("hm", g, i)]].banks[0])).then_inc(vector_done, 1)

            def v_hr(g):
                dve.wait_ge(scalar_done, scalar_at("hr", g))
                dve.wait_ge(scalar_done, scalar_at("z1", g, 1))
                gated(HOT, HRN, v("hgrn_g"), tiles(HZ, g % 2 * HG, HG), tiles(YT, g * HG, HG)).then_inc(vector_done, 1)

            def v_rmsb(i):
                dve.wait_ge(scalar_done, scalar_at("rms", i))
                link(dve.reciprocal(RSTD[:], RSTD[:]))
                for c in range(NT):
                    last = ts(XN[:, c, :], X[:, c, :], RSTD[:, c:c + 1], None, ALU.mult)
                last.then_inc(vector_done, 1)

            def v_gates(c):
                dve.wait_ge(tensor_done, tensor_at("gates", c))
                tt(GA[:, c, :], PS[:, bank_of("gates", c), 0:NG], v("gate_bias", 0, NG), ALU.add).then_inc(vector_done, 1)

            def v_ga():
                stt(flat(GB), flat(GA), -1.0, flat(GA), ALU.mult, ALU.min).then_inc(vector_done, 1)

            def v_gb():
                dve.wait_ge(scalar_done, scalar_at("ga"))
                ts(flat(GB), flat(GB), 1.0, None, ALU.add).then_inc(vector_done, 1)

            def v_gd():
                dve.wait_ge(scalar_done, scalar_at("gb"))
                link(stt(flat(NLS), flat(GA), 0.0, flat(GB), ALU.min, ALU.subtract))
                ts(flat(NLS), flat(NLS), -1.0, None, ALU.mult).then_inc(vector_done, 1)

            def spread(eng, lnk, c, tmp):
                eng.tensor_tensor(GSP[c][:, 0:FOX, :], rep(triu, FOX), bc(NLS[:, c, 0:FOX], P), ALU.mult)
                eng.tensor_tensor(GSP[c][:, FOX:FOX + ML, :], rep(triu, ML), bc(NLS[:, c, FOX + ML:NG], P), ALU.mult)
                lnk(eng.tensor_tensor(tmp, rep(ident, ML), bc(GA[:, c, FOX:FOX + ML], P), ALU.mult))
                o = GSP[c][:, FOX:FOX + ML, :]
                return eng.tensor_tensor(o, o, tmp, ALU.add)

            def v_gsp():
                spread(dve, link, 1, flat(PTT)[:, 0:ML * P].rearrange("p (h k) -> p h k", h=ML)).then_inc(vector_done, 1)

            def v_gcol():
                dve.wait_ge(tensor_done, tensor_at("gcol"))
                ts(flat(GCC), PS[:, 3, 0:2 * NG], -1.0, None, ALU.mult).then_inc(vector_done, 1)

            def v_grow(part):
                dve.wait_ge(tensor_done, tensor_at("grow", part))
                for j in range(FOX) if part == 0 else range(FOX, FOX + ML):
                    b, o = (j - (0 if part == 0 else FOX)) // 2, (j % 2) * T
                    for c in range(NT):
                        last = stt(B2[:, j, rows(c)], PS[:, b, o:o + (c + 1) * P], GCC[:, c, gate_of(j):gate_of(j) + 1],
                                   mask3[:, rows(c)], ALU.add, ALU.add)
                last.then_inc(vector_done, 1)

            def v_gm():
                for h in range(FOX, FOX + ML):
                    for c in range(NT):
                        last = dve.tensor_reduce(MX[:, h, c:c + 1], B2[:, h, rows(c)], AX.X, ALU.max)
                link(last)
                for h in range(FOX, FOX + ML):
                    last = tt(MX[:, h, :], MX[:, h, :], GCC[:, :, gate_of(h)], ALU.max)
                link(last)
                ts(MX[:, FOX:FOX + ML, :], MX[:, FOX:FOX + ML, :], -1.0, None, ALU.mult).then_inc(vector_done, 1)

            def v_feat(j):
                dve.wait_ge(tensor_done, tensor_at("feat", j))
                conv(two(CV2[:, j % 2, :]), two(PS[:, bank_of("feat", j), :]),
                            lambda a, k: v("mlw", (2 * j - QT["mq"] + a) * 4 + k), 4).then_inc(vector_done, 1)

            def v_qn(i):
                dve.wait_ge(scalar_done, scalar_at("qn", i))
                for b in range(3):
                    last = dve.reciprocal(SQ2[:, SQ_SLOTS[i][b], :], SQ2[:, SQ_SLOTS[i][b], :])
                link(last)
                for b in range(3):
                    for a in range(2):
                        n = 2 * b + a
                        t = n + (0 if i == 0 else QT["bq"])
                        gain = v((("foxq", "foxk"), ("mobaq", "mobak"))[i][n // 3])
                        last = stt(Q2[:, t, :], Q2[:, t, :], gain, SQ2[:, SQ_SLOTS[i][b], a * T:(a + 1) * T],
                                   ALU.mult, ALU.mult)
                last.then_inc(vector_done, 1)

            def v_mb():
                for i in range(MOBA):
                    slope = 2.0 ** (-8.0 * (i + 1) / MOBA)
                    last = stt(B2[:, FOX + ML + i, :], dist3, slope, mask3, ALU.mult, ALU.add)
                last.then_inc(vector_done, 1)

            def v_score(h):
                dve.wait_ge(tensor_done, tensor_at("score", h))
                dve.wait_ge(scalar_done, scalar_at("gm"))
                if h >= 2:
                    dve.wait_ge(tensor_done, tensor_at("turn", h - 2))
                b = PS[:, bank_of("score", h), 0:3 * P]
                s = SC[:, h % 2, :]
                if FOX <= h < FOX + ML:
                    for c in range(NT):
                        last = stt(s[:, rows(c)], b[:, rows(c)], SCALE64, B2[:, h, rows(c)], ALU.mult, ALU.mult,
                                   accum_out=SM[:, h, c:c + 1])
                    last.then_inc(vector_done, 1)
                    return
                link(stt(s, b, SCALE64, B2[:, h, :], ALU.mult, ALU.add))
                for c in range(NT):
                    last = dve.tensor_reduce(MX[:, h, c:c + 1], s[:, rows(c)], AX.X, ALU.max, negate=True)
                last.then_inc(vector_done, 1)

            def v_turn(h):
                if FOX <= h < FOX + ML:
                    link(stt(RI[:, h, :], SM[:, h, :], -1.0, SM[:, h, :], ALU.mult, ALU.max))
                    link(tt(RI[:, h, :], RI[:, h, :], EM[:, h - FOX, :], ALU.max))
                    link(dve.reciprocal(RI[:, h, :], RI[:, h, :]))
                else:
                    dve.wait_ge(scalar_done, scalar_at("score", h))
                    link(dve.reciprocal(RI[:, h, :], SM[:, h, :]))
                s = SC[:, h % 2, :]
                for c in range(NT):
                    last = ts(s[:, rows(c)], s[:, rows(c)], RI[:, h, c:c + 1], None, ALU.mult)
                last.then_inc(vector_done, 1)

            def v_mln():
                dve.wait_ge(scalar_done, scalar_at("mln"))
                link(dve.reciprocal(SQ2[:, 1, :], SQ2[:, 1, :]))
                y = tiles(YT, FOX // 2, 2)
                link(tt(y, y, SQ2[:, 1, :], ALU.mult))
                for a in range(2):
                    t = FOX // 2 + a
                    last = stt(YT[:, t, :], YT[:, t, :], v("mlg", a), Q2[:, QT["mo"] + a, :], ALU.mult, ALU.mult)
                last.then_inc(vector_done, 1)

            def residual(name, n, gain):
                dve.wait_ge(tensor_done, tensor_at(name, n))
                b = bank_of(name, n)
                s = slice(n * SLAB, (n + 1) * SLAB)
                for c in range(NT):
                    last = tt(XN[:, c, s], PS[:, b + c, :], LNW[:, gain, s], ALU.mult)
                link(last)
                return tt(X[:, :, s], X[:, :, s], XN[:, :, s], ALU.add)

            def v_out2(n):
                residual("out2", n, 0).then_inc(vector_done, 1)

            def v_down(n):
                residual("down", n, 1).then_inc(vector_done, 1)

            def v_ff(j):
                dve.wait_ge(scalar_done, scalar_at("ff", j))
                tt(YT[:, j, :], CV2[:, j % 2, 0:T], PS[:, bank_of("ff", j), T:2 * T], ALU.mult).then_inc(vector_done, 1)

            parts = {"ba": v_ba, "ba1": v_ba1, "ba2": v_ba2, "c1": v_c1, "k": v_conv("k", 8), "q": v_conv("q", 0),
                     "v": v_conv("v", 16), "gc": v_gc, "gc2": v_gc2, "norm": v_norm, "vtr": v_vtr, "gk": v_gk,
                     "gkk": v_gkk, "gp": v_gp, "gu": v_gu, "gks": v_gks, "gr": v_gr, "ac": v_ac, "ab": v_ab,
                     "out": v_out, "lna": v_lna, "lnb": v_lnb, "xt": v_xt, "gate": v_gate, "ada": v_ada,
                     "adat": v_adat, "mod": v_mod, "lb": v_lb, "lb2": v_lb2, "f": v_f, "hf": v_hf, "hd": v_hd,
                     "hx": v_hx, "hy": v_hy, "hm": v_hm, "hr": v_hr, "rmsb": v_rmsb, "gates": v_gates,
                     "ga": v_ga, "gb": v_gb, "gd": v_gd, "gsp": v_gsp, "gcol": v_gcol, "grow": v_grow, "gm": v_gm,
                     "feat": v_feat, "qn": v_qn, "mb": v_mb, "score": v_score, "turn": v_turn, "mln": v_mln,
                     "out2": v_out2, "down": v_down, "ff": v_ff}
            dve.wait_ge(cst_loaded, 16)
            dve.wait_ge(gpsimd_done, gpsimd_at("setup"))
            mine = 0
            for step in script:
                if "V" in step.engines:
                    if mine:
                        dve.wait_ge(vector_done, mine)
                    parts[step.kind](*step.args)
                    mine += 1

        @block.gpsimd
        def _(pool):
            links = [0]

            def link(ins):
                links[0] += 1
                ins.then_inc(gpsimd_link, 1)
                pool.wait_ge(gpsimd_link, links[0])

            tt = pool.tensor_tensor

            def g_setup():
                pool.memset(ONES[:], 1.0)
                pool.memset(EPS[:, 0:1], LN_EPS)
                last = pool.memset(EPS[:, 1:2], L2_EPS)
                pool.wait_ge(cst_loaded, 16)
                last.then_inc(gpsimd_done, 1)

            def g_gt(g):
                pool.wait_ge(vector_done, vector_at("ba2"))
                if g:
                    pool.wait_ge(vector_done, vector_at("gr", 0))
                tt(PM, rep(triu, 8), bc(GG[:, g, :], P), ALU.mult).then_inc(gpsimd_done, 1)

            def g_gc2(g):
                if g:
                    pool.wait_ge(vector_done, vector_at("gr", 0))
                pool.tensor_copy(U, rep(ident, 8))
                pool.tensor_copy(XI, rep(ident, 8)).then_inc(gpsimd_done, 1)

            def g_norm2(g):
                pool.wait_ge(vector_done, vector_at("norm", g))
                q = tiles(QT0, g * HG, HG)
                tt(q, q, flat(SQ[:, 2:4, :]), ALU.mult).then_inc(gpsimd_done, 1)

            def g_hy(g, i):
                pool.wait_ge(scalar_done, scalar_at("hx", g, i))
                if i >= 2:
                    pool.wait_ge(tensor_done, tensor_at("hm", g, i - 2))
                r = slice(i % 2 * HG, (i % 2 + 1) * HG)
                k = HK[:, g % 2 * HG:(g % 2 + 1) * HG, :]
                if i == NL:
                    tt(HX[:, r, 0:P], k[:, :, 0:P], HE[:, r, 0:P], ALU.mult).then_inc(gpsimd_done, 1)
                    return
                s = LEVELS[i]
                x, e, y = (flat(a).rearrange("p (b s) -> p b s", s=2 * s)[:, :, 0:s]
                           for a in (HX[:, r, :], HE[:, r, :], k))
                tt(x, y, e, ALU.mult).then_inc(gpsimd_done, 1)

            def g_gsp():
                pool.wait_ge(vector_done, vector_at("gd"))
                tmp = flat(SC)[:, 0:ML * P].rearrange("p (h k) -> p h k", h=ML)
                tt(GSP[0][:, 0:FOX, :], rep(triu, FOX), bc(NLS[:, 0, 0:FOX], P), ALU.mult)
                tt(GSP[0][:, FOX:FOX + ML, :], rep(triu, ML), bc(NLS[:, 0, FOX + ML:NG], P), ALU.mult)
                link(tt(tmp, rep(ident, ML), bc(GA[:, 0, FOX:FOX + ML], P), ALU.mult))
                o = GSP[0][:, FOX:FOX + ML, :]
                tt(o, o, tmp, ALU.add).then_inc(gpsimd_done, 1)

            parts = {"setup": g_setup, "gt": g_gt, "gc2": g_gc2, "norm2": g_norm2, "hy": g_hy, "gsp": g_gsp}
            mine = 0
            for step in script:
                if "G" in step.engines:
                    if mine:
                        pool.wait_ge(gpsimd_done, mine)
                    parts[step.kind](*step.args)
                    mine += 1


def _blocks(w):
    return w.reshape(w.shape[0] // P, P, w.shape[1]).transpose(1, 0, 2)


def _slab(name, w):
    kind, a = name[0], name[1:]
    if kind in ("k", "q", "v", "zb"):
        at = {"q": 4096, "k": 5120, "v": 6144, "zb": 7168}[kind] + a[0] * SLAB
        s = _blocks(w["even"][:, at:at + SLAB])
    elif kind in ("ah", "ac", "ab", "az"):
        at = {"ah": 0, "ac": 1024, "ab": 2048, "az": 3072}[kind] + a[0] * SLAB
        s = _blocks(w["even"][:, at:at + SLAB])
    elif kind in ("q1", "f", "i", "z1"):
        at = {"q1": 0, "f": 2048, "i": 4096, "z1": 6144}[kind] + a[0] * SLAB
        s = _blocks(w["odd"][:, at:at + SLAB])
    elif kind == "out":
        s = _blocks(w["out"][a[0]][a[2] * D:(a[2] + 1) * D, a[1] * SLAB:(a[1] + 1) * SLAB])
    elif kind == "pl":
        s = _blocks(w["pl"][a[0]])
    elif kind == "gate":
        s = _blocks(w["gate"][a[0]][:, a[1] * SLAB:(a[1] + 1) * SLAB])
    elif kind == "ada":
        s = _blocks(w["ada"][:, a[0] * SLAB:(a[0] + 1) * SLAB])
    elif kind == "feat":
        s = _blocks(w["feat"][:, a[0] * SLAB:(a[0] + 1) * SLAB])
    elif kind == "val":
        s = _blocks(w["val"][:, a[0] * SLAB:(a[0] + 1) * SLAB])
    elif kind == "out2":
        s = _blocks(w["out2"][:, a[0] * SLAB:(a[0] + 1) * SLAB])
    elif kind == "ff":
        s = _blocks(w["ff"][:, a[0] * SLAB:(a[0] + 1) * SLAB])
    else:
        s = _blocks(w["down"][a[1] * D:(a[1] + 1) * D, a[0] * SLAB:(a[0] + 1) * SLAB])
    s = s.reshape(P, -1)
    return np.pad(s, ((0, 0), (0, KC * SLAB - s.shape[1])))


def _width(name):
    if name[0] == "pl":
        return 2 * D
    if name[0] == "down" and name[2] == 2:
        return (FF - 2 * KC) * SLAB
    return KC * SLAB


def _columns(x):
    return x.reshape(-1, P).T


def _constants():
    i, j = np.arange(P)[:, None], np.arange(P)[None, :]
    parts = [i == j, i <= j, i // HD == j // HD]
    parts += [(i // (2 * s) == j // (2 * s)) & (i // s < j // s) for s in LEVELS]
    k = np.concatenate([np.arange(P), np.arange(T)])[None, :]
    q = i + np.concatenate([np.zeros(P), np.full(T, P)])[None, :]
    parts += [np.where(k <= q, 0.0, NEG), k - q]
    return np.concatenate([np.asarray(x, np.float32) for x in parts], axis=1)


def kernel(**inputs):
    import concourse.bacc as _bacc
    from concourse.bass_utils import run_bass_kernel_spmd as _run

    z = {n: np.asarray(a) for n, a in inputs.items()}
    _, slabs = plan(STAGE)
    w2 = z["w_in_2"][0]
    fx, mw = FOX * HD, ML * HD
    at = np.cumsum([0, fx, fx, fx, FOX, mw, mw, mw, ML, ML, mw, fx, fx, fx])
    fq, fk, fv, ff, mq, mk, mv, mi, mf, mo, bq, bk, bv = (w2[:, a:b] for a, b in zip(at[:-1], at[1:]))
    feat = np.concatenate([fq, fk, mq, mk, mo, bq, bk, ff, mi, mf], axis=1)
    feat = np.pad(feat, ((0, 0), (0, 5 * SLAB - feat.shape[1])))
    gu = z["w_gate_up_2"][0].reshape(D, 2, FF, P).transpose(0, 2, 1, 3).reshape(D, 2 * D_FF)
    w = {"even": z["w_in_even"][0], "odd": z["w_in_odd"][0], "out": [z["w_out_even"][0], z["w_out_odd"][0]],
         "pl": z["w_pl"], "gate": z["w_pl_gate"], "ada": z["w_ada_2"][0], "feat": feat,
         "val": np.concatenate([fv, mv, bv], axis=1), "out2": z["w_out_2"][0], "ff": gu, "down": z["w_down_2"][0]}
    x, p = z["x"][0], z["p"][:, 0]
    bada = z["b_ada_2"][0].reshape(6, D)
    lane = lambda a: np.broadcast_to(a.reshape(1, -1), (P, a.size))
    twice = lambda a: np.concatenate([a, a]).reshape(P, 1)
    taps = lambda a: a.reshape(a.shape[0], -1, P).transpose(2, 1, 0).reshape(P, -1)
    vec = {"conv_b": taps(z["conv_b_w"][0]), "conv_a": taps(z["conv_a_w"][0]), "gdn_g": _columns(z["gdn_norm_g"][0]),
           "hgrn_g": _columns(z["hgrn_norm_g"][0]), "lb": _columns(z["lower_bounds"].reshape(-1)),
           "n1": _columns(z["norm1_g_2"][0]), "n2": _columns(z["norm2_g_2"][0]), "mlw": taps(z["ml_conv_w_2"][0]),
           "mlb": _columns(z["ml_conv_b_2"][0]), "mlg": _columns(z["ml_h_g_2"][0]),
           "bada": np.concatenate([_columns(bada[i]) for i in (0, 1, 3, 4)], axis=1), "c": _columns(z["c_2"][0]),
           "foxq": twice(z["fox_q_g_2"][0]), "foxk": twice(z["fox_k_g_2"][0]), "mobaq": twice(z["moba_q_g_2"][0]),
           "mobak": twice(z["moba_k_g_2"][0]), "a_log": lane(z["a_log"]), "dt": lane(z["dt_bias"]),
           "gate_bias": lane(np.concatenate([z["fox_f_bias_2"][0], z["ml_i_bias_2"][0], z["ml_f_bias_2"][0]]))}
    arrays = {
        "wst": np.stack([_slab(s, w) for s in slabs]),
        "x": x.reshape(NT, P, D).transpose(1, 0, 2),
        "xt": _blocks(x.T),
        "pt": p.transpose(0, 2, 1).reshape(2, 2, P, T).transpose(2, 0, 1, 3),
        "wba": _blocks(z["w_in_even"][0][:, 8192:8208]),
        "cst": _constants(),
        "vec": np.concatenate([vec[n] for n, _ in _SIZES], axis=1),
        "lnrow": np.stack([np.stack([z["ln_g"][0], z["ln_b"][0]]), np.stack([z["ln_g"][1], z["ln_b"][1]]),
                           np.stack([bada[2], bada[5]])]),
    }
    nc = _bacc.Bacc("TRN2", target_bir_lowering=False, num_devices=1)
    arrays = {n: np.ascontiguousarray(a) for n, a in arrays.items()}
    args = [nc.dram_tensor(n, a.shape, F32, kind="ExternalInput").ap() for n, a in arrays.items()]
    out = nc.dram_tensor("out", (P, NT, D), F32, kind="ExternalOutput").ap()
    build(nc, *args, out)
    got = _run(nc, [arrays], core_ids=[0]).results[0]["out"]
    return np.asarray(got).transpose(1, 0, 2).reshape(1, T, D)
```

```python
import math
from contextlib import ExitStack

import numpy as np

import concourse.bass as bass
from concourse import mybir

F32 = mybir.dt.float32
F32R = mybir.dt.float32r
U32 = mybir.dt.uint32
ALU = mybir.AluOpType
ACT = mybir.ActivationFunctionType
AX = mybir.AxisListType

P = 128
T = 256
NT = T // P
D = 1024
KC = D // P
SLAB = 512
HALF = 4 * SLAB
RAW_RING, SPLIT_RING, LEAD = 3, 3, 2
EARLY_LATE = 2
AFTER = 3
LEVELS = [1, 2, 4, 8, 16, 32, 64]
NL = len(LEVELS)
HG = 4
GDN_HEADS = 8
HGRN_GROUPS = 4
ALPHA = math.sqrt(2.0)
LN_EPS = 1e-5
L2_EPS = 1e-6
RMS_EPS = 1e-6
D_FF = 2816
FF = D_FF // P
FOX, ML, MOBA = 6, 4, 6
HD = 64
NEG = -1e30
SCALE64 = HD ** -0.5
SCALE128 = 128 ** -0.5

C_ID, C_TRIU, C_BD = 0, P, 2 * P
C_LVL = 3 * P
C_N = C_LVL + NL * P
NORM_AT = 10240

_SIZES = [("conv_b", 96), ("conv_a", 24), ("gdn_g", 1), ("hgrn_g", 1), ("lb", 32), ("n1", 8), ("n2", 8),
          ("mlw", 16), ("mlb", 4), ("mlg", 2), ("bada", 32), ("c", 8), ("foxq", 1), ("foxk", 1),
          ("mobaq", 1), ("mobak", 1), ("a_log", 8), ("dt", 8), ("gate_bias", 14)]
VC = {}
_at = 0
for _n, _s in _SIZES:
    VC[_n] = _at
    _at += _s
V_N = _at

QT = {"fq": 0, "fk": 3, "mq": 6, "mk": 8, "mo": 10, "bq": 12, "bk": 15}
N_QT = 18
A2_SC = N_QT * T + 10 * 3 * P + 2 * 10 * P + 2 * 2 * T
HEADS = FOX + ML + MOBA
TAIL_ADA = [[(0,), (1,)], [(8,), ()]]
WHOLE = ("ada", "pl")
MOD_ROW = [0, 0, 1, 1, None, None, 2, 2, 3, 3, None, None]
SQ_SLOTS = [(0, 1, 2), (0, 1, 3)]
NG = FOX + 2 * ML


class Step:

    def __init__(self, kind, args, engines, banks, slabs, readers, opens, read_in=None):
        self.kind, self.args, self.engines, self.banks = kind, args, engines, banks
        self.slabs, self.readers, self.opens = slabs, readers, opens
        self.name = (kind,) + args
        self.read_in = read_in or self.name
        self.late, self.until = 0, 0


def plan(stage):
    script, slabs = [], []
    ring, open_banks, rows = [0], [()], []

    def step(kind, *args, on, banks=(), slab=(), readers=None, opens=True, read_in=None):
        at = []
        for s in slab:
            if s not in slabs:
                slabs.append(s)
            at.append(slabs.index(s))
        if readers is None:
            readers = "".join(e for e in on if e in "SV")
        script.append(Step(kind, args, on, tuple(banks), at, readers, opens, read_in))

    def unit(kind, *args, on, slab=None, readers=None):
        step(kind, *args, on=on, banks=(4 + ring[0] % 4,), slab=(slab,) if slab else (), readers=readers)
        ring[0] += 1

    def unit_tokens(kind, *args, on, slab, parts, part, readers=None):
        if part == 0:
            ring[0] += ring[0] % 2
            open_banks[0] = (4 + ring[0] % 4, 5 + ring[0] % 4)
            ring[0] += 2
        last = part == parts - 1
        step(kind, *args, part, on=on if last else "T", banks=open_banks[0], slab=(slab + (part,),),
             readers=(readers if last else ""), opens=part == 0)

    def later(f, *args, **kw):
        return lambda: f(*args, **kw)

    def pair(name, g, on, readers=None):
        return [later(unit, name, g, p, on=on, slab=(name, g, p), readers=readers) for p in range(2)]

    def token_pair(name, *a, on, parts=2, readers=None):
        return [later(unit_tokens, name, *a, on=on, slab=(name,) + a, parts=parts, part=k, readers=readers)
                for k in range(parts)]

    def ada(i):
        def halves():
            unit("ada", i, 0, on="T", slab=("ada", i, 0), readers="")
            bank = script[-1].banks
            end_row()
            step("ada", i, 1, on="TS", banks=bank, slab=(("ada", i, 1),), opens=False)
            rows.append(i)
        return [halves]

    def end_row():
        if rows:
            unit("adat", rows.pop(), on="TV")

    def interleave(chain, fill, late=0):
        chain = [c if isinstance(c, tuple) else (c, 1.0) for c in chain]
        fill = list(fill)
        rate, owed = len(fill) / sum(w for _, w in chain), 0.5
        filled = []

        def put():
            n = len(script)
            fill.pop(0)()
            filled.extend(script[n:])

        def settle(until):
            for s in filled:
                if min(s.banks) >= 4:
                    s.late, s.until = late, until
            filled.clear()

        for c, w in chain:
            n = len(script)
            c()
            if script[n].kind in ("hf", "ho", "hr"):
                settle(n)
            owed += rate * w
            while owed >= 1 and fill:
                put()
                owed -= 1
        while fill:
            put()
        settle(len(script))

    def tail(layer):
        for n in range(2):
            for u in token_pair("out", layer, n, on="TV", parts=4, readers="V"):
                u()
        for n in range(2):
            step("pl", layer, n, on="TS", banks=(2 * n, 2 * n + 1), slab=[("pl", layer)])
        step("lna", layer, on="VS")
        step("lnb", layer, on="V")
        for i in TAIL_ADA[layer][0]:
            ada(i)[0]()
        for k in range(2):
            step("xt", 2 * layer, k, on="TSV", banks=(2 * k, 2 * k + 1))
        for n in range(2):
            for u in token_pair("gate", layer, n, on="TSV", readers="S"):
                u()
        for i in TAIL_ADA[layer][1]:
            ada(i)[0]()
        if layer == 0:
            for k in range(2):
                step("xt", 1, k, on="TSV", banks=(2 * k, 2 * k + 1))

    step("setup", on="SGV")
    step("xs", on="SV")

    def conv(name, g):
        return pair(name, g, on="TVS", readers="V")

    def gdn(g):
        out = [later(step, "gt", g, on="G"),
               later(step, "gc", g, on="TVS", banks=(0, 1, 2)),
               later(step, "gc2", g, on="V"),
               later(step, "norm", "q", g, on="TSV", banks=(2, 3), readers="V"),
               later(step, "vtr", g, on="TV", banks=(0, 1)),
               later(step, "gk", g, on="TV", banks=(2,)),
               later(step, "gkk", g, on="TV", banks=(0, 1, 2, 3))]
        for i in range(NL):
            for c in range(NT):
                out.append((later(step, "gp", g, i, c, on="TV", banks=(c,)), 0.5 * c))
            for c in range(NT):
                out.append((later(step, "gu", g, i, c, on="TV",
                                  banks={0: (c,), NL - 1: (2 + c,)}.get(i, (c, 2 + c))), 1.0 * c))
        out += [later(step, "gv", g, 0, on="TS", banks=(0,)),
                later(step, "gs", g, on="TS", banks=(1,)),
                later(step, "gks", g, on="TV", banks=(2,)),
                later(step, "gv", g, 1, on="TS", banks=(3,)),
                later(step, "go", g, on="TS", banks=(0, 1)),
                later(step, "gr", g, on="TSV", banks=(2, 3), readers="V")]
        return out

    def norm_k(g):
        return later(step, "norm", "k", g, on="TSV", banks=(0, 1), readers="V")

    first = len(script)
    for u in conv("k", 0) + conv("v", 0):
        u()
    step("ba", on="TV", banks=(0,))
    norm_k(0)()
    step("ba1", on="SV")
    conv("q", 0)[0]()
    step("ba2", on="SV")
    conv("q", 0)[1]()
    for s in script[first:]:
        if s.kind in ("k", "q", "v"):
            s.late, s.until = EARLY_LATE, len(script)
    a = []
    for hf in range(2):
        for p in range(2):
            a += [later(unit, name, hf, p, on=on, slab=(name, hf, p))
                  for name, on in (("ah", "TS"), ("ac", "TV"), ("az", "TS"), ("ab", "TV"))]
    interleave(late=3, chain=gdn(0), fill=pair("zb", 0, "TS") + conv("k", 1) + conv("v", 1) + [norm_k(1)] + conv("q", 1) + a[:6])
    interleave(late=3, chain=gdn(1), fill=pair("zb", 1, "TS") + a[6:])
    step("wg", on="V")
    step("c1", on="SV")
    step("xl", on="S")
    tail(0)
    if stage == 0:
        return script, slabs

    def hgrn(g):
        out = []
        for i in range(NL):
            out.append((later(step, "hm", g, i, on="T", banks=(0, 1) if i % 2 else (2, 3), readers="V",
                              read_in=("hp", g, i)), 1.0))
            if i:
                out.append((later(step, "hp", g, i - 1, on="V"), 0.0))
            if i + 2 <= NL:
                out.append((later(step, "hx", g, i + 2, on="VS"), 0.0))
            out.append((later(step, "hy", g, i + 1, on="VG"), 0.0))
        more = g + 1 < HGRN_GROUPS
        out += [(later(step, "hp", g, NL - 1, on="V"), 0.0)]
        if more:
            out += [(later(step, "hf", g + 1, on="SV"), 0.0),
                    (later(step, "hx", g + 1, 0, on="VS"), 0.0)]
        out += [(later(step, "hc", g, on="TS", banks=(2,)), 0.7),
                (later(step, "ho", g, on="TS", banks=(0, 1)), 1.0)]
        if more:
            out += start(g + 1)[2:]
        out += [(later(step, "hr", g, on="TSV", banks=(2, 3), readers="V"), 1.0)]
        return out

    def start(g):
        return [(later(step, "hf", g, on="SV"), 1.0),
                (later(step, "hx", g, 0, on="VS"), 0.0),
                (later(step, "hd", g, on="TV", banks=(0, 1)), 1.0),
                (later(step, "hx", g, 1, on="VS"), 0.0),
                (later(step, "hy", g, 0, on="VG"), 0.0)]

    def gates(g):
        return pair("f", g, "TSV", readers="S") if g < HGRN_GROUPS else []

    def queries(g):
        return pair("q1", g, "TS") if g < HGRN_GROUPS else []

    def values(g):
        return token_pair("i", g, on="TS", readers="S")

    step("lb", on="VS")
    step("lb2", on="V")
    for u in gates(0) + queries(0):
        u()
    interleave(start(0), values(0))
    for g in range(HGRN_GROUPS):
        last = g == HGRN_GROUPS - 1
        interleave(late=7, chain=hgrn(g), fill=gates(g + 1) + pair("z1", g, "TS") + queries(g + 1)
                   + (sum([ada(i) for i in (2, 3, 6, 7)], []) if last else values(g + 1)))
    end_row()
    step("mod", 0, on="V")
    tail(1)
    if stage == 1:
        return script, slabs

    def feat(j):
        if j in (3, 4):
            unit("feat", j, on="TVS", slab=("feat", j), readers="V")
        else:
            unit("feat", j, on="TS", slab=("feat", j))

    def root(i, b):
        step("qn", i, b, on="TSV", banks=(b,), readers="V")

    step("rms", 0, on="S")
    step("rmsb", 0, on="V")
    ada(9)[0]()
    for k in range(2):
        step("xt", 4, k, on="TSV", banks=(2 * k, 2 * k + 1))
    ada(4)[0]()
    for c in range(NT):
        unit("gates", c, on="TV")
    feat(8)
    step("ga", on="VS")
    feat(0)
    step("gb", on="VS")
    root(1, 2)
    feat(1)
    step("gd", on="V")
    root(0, 0)
    step("gsp", on="GV")
    feat(2)
    root(0, 1)
    step("gcol", on="TV", banks=(3,))
    feat(3)
    root(0, 2)
    feat(4)
    step("grow", 0, on="TV", banks=(0, 1, 2))
    feat(5)
    step("grow", 1, on="TV", banks=(0, 1))
    feat(6)
    step("gm", on="VS")
    feat(7)
    root(1, 0)
    values2 = sum([token_pair("val", n, on="TS", readers="S") for n in range(2)], [])
    values2[0]()
    root(1, 1)
    for u in values2[1:]:
        u()
    step("mb", on="V")
    ada(5)[0]()
    for n in range(HEADS + 2):
        if 1 <= n <= HEADS:
            step("ratio", n - 1, on="V")
        if n < HEADS:
            step("score", n, on="TV" if FOX <= n < FOX + ML else "TVS", banks=(n % 2,), readers="V")
        if 1 <= n <= HEADS:
            step("turn", n - 1, on="TS", banks=(2,))
        if n >= 2:
            if n % 2 == 0:
                step("pv", n - 2, on="T", banks=(3,))
            else:
                step("pv", n - 2, on="TS" if FOX < n - 2 < FOX + ML else "TSV", banks=(3,), opens=False)
        if n == 14:
            step("mln", on="TSV", banks=(0,), readers="V")
    end_row()
    for n in range(2):
        for u in token_pair("out2", n, on="TV", readers="V"):
            u()
    end_row()
    step("mod", 1, on="V")
    step("rms", 1, on="S")
    step("rmsb", 1, on="V")
    ada(10)[0]()
    for k in range(2):
        step("xt", 5, k, on="TSV", banks=(2 * k, 2 * k + 1))
    ada(11)[0]()
    end_row()
    for j in range(FF):
        unit("ff", j, on="TSV", slab=("ff", j))
    for n in range(2):
        for u in token_pair("down", n, on="TV", parts=6, readers="V"):
            u()
    return script, slabs


def with_splits(script, slabs):
    use, last_use = [None] * len(slabs), [None] * len(slabs)
    for n, s in enumerate(script):
        for i in s.slabs:
            last_use[i] = n
            if use[i] is None:
                use[i] = n
    halved = [i for i, name in enumerate(slabs) if name[0] not in WHOLE]
    splits = []
    for k, i in enumerate(halved):
        before = 0 if k < LEAD else use[halved[k - LEAD]]
        before = max([before] + [min(last_use[j] + AFTER, use[i]) for j in range(i - RAW_RING + 1) if j not in halved])
        splits.append((max(before, 1 + (k > 0)) - 0.5, Step("split", (k, i), "SV", (), [], "", True)))
    at = list(enumerate(script))
    by_place = lambda steps: [s for _, s in sorted(steps, key=lambda a: a[0])]
    behind = [(min(n + s.late, max(n, s.until - 0.75)), s) for n, s in at]
    order = {"T": script, "G": script, "S": by_place(splits + behind), "V": by_place(splits + behind)}
    order = {e: [s for s in steps if e in s.engines] for e, steps in order.items()}
    return by_place(splits + at), order, {i: k for k, i in enumerate(halved)}


STAGE = 2


def build(nc, wst, x_in, xt_in, pt_in, wba, wga, cst_in, msk_in, vec_in, lnrow, out):
    script, slabs = plan(STAGE)
    script, order, split_no = with_splits(script, slabs)
    where = {s.name: n for n, s in enumerate(script)}
    assert len(where) == len(script)
    counts = {e: {s.name: n + 1 for n, s in enumerate(steps)} for e, steps in order.items()}
    last_use = {}
    for n, s in enumerate(script):
        for b in s.slabs:
            last_use[b] = n

    ctx = ExitStack()
    with ctx:
        def sem(name):
            return ctx.enter_context(nc.semaphore(name))

        tensor_done, scalar_done, vector_done = sem("tensor_done"), sem("scalar_done"), sem("vector_done")
        gpsimd_done = sem("gpsimd_done")
        done = {"T": tensor_done, "S": scalar_done, "V": vector_done, "G": gpsimd_done}
        vector_link, scalar_link, gpsimd_link = sem("vector_link"), sem("scalar_link"), sem("gpsimd_link")
        slab_loaded = [sem(f"slab_loaded{i}") for i in range(RAW_RING)]
        x_loaded, small_loaded, cst_loaded = sem("x_loaded"), sem("small_loaded"), sem("cst_loaded")
        vec_loaded = sem("vec_loaded")
        ln_loaded, wba_loaded, mask_loaded = sem("ln_loaded"), sem("wba_loaded"), sem("mask_loaded")
        out_stored = sem("out_stored")

        def count(engine, name):
            assert engine in script[where[name]].engines, name
            return counts[engine][name]

        def tensor_at(*name):
            return count("T", name)

        def scalar_at(*name):
            return count("S", name)

        def vector_at(*name):
            return count("V", name)

        def gpsimd_at(*name):
            return count("G", name)

        at = [(nc.sbuf_base + 31) // 32 * 32]
        end = nc.sbuf_usable_end

        def place(name, offset, shape, dtype=F32):
            size = 4 * int(np.prod(shape[1:]))
            assert offset + size <= end, (name, offset + size - end)
            return nc.alloc_sbuf_tensor_at(name, shape, dtype, offset=offset)

        def sb(name, shape, dtype=F32):
            t = place(name, at[0], shape, dtype)
            at[0] += (4 * int(np.prod(shape[1:])) + 31) // 32 * 32
            return t

        RAW = sb("RAW", [P, RAW_RING, HALF])
        WH, WL = sb("WH", [P, SPLIT_RING, HALF], F32R), sb("WL", [P, SPLIT_RING, HALF], F32R)
        x_at = at[0]
        X = sb("X", [P, NT, D])
        XTH, XTL = sb("XTH", [P, KC, T], F32R), sb("XTL", [P, KC, T], F32R)
        y_at = at[0]
        YH = sb("YH", [P, 16, T], F32R)
        yl_at = at[0]
        YL = sb("YL", [P, 16, T], F32R)
        PT = sb("PT", [P, 2, 2, T])
        CST = sb("CST", [P, C_N])
        VEC = sb("VEC", [P, V_N])
        ONES = sb("ONES", [P, P])
        EPS = sb("EPS", [P, 4])
        ln_at = at[0]
        LNW = sb("LNW", [P, 2, D])
        WBA = sb("WBA", [P, KC, 16])
        WGA = sb("WGA", [P, KC * NG])
        WGH, WGL = sb("WGH", [P, KC, NG], F32R), sb("WGL", [P, KC, NG], F32R)
        SC8 = sb("SC8", [P, KC])
        MROW = sb("MROW", [1, SLAB])
        MODT = sb("MODT", [P, 4, KC])
        MODG = sb("MODG", [P, 2, KC])
        STAT = sb("STAT", [P, NT, 2, 6])
        AGG = sb("AGG", [P, NT, 2])
        RSTD = sb("RSTD", [P, NT])
        SUMSQ = sb("SUMSQ", [P, NT])
        arena_at = at[0]
        ident = CST[:, C_ID:C_ID + P]
        triu = CST[:, C_TRIU:C_TRIU + P]
        bd64 = CST[:, C_BD:C_BD + P]
        lvl = [CST[:, C_LVL + i * P:C_LVL + (i + 1) * P] for i in range(NL)]

        def flat_of(ap):
            return ap.rearrange("p a b -> p (a b)")

        class Arena:

            def __init__(self, name, start=None, words=None):
                start = arena_at if start is None else start
                self.words = (end - start) // 4 // 8 * 8 if words is None else words
                self.buffer = place(name, start, [P, self.words])
                self.at = 0

            def take(self, *shape):
                n = int(np.prod(shape))
                assert self.at + n <= self.words, (self.at, n, self.words)
                ap = self.buffer[:, self.at:self.at + n]
                self.at += n
                return ap.rearrange("p (a b) -> p a b", a=shape[0]) if len(shape) == 2 else (
                    ap.rearrange("p (a b c) -> p a b c", a=shape[0], b=shape[1]) if len(shape) == 3 else ap)

        PS = ctx.enter_context(nc.psum_tensor("PS", [P, 8, SLAB], F32))

        A0 = Arena("layer0")
        KT, QT0 = A0.take(2 * HG, T), A0.take(2 * HG, T)
        VT = A0.take(HG, T)
        ZB = A0.take(HG, T)
        CV = A0.take(2, 2 * T)
        SQ = A0.take(2, 2 * T)
        AH, AC, AZ = A0.take(2 * T), A0.take(2 * T), A0.take(2 * T)
        ER = A0.take(4, P)
        assert A0.at == NORM_AT
        DLU = A0.take(16, P)
        DL, DU = DLU[:, 0:8, :], DLU[:, 8:16, :]
        XT0 = flat_of(DLU).rearrange("p (k t) -> p k t", k=KC)
        PM = A0.take(8, P)
        KD, ST = A0.take(4, P), A0.take(4, P)
        TA, TB, TC, TD = A0.take(16), A0.take(16), A0.take(16), A0.take(16)
        BE, GG = A0.take(2, 8), A0.take(2, 8)
        GCOL, EGC, BEG = A0.take(8), A0.take(8), A0.take(8)
        KDF = A0.take(4)
        AX0 = Arena("layer0_x", x_at, 2 * D)
        U, XI = AX0.take(8, P), AX0.take(8, P)
        AL0 = Arena("layer0_ln", ln_at, 2 * D)
        BV, VN = AL0.take(8, P), AL0.take(8, P)
        OT = U.rearrange("p (h c) t -> p h (c t)", h=HG)
        SQO = PM.rearrange("p (h c) t -> p h (c t)", h=HG)
        RO = XI.rearrange("p (h c) t -> p h (c t)", h=HG)

        AN = Arena("norms")
        AN.take(NORM_AT)
        PLB = AN.take(NT, D)
        GT = AN.take(NT, SLAB)

        A1 = Arena("layer1")
        HK, HQ = A1.take(2 * HG, T), A1.take(2 * HG, T)
        HV = A1.take(2, NT, HG * P)
        HB, HZ = A1.take(HG, T), A1.take(HG, T)
        FS = A1.take(HG, T)
        HE, HX = A1.take(2 * HG, T), A1.take(2 * HG, T)
        LBV, OML, LT1, LT2 = A1.take(16), A1.take(16), A1.take(32), A1.take(16)
        AL1 = Arena("layer1_ln", ln_at, 2 * D)
        HA, HC = AL1.take(8, P), AL1.take(HG, P)
        HOT = A1.take(HG, T)
        HS = HX[:, HG:2 * HG, :]

        A2 = Arena("block2")
        Q2 = A2.take(N_QT, T)
        B2 = A2.take(HEADS, 3 * P)
        A2.take(2 * 10 * P - MOBA * 3 * P)
        SQ2 = A2.take(4, 2 * T)
        CV2 = A2.take(2, 2 * T)
        GA, GB, NLS, GCC = A2.take(NT, NG), A2.take(NT, NG), A2.take(NT, NG), A2.take(NT, NG)
        MX, SM, RI, EM = A2.take(HEADS, 2), A2.take(HEADS, 2), A2.take(HEADS, 2), A2.take(ML, 2)
        b2 = A2.buffer[:, N_QT * T:]
        XN = b2[:, 0:NT * D].rearrange("p (c d) -> p c d", c=NT)
        spread_at = (FOX + ML) * 3 * P
        GSP = [b2[:, spread_at + c * 10 * P:spread_at + (c + 1) * 10 * P].rearrange("p (h k) -> p h k", h=10)
               for c in range(NT)]
        sc = A2.buffer[:, A2_SC:A2_SC + 2 * 6 * P].rearrange("p (n b k) -> p n b k", n=2, b=2)
        SC, PTT = sc[:, 0], sc[:, 1]
        AY = Arena("values", y_at + 8 * T * 4, 8 * T)
        V2 = AY.take(NT, D)
        AM = Arena("masks", yl_at + 8 * T * 4, 8 * T)
        MSK = AM.take(2, 3 * P)
        YML = AM.take(2, T)
        mask3, dist3 = MSK[:, 0], MSK[:, 1]
        A3 = Arena("mlp", arena_at + 4 * 2048)
        SG, HT = A3.take(2, T), A3.take(2, T)
        eh_at = arena_at + 4 * 2048 + 4 * 4 * T
        EH = place("EH", eh_at, [P, FF - 16, T], F32R)
        EL = place("EL", eh_at + 4 * (FF - 16) * T, [P, FF - 16, T], F32R)
        AR = Arena("mlp_residual", arena_at, 2048)
        XR = AR.take(NT, D)

        def as_float(ap):
            return ap.bitcast(F32)

        def y_tile(j):
            return (YH[:, j, :], YL[:, j, :]) if j < 16 else (EH[:, j - 16, :], EL[:, j - 16, :])

        def v(name, i=0, n=1):
            return VEC[:, VC[name] + i:VC[name] + i + n]

        def bc(ap, n):
            return ap.unsqueeze(2).to_broadcast([ap.shape[0], ap.shape[1], n])

        def rep(ap, n):
            return ap.unsqueeze(1).to_broadcast([ap.shape[0], n, ap.shape[1]])

        def flat(ap):
            return ap.rearrange("p a b -> p (a b)")

        def tiles(ap, a, n):
            return flat(ap[:, a:a + n, :])

        def bank_of(*name):
            return script[where[name]].banks[0]

        def split_at(i):
            return count("V", ("split", split_no[i], i))

        def gate_of(j):
            return j if j < FOX else j + ML

        def head(h):
            fam, i = ("f", h) if h < FOX else ("m", h - FOX) if h < FOX + ML else ("b", h - FOX - ML)
            return QT[fam + "q"] + i // 2, QT[fam + "k"] + i // 2, (h % 2) * HD, h * HD, h // 2

        def rows(c):
            return slice(0, P) if c == 0 else slice(P, 3 * P)

        conv_units = [s.name for s in script if s.kind in ("k", "q", "v")]
        halved = sorted(split_no, key=split_no.get)
        block = ctx.enter_context(nc.Block())

        @block.sync
        def _(sp):
            def slab(i):
                if i >= RAW_RING:
                    before = i - RAW_RING
                    if before in split_no:
                        sp.wait_ge(vector_done, split_at(before))
                    else:
                        sp.wait_ge(tensor_done, counts["T"][script[last_use[before]].name])
                n = _width(slabs[i])
                sp.dma_start(RAW[:, i % RAW_RING, 0:n], wst[i, :, 0:n]).then_inc(slab_loaded[i % RAW_RING], 16)

            sp.dma_start(XT0, xt_in).then_inc(x_loaded, 16)
            for i in range(len(slabs)):
                slab(i)
                if i == 12:
                    sp.dma_start(PT[:], pt_in).then_inc(small_loaded, 16)
                    sp.dma_start(WGA[:], wga).then_inc(small_loaded, 16)
            if STAGE == 2:
                for n in range(2):
                    sp.wait_ge(vector_done, vector_at("down", n, 5))
                    sp.dma_start(out[:, :, n * SLAB:(n + 1) * SLAB], X[:, :, n * SLAB:(n + 1) * SLAB]).then_inc(out_stored, 16)
                sp.wait_ge(out_stored, 32)
            else:
                sp.wait_ge(vector_done, vector_at("gate", STAGE, 1, 1))
                sp.dma_start(out, X[:]).then_inc(out_stored, 16)
                sp.wait_ge(out_stored, 16)
                sp.wait_ge(ln_loaded, 16 + 32 * STAGE)

        @block.tensor
        def _(pe):
            def mm(o, lhsT, rhs, start=True, stop=True):
                return pe.matmul(o, lhsT, rhs, start=start, stop=stop)

            def claim(step):
                n = where[step.name]
                for b in step.banks if step.opens else ():
                    before = [s for s in script[:n] if b in s.banks]
                    if before:
                        for r in before[-1].readers or "":
                            pe.wait_ge(done[r], count(r, before[-1].read_in))

            def split_ready(i):
                pe.wait_ge(vector_done, split_at(i))

            def products(o, pairs):
                n = len(pairs)
                for j, ((ah, al), (bh, bl)) in enumerate(pairs):
                    mm(o, ah, bh, start=j == 0, stop=False)
                    mm(o, ah, bl, start=False, stop=False)
                    last = mm(o, al, bh, start=False, stop=j == n - 1)
                return last

            def wt(step, blocks):
                i = split_no[step.slabs[0]] % SPLIT_RING
                return (w[:, i, :].rearrange("p (k n) -> p k n", k=blocks) for w in (WH, WL))

            def features(step):
                split_ready(step.slabs[0])
                wh, wl = wt(step, KC)
                for a in range(2):
                    s = slice(a * P, (a + 1) * P)
                    last = products(PS[:, step.banks[0], a * T:(a + 1) * T],
                                    [((wh[:, k, s], wl[:, k, s]), (XTH[:, k, :], XTL[:, k, :])) for k in range(KC)])
                return last

            def tokens(step, part, operand, blocks):
                split_ready(step.slabs[0])
                wh, wl = wt(step, 4)
                for c in range(NT):
                    s = slice(c * P, (c + 1) * P)
                    for j in range(min(4, blocks - 4 * part)):
                        k = 4 * part + j
                        ah, al = operand(k)
                        o = PS[:, step.banks[c], :]
                        mm(o, ah[:, s], wh[:, j, :], start=k == 0, stop=False)
                        mm(o, ah[:, s], wl[:, j, :], start=False, stop=False)
                        last = mm(o, al[:, s], wh[:, j, :], start=False, stop=k == blocks - 1)
                return last

            def x_tile(k):
                return XTH[:, k, :], XTL[:, k, :]

            def t_ba(step):
                pe.wait_ge(x_loaded, 16)
                pe.wait_ge(wba_loaded, 16)
                for c in range(NT):
                    for k in range(KC):
                        last = mm(PS[:, 0, c * 16:(c + 1) * 16], XT0[:, k, c * P:(c + 1) * P], WBA[:, k, :],
                                  start=k == 0, stop=k == KC - 1)
                last.then_inc(tensor_done, 1)

            def unit2(step, g, p):
                pe.wait_ge(vector_done, vector_at("xs"))
                features(step).then_inc(tensor_done, 1)

            def t_gc(step, g):
                pe.wait_ge(vector_done, vector_at("ba2"))
                pe.wait_ge(gpsimd_done, gpsimd_at("gt", g))
                pe.wait_ge(cst_loaded, 16)
                gt = flat(PM)
                for i in range(2):
                    mm(PS[:, i, :], ONES[:], gt[:, i * SLAB:(i + 1) * SLAB])
                mm(PS[:, 2, 0:8], triu, GG[:, g, :]).then_inc(tensor_done, 1)

            def t_norm(step, kind, g):
                pe.wait_ge(scalar_done, scalar_at(kind, g, 1))
                for i in range(2):
                    last = mm(PS[:, step.banks[i], :], ONES[:], SQ[:, i, :])
                last.then_inc(tensor_done, 1)

            def t_vtr(step, g):
                pe.wait_ge(scalar_done, scalar_at("v", g, 1))
                for c in range(NT):
                    for h in range(HG):
                        last = pe.transpose(PS[:, c, h * P:(h + 1) * P], VT[:, h, c * P:(c + 1) * P], ident)
                last.then_inc(tensor_done, 1)

            def t_gk(step, g):
                pe.wait_ge(vector_done, vector_at("norm", "k", g))
                for h in range(HG):
                    last = pe.transpose(PS[:, 2, h * P:(h + 1) * P], KT[:, g * HG + h, 0:P], ident)
                last.then_inc(tensor_done, 1)

            def t_gkk(step, g):
                pe.wait_ge(vector_done, vector_at("norm", "q", g))
                for c in range(NT):
                    for h in range(HG):
                        kt = KT[:, g * HG + h, c * P:(c + 1) * P]
                        mm(PS[:, c, h * P:(h + 1) * P], kt, kt)
                        last = mm(PS[:, 2 + c, h * P:(h + 1) * P], kt, QT0[:, g * HG + h, c * P:(c + 1) * P])
                last.then_inc(tensor_done, 1)

            def t_gp(step, g, i, c):
                if i == 0:
                    pe.wait_ge(vector_done, vector_at("gkk", g))
                    for h in range(HG):
                        last = pe.transpose(PS[:, c, h * P:(h + 1) * P], DL[:, c * HG + h, :], ident)
                    last.then_inc(tensor_done, 1)
                    return
                pe.wait_ge(vector_done, vector_at("gu", g, i - 1, c))
                for h in range(HG):
                    last = mm(PS[:, c, h * P:(h + 1) * P], DL[:, c * HG + h, :], U[:, c * HG + h, :])
                last.then_inc(tensor_done, 1)

            def t_gu(step, g, i, c):
                pe.wait_ge(vector_done, vector_at("gp", g, i, c))
                if i == 0:
                    for h in range(HG):
                        last = pe.transpose(PS[:, c, h * P:(h + 1) * P], PM[:, c * HG + h, :], ident)
                    last.then_inc(tensor_done, 1)
                    return
                for h in range(HG):
                    m = c * HG + h
                    last = mm(PS[:, 2 + c, h * P:(h + 1) * P], XI[:, m, :], PM[:, m, :])
                if i < NL - 1:
                    for h in range(HG):
                        m = c * HG + h
                        last = mm(PS[:, c, h * P:(h + 1) * P], PM[:, m, :], XI[:, m, :])
                last.then_inc(tensor_done, 1)

            def t_gv(step, g, c):
                pe.wait_ge(vector_done, vector_at("gu", g, NL - 1, c))
                if c:
                    pe.wait_ge(vector_done, vector_at("gks", g))
                for h in range(HG):
                    m = c * HG + h
                    last = mm(PS[:, step.banks[0], h * P:(h + 1) * P], U[:, m, :], BV[:, m, :])
                last.then_inc(tensor_done, 1)

            def t_gs(step, g):
                pe.wait_ge(scalar_done, scalar_at("gv", g, 0))
                for h in range(HG):
                    last = mm(PS[:, 1, h * P:(h + 1) * P], KD[:, h, :], VN[:, h, :])
                last.then_inc(tensor_done, 1)

            def t_gks(step, g):
                pe.wait_ge(scalar_done, scalar_at("gs", g))
                for h in range(HG):
                    last = mm(PS[:, 2, h * P:(h + 1) * P], KT[:, g * HG + h, P:T], ST[:, h, :])
                last.then_inc(tensor_done, 1)

            def t_go(step, g):
                pe.wait_ge(scalar_done, scalar_at("gv", g, 1))
                for h in range(HG):
                    mm(PS[:, 0, h * P:(h + 1) * P], VN[:, h, :], DU[:, h, :])
                for h in range(HG):
                    mm(PS[:, 1, h * P:(h + 1) * P], VN[:, HG + h, :], DU[:, HG + h, :], stop=False)
                    last = mm(PS[:, 1, h * P:(h + 1) * P], ST[:, h, :], QT0[:, g * HG + h, P:T], start=False)
                last.then_inc(tensor_done, 1)

            def t_gr(step, g):
                pe.wait_ge(scalar_done, scalar_at("go", g))
                for i in range(2):
                    last = mm(PS[:, 2 + i, :], ONES[:], tiles(SQO, 2 * i, 2))
                last.then_inc(tensor_done, 1)

            def t_out(step, layer, n, part):
                if layer == 0:
                    pe.wait_ge(vector_done, vector_at("gr", 1))
                    pe.wait_ge(vector_done, vector_at("ab", 1, 1))
                else:
                    pe.wait_ge(vector_done, vector_at("hr", HGRN_GROUPS - 1))
                tokens(step, part, y_tile, 2 * KC).then_inc(tensor_done, 1)

            def t_pl(step, layer, n):
                i = step.slabs[0]
                pe.wait_ge(slab_loaded[i % RAW_RING], 16 * (i // RAW_RING + 1))
                pe.wait_ge(small_loaded, 32)
                w = RAW[:, i % RAW_RING, :].rearrange("p (k n) -> p k n", k=2)
                for c in range(NT):
                    for k in range(2):
                        last = mm(PS[:, step.banks[c], :], PT[:, layer, k, c * P:(c + 1) * P],
                                  w[:, k, n * SLAB:(n + 1) * SLAB], start=k == 0, stop=k == 1)
                last.then_inc(tensor_done, 1)

            def t_xt(step, i, half):
                src = X if i < 4 else XN
                if i in (0, 2):
                    pe.wait_ge(vector_done, vector_at("lnb", i // 2))
                elif i == 1:
                    pe.wait_ge(vector_done, vector_at("gate", 0, 1, 1))
                else:
                    pe.wait_ge(vector_done, vector_at("rmsb", i - 4))
                for j in range(4):
                    k = 4 * half + j
                    for c in range(NT):
                        o = (j % 2) * T + c * P
                        last = pe.transpose(PS[:, step.banks[j // 2], o:o + P], src[:, c, k * P:(k + 1) * P], ident)
                last.then_inc(tensor_done, 1)

            def xt_ready(i):
                pe.wait_ge(vector_done, vector_at("xt", i, 1))

            def t_gate(step, layer, n, part):
                xt_ready(2 * layer)
                tokens(step, part, x_tile, KC).then_inc(tensor_done, 1)

            def unit1(step, g, p):
                xt_ready(1)
                features(step).then_inc(tensor_done, 1)

            def t_i(step, g, part):
                xt_ready(1)
                tokens(step, part, x_tile, KC).then_inc(tensor_done, 1)

            def t_ada(step, i, part):
                pe.wait_ge(vector_done, vector_at("c1"))
                n = step.slabs[0]
                pe.wait_ge(slab_loaded[n % RAW_RING], 16 * (n // RAW_RING + 1))
                w = RAW[:, n % RAW_RING, :].rearrange("p (k n) -> p k n", k=4)
                for j in range(4):
                    k = 4 * part + j
                    last = mm(PS[0:1, step.banks[0], :], SC8[:, k:k + 1], w[:, j, :], start=k == 0, stop=k == KC - 1)
                last.then_inc(tensor_done, 1)

            def t_adat(step, i):
                pe.wait_ge(scalar_done, scalar_at("ada", i, 1))
                if MOD_ROW[i] is None:
                    mm(PS[:, step.banks[0], :], ONES[0:1, :], MROW[0:1, :]).then_inc(tensor_done, 1)
                    return
                for j in range(4):
                    last = mm(PS[:, step.banks[0], j:j + 1], MROW[0:1, j * P:(j + 1) * P], ONES[0:1, 0:1])
                last.then_inc(tensor_done, 1)

            def t_hd(step, g):
                pe.wait_ge(scalar_done, scalar_at("q1", g, 1))
                pe.wait_ge(vector_done, vector_at("hf", g))
                for c in range(NT):
                    for h in range(HG):
                        s = slice(c * P, (c + 1) * P)
                        last = mm(PS[:, c, h * P:(h + 1) * P], HK[:, g % 2 * HG + h, s], HQ[:, g % 2 * HG + h, s])
                last.then_inc(tensor_done, 1)

            def t_hm(step, g, i):
                pe.wait_ge(vector_done, vector_at("hy", g, i))
                pe.wait_ge(gpsimd_done, gpsimd_at("hy", g, i))
                for c in range(NT):
                    for h in range(HG):
                        x = HX[:, i % 2 * HG + h, c * P:(c + 1) * P]
                        last = mm(PS[:, step.banks[c], h * P:(h + 1) * P], x, x)
                last.then_inc(tensor_done, 1)

            def t_hc(step, g):
                pe.wait_ge(vector_done, vector_at("hy", g, NL))
                pe.wait_ge(gpsimd_done, gpsimd_at("hy", g, NL))
                for h in range(HG):
                    x = HX[:, NL % 2 * HG + h, :]
                    last = mm(PS[:, 2, h * P:(h + 1) * P], x[:, 0:P], x[:, P:T])
                last.then_inc(tensor_done, 1)

            def t_ho(step, g):
                pe.wait_ge(vector_done, vector_at("hp", g, NL - 1))
                pe.wait_ge(scalar_done, scalar_at("hc", g))
                pe.wait_ge(scalar_done, scalar_at("i", g, 1))
                vv = HV[:, g % 2]
                for h in range(HG):
                    s = slice(h * P, (h + 1) * P)
                    mm(PS[:, 0, s], vv[:, 0, s], HA[:, h, :])
                    mm(PS[:, 1, s], vv[:, 0, s], HC[:, h, :], stop=False)
                    last = mm(PS[:, 1, s], vv[:, 1, s], HA[:, HG + h, :], start=False)
                last.then_inc(tensor_done, 1)

            def t_hr(step, g):
                pe.wait_ge(scalar_done, scalar_at("ho", g))
                for i in range(2):
                    last = mm(PS[:, 2 + i, :], ONES[:], tiles(HS, 2 * i, 2))
                last.then_inc(tensor_done, 1)

            def t_gates(step, c):
                xt_ready(4)
                s = slice(c * P, (c + 1) * P)
                products(PS[:, step.banks[0], 0:NG],
                                [((XTH[:, k, s], XTL[:, k, s]), (WGH[:, k, :], WGL[:, k, :])) for k in range(KC)]).then_inc(tensor_done, 1)

            def t_feat(step, j):
                xt_ready(4)
                features(step).then_inc(tensor_done, 1)

            def t_val(step, n, part):
                xt_ready(4)
                tokens(step, part, x_tile, KC).then_inc(tensor_done, 1)

            def t_qn(step, i, b):
                pe.wait_ge(scalar_done, scalar_at("feat", 6 * i + b))
                mm(PS[:, b, :], bd64, SQ2[:, SQ_SLOTS[i][b], :]).then_inc(tensor_done, 1)

            def t_gcol(step):
                pe.wait_ge(vector_done, vector_at("gd"))
                mm(PS[:, 3, 0:NG], triu, NLS[:, 0, :])
                mm(PS[:, 3, NG:2 * NG], ONES[:], NLS[:, 0, :], stop=False)
                mm(PS[:, 3, NG:2 * NG], triu, NLS[:, 1, :], start=False).then_inc(tensor_done, 1)

            def t_grow(step, part):
                pe.wait_ge(vector_done, vector_at("gsp"))
                pe.wait_ge(gpsimd_done, gpsimd_at("gsp"))
                pairs = range(3) if part == 0 else range(3, 5)
                for b, pr in enumerate(pairs):
                    for a in range(2):
                        j = 2 * pr + a
                        o = a * T
                        mm(PS[:, b, o:o + P], ONES[:], GSP[0][:, j, :])
                        tot = NLS[:, 0, gate_of(j):gate_of(j) + 1].to_broadcast([P, P])
                        mm(PS[:, b, o + P:o + T], ONES[:], tot, stop=False)
                        last = mm(PS[:, b, o + P:o + T], ONES[:], GSP[1][:, j, :], start=False)
                last.then_inc(tensor_done, 1)

            def t_score(step, h):
                q, k, r, _, _ = head(h)
                pe.wait_ge(vector_done, vector_at("qn", 1, 1))
                pe.wait_ge(scalar_done, scalar_at("feat", 5))
                o = PS[:, step.banks[0], :]
                mm(o[:, 0:P], Q2[r:r + HD, q, 0:P], Q2[r:r + HD, k, 0:P])
                mm(o[:, P:3 * P], Q2[r:r + HD, q, P:T], Q2[r:r + HD, k, :]).then_inc(tensor_done, 1)

            def t_turn(step, h):
                pe.wait_ge(vector_done, vector_at("ratio", h))
                for j in range(3):
                    last = pe.transpose(PS[:, 2, j * P:(j + 1) * P], SC[:, h % 2, j * P:(j + 1) * P], ident)
                last.then_inc(tensor_done, 1)

            def t_pv(step, h):
                pe.wait_ge(scalar_done, scalar_at("turn", h))
                if h == 0:
                    pe.wait_ge(scalar_done, scalar_at("val", 1, 1))
                _, _, r, vcol, _ = head(h)
                o = PS[r:r + HD, 3, :]
                pt = PTT[:, h % 2, :]
                mm(o[:, 0:P], V2[:, 0, vcol:vcol + HD], pt[:, 0:P])
                mm(o[:, P:T], V2[:, 0, vcol:vcol + HD], pt[:, P:2 * P], stop=False)
                mm(o[:, P:T], V2[:, 1, vcol:vcol + HD], pt[:, 2 * P:3 * P], start=False).then_inc(tensor_done, 1)

            def t_mln(step):
                pe.wait_ge(scalar_done, scalar_at("pv", FOX + ML - 1))
                mm(PS[:, 0, :], bd64, SQ2[:, 0, :]).then_inc(tensor_done, 1)

            def t_out2(step, n, part):
                pe.wait_ge(vector_done, vector_at("mln"))
                pe.wait_ge(vector_done, vector_at("pv", HEADS - 1))
                tokens(step, part, y_tile, KC).then_inc(tensor_done, 1)

            def t_ff(step, j):
                xt_ready(5)
                features(step).then_inc(tensor_done, 1)

            def t_down(step, n, part):
                pe.wait_ge(vector_done, vector_at("ff", FF - 1))
                tokens(step, part, y_tile, FF).then_inc(tensor_done, 1)

            parts = {"ba": t_ba, "k": unit2, "q": unit2, "v": unit2, "zb": unit2, "ah": unit2, "ac": unit2,
                     "az": unit2, "ab": unit2, "gc": t_gc, "norm": t_norm, "vtr": t_vtr, "gk": t_gk, "gkk": t_gkk,
                     "gp": t_gp, "gu": t_gu, "gv": t_gv, "gs": t_gs, "gks": t_gks, "go": t_go, "gr": t_gr,
                     "out": t_out, "pl": t_pl, "xt": t_xt, "gate": t_gate, "f": unit1, "q1": unit1, "z1": unit1,
                     "i": t_i, "ada": t_ada, "adat": t_adat, "hd": t_hd, "hm": t_hm, "hc": t_hc, "ho": t_ho,
                     "hr": t_hr, "gates": t_gates, "feat": t_feat, "val": t_val, "qn": t_qn, "gcol": t_gcol,
                     "grow": t_grow, "score": t_score, "turn": t_turn, "pv": t_pv, "mln": t_mln, "out2": t_out2,
                     "ff": t_ff, "down": t_down}
            pe.wait_ge(gpsimd_done, gpsimd_at("setup"))
            for step in order["T"]:
                claim(step)
                parts[step.kind](step, *step.args)

        @block.scalar
        def _(act):
            links = [0]

            def link(ins):
                links[0] += 1
                ins.then_inc(scalar_link, 1)
                act.wait_ge(scalar_link, links[0])

            fn = act.activation

            def s_setup():
                act.dma_start(VEC[:], vec_in).then_inc(vec_loaded, 16)
                act.dma_start(WBA[:], wba).then_inc(wba_loaded, 16)
                act.dma_start(CST[:], cst_in).then_inc(cst_loaded, 16)
                act.wait_ge(gpsimd_done, gpsimd_at("setup"))
                fn(EPS[:, 2:3], EPS[:, 0:1], ACT.Silu).then_inc(scalar_done, 1)

            def s_split(k, i):
                act.wait_ge(slab_loaded[i % RAW_RING], 16 * (i // RAW_RING + 1))
                if k >= SPLIT_RING:
                    act.wait_ge(tensor_done, counts["T"][script[last_use[halved[k - SPLIT_RING]]].name])
                n = _width(slabs[i])
                fn(WH[:, k % SPLIT_RING, 0:n], RAW[:, i % RAW_RING, 0:n], ACT.Copy).then_inc(scalar_done, 1)

            def s_xs():
                act.wait_ge(x_loaded, 16)
                fn(flat(XTH[:]), flat(XT0), ACT.Copy).then_inc(scalar_done, 1)

            def rsqrt(dst, src, scale, eps):
                act.preload_act_table_set("natural_log_exp_and_others")
                link(fn(dst, src, ACT.Ln, scale=scale, bias=EPS[:, eps:eps + 1]))
                return fn(dst, dst, ACT.Exp, scale=-0.5)

            def s_c1():
                act.wait_ge(vec_loaded, 16)
                fn(SC8[:], v("c", 0, 8), ACT.Sigmoid).then_inc(scalar_done, 1)

            def s_ba1():
                act.wait_ge(vector_done, vector_at("ba"))
                fn(flat(BE), TA, ACT.Exp, scale=-1.0)
                fn(TB, TB, ACT.Exp)
                fn(TC[:, 0:8], v("a_log", 0, 8), ACT.Exp).then_inc(scalar_done, 1)

            def s_ba2():
                act.wait_ge(vector_done, vector_at("ba1"))
                fn(TB, TB, ACT.Ln).then_inc(scalar_done, 1)

            def s_conv(kind):
                def part(g, p):
                    act.wait_ge(vector_done, vector_at(kind, g, p))
                    i = conv_units.index((kind, g, p))
                    if kind == "v":
                        if g:
                            act.wait_ge(tensor_done, tensor_at("vtr", 0))
                        fn(tiles(VT, 2 * p, 2), CV[:, i % 2, :], ACT.Silu).then_inc(scalar_done, 1)
                        return
                    if kind == "q":
                        act.wait_ge(vector_done, vector_at("norm", "k", g))
                    elif g:
                        act.wait_ge(vector_done, vector_at("norm", "q", 0))
                    dst = tiles(KT if kind == "k" else QT0, g * HG + 2 * p, 2)
                    link(fn(dst, CV[:, i % 2, :], ACT.Silu))
                    fn(SQ[:, p, :], dst, ACT.Square).then_inc(scalar_done, 1)
                return part

            def s_gc(g):
                act.wait_ge(vector_done, vector_at("gc", g))
                fn(flat(ER), PS[:, 1, :], ACT.Exp)
                fn(EGC, GCOL, ACT.Exp)
                fn(KDF, KDF, ACT.Exp)
                fn(flat(DU), flat(DU), ACT.Exp)
                fn(flat(DL), flat(DL), ACT.Exp, scale=-1.0).then_inc(scalar_done, 1)

            def s_norm(kind, g):
                act.wait_ge(tensor_done, tensor_at("norm", kind, g))
                b = bank_of("norm", kind, g)
                rsqrt(flat(SQ), PS[:, b:b + 2, :].rearrange("p b n -> p (b n)"), 1.0, 1).then_inc(scalar_done, 1)

            def s_gv(g, c):
                act.wait_ge(tensor_done, tensor_at("gv", g, c))
                fn(tiles(VN, c * HG, HG), PS[:, bank_of("gv", g, c), :], ACT.Copy).then_inc(scalar_done, 1)

            def s_gs(g):
                act.wait_ge(tensor_done, tensor_at("gs", g))
                fn(flat(ST), PS[:, 1, :], ACT.Copy).then_inc(scalar_done, 1)

            def outputs(dst, squares):
                for c in range(NT):
                    src = PS[:, c, :].rearrange("p (h t) -> p h t", h=HG)
                    fn(dst[:, :, c * P:(c + 1) * P], src, ACT.Copy)
                    last = fn(squares[:, :, c * P:(c + 1) * P], src, ACT.Square)
                return last

            def s_go(g):
                act.wait_ge(tensor_done, tensor_at("go", g))
                outputs(OT, SQO).then_inc(scalar_done, 1)

            def root(dst, banks):
                return rsqrt(flat(dst), banks.rearrange("p b n -> p (b n)"), 1.0 / P, 0)

            def s_gr(g):
                act.wait_ge(tensor_done, tensor_at("gr", g))
                root(RO, PS[:, 2:4, :]).then_inc(scalar_done, 1)

            def s_zb(g, p):
                act.wait_ge(tensor_done, tensor_at("zb", g, p))
                if g:
                    act.wait_ge(vector_done, vector_at("gr", 0))
                fn(tiles(ZB, 2 * p, 2), PS[:, bank_of("zb", g, p), :], ACT.Silu).then_inc(scalar_done, 1)

            def s_ah(hf, p):
                act.wait_ge(tensor_done, tensor_at("ah", hf, p))
                if hf or p:
                    act.wait_ge(vector_done, vector_at("ac", *((hf, 0) if p else (0, 1))))
                fn(AH, PS[:, bank_of("ah", hf, p), :], ACT.Copy).then_inc(scalar_done, 1)

            def s_az(hf, p):
                act.wait_ge(tensor_done, tensor_at("az", hf, p))
                if hf or p:
                    act.wait_ge(vector_done, vector_at("ab", *((hf, 0) if p else (0, 1))))
                fn(AZ, PS[:, bank_of("az", hf, p), :], ACT.Silu).then_inc(scalar_done, 1)

            def s_xl():
                act.wait_ge(vector_done, vector_at("gr", 1))
                act.dma_start(X[:], x_in).then_inc(x_loaded, 16)
                fn(EPS[:, 2:3], EPS[:, 0:1], ACT.Copy).then_inc(scalar_done, 1)

            def s_pl(layer, n):
                act.wait_ge(tensor_done, tensor_at("pl", layer, n))
                act.wait_ge(vector_done, vector_at(*(("gr", 1) if layer == 0 else ("hr", HGRN_GROUPS - 1))))
                if n == 0:
                    act.dma_start(LNW[:], lnrow[layer].partition_broadcast(P)).then_inc(ln_loaded, 16)
                for c in range(NT):
                    last = fn(PLB[:, c, n * SLAB:(n + 1) * SLAB], PS[:, 2 * n + c, :], ACT.Copy)
                last.then_inc(scalar_done, 1)

            def s_lna(layer):
                act.wait_ge(vector_done, vector_at("lna", layer))
                rsqrt(RSTD[:], AGG[:, :, 1], 1.0, 0).then_inc(scalar_done, 1)

            def s_xt(i, half):
                act.wait_ge(tensor_done, tensor_at("xt", i, half))
                b = bank_of("xt", i, half)
                if i >= 4:
                    for j in range(4):
                        k = 4 * half + j
                        o = PS[:, b + j // 2, (j % 2) * T:(j % 2 + 1) * T]
                        last = fn(o, o, ACT.Identity, scale=MODG[:, i - 4, k:k + 1], bias=MODT[:, 2 * (i - 4), k:k + 1])
                    link(last)
                fn(tiles(XTH, 4 * half, 4), PS[:, b:b + 2, :].rearrange("p b n -> p (b n)"), ACT.Copy).then_inc(scalar_done, 1)

            def s_gate(layer, n, part):
                act.wait_ge(vector_done, vector_at("lnb", layer))
                if n == 0 and layer == 1:
                    act.dma_start(LNW[:], lnrow[2].partition_broadcast(P)).then_inc(ln_loaded, 16)
                    act.dma_start(MSK, msk_in).then_inc(mask_loaded, 16)
                act.wait_ge(tensor_done, tensor_at("gate", layer, n, 1))
                if n:
                    act.wait_ge(vector_done, vector_at("gate", layer, 0, 1))
                fn(flat(GT), PS[:, bank_of("gate", layer, n, 1):bank_of("gate", layer, n, 1) + 2, :]
                          .rearrange("p b n -> p (b n)"), ACT.Sigmoid).then_inc(scalar_done, 1)

            def s_ada(i, part):
                act.wait_ge(tensor_done, tensor_at("ada", i, 1))
                before = [s for s in script[:where[("ada", i, 1)]] if s.kind == "adat"]
                if before:
                    act.wait_ge(tensor_done, tensor_at(*before[-1].name))
                fn(MROW[:], PS[0:1, bank_of("ada", i, 1), :], ACT.Copy).then_inc(scalar_done, 1)

            def s_lb():
                act.wait_ge(vector_done, vector_at("lb"))
                fn(LT1, LT1, ACT.Exp).then_inc(scalar_done, 1)

            def s_f(g, p):
                act.wait_ge(tensor_done, tensor_at("f", g, p))
                if g == 0:
                    act.wait_ge(vector_done, vector_at("gate", 0, 1, 1))
                if g >= 1:
                    act.wait_ge(vector_done, vector_at("hf", g - 1))
                if g >= 2:
                    act.wait_ge(vector_done, vector_at("hr", g - 2))
                    act.wait_ge(gpsimd_done, gpsimd_at("hy", g - 2, NL))
                b = bank_of("f", g, p)
                fn(tiles(FS, 2 * p, 2), PS[:, b, :], ACT.Sigmoid)
                fn(tiles(HK, g % 2 * HG + 2 * p, 2), PS[:, b, :], ACT.Sigmoid, scale=-1.0).then_inc(scalar_done, 1)

            def s_q1(g, p):
                act.wait_ge(tensor_done, tensor_at("q1", g, p))
                if g >= 2:
                    act.wait_ge(vector_done, vector_at("hr", g - 2))
                fn(tiles(HQ, g % 2 * HG + 2 * p, 2), PS[:, bank_of("q1", g, p), :], ACT.Silu).then_inc(scalar_done, 1)

            def s_z1(g, p):
                act.wait_ge(tensor_done, tensor_at("z1", g, p))
                if g:
                    act.wait_ge(vector_done, vector_at("hr", g - 1))
                fn(tiles(HZ, 2 * p, 2), PS[:, bank_of("z1", g, p), :], ACT.Silu).then_inc(scalar_done, 1)

            def s_i(g, part):
                act.wait_ge(tensor_done, tensor_at("i", g, 1))
                b = bank_of("i", g, 1)
                fn(HV[:, g % 2], PS[:, b:b + 2, :], ACT.Copy).then_inc(scalar_done, 1)

            def s_hf(g):
                act.wait_ge(vector_done, vector_at("f", g, 1))
                fn(flat(FS), flat(FS), ACT.Ln).then_inc(scalar_done, 1)

            def s_hx(g, i):
                act.wait_ge(vector_done, vector_at("hx", g, i))
                e = HE[:, i % 2 * HG:(i % 2 + 1) * HG, :]
                if i < NL:
                    s = LEVELS[i]
                    blocks = flat(e).rearrange("p (b s) -> p b s", s=2 * s)
                    fn(blocks[:, :, 0:s], blocks[:, :, 0:s], ACT.Exp, scale=-1.0)
                    fn(blocks[:, :, s:2 * s], blocks[:, :, s:2 * s], ACT.Exp).then_inc(scalar_done, 1)
                    return
                fn(e[:, :, 0:P], e[:, :, 0:P], ACT.Exp, scale=-1.0)
                fn(e[:, :, P:T], HB[:, :, P:T], ACT.Exp).then_inc(scalar_done, 1)

            def s_hc(g):
                act.wait_ge(tensor_done, tensor_at("hc", g))
                fn(flat(HC), PS[:, 2, :], ACT.Copy).then_inc(scalar_done, 1)

            def s_ho(g):
                act.wait_ge(tensor_done, tensor_at("ho", g))
                act.wait_ge(vector_done, vector_at("hy", g, NL))
                act.wait_ge(gpsimd_done, gpsimd_at("hy", g, NL))
                outputs(HOT, HS).then_inc(scalar_done, 1)

            def s_hr(g):
                act.wait_ge(tensor_done, tensor_at("hr", g))
                root(HS, PS[:, 2:4, :]).then_inc(scalar_done, 1)

            def s_rms(i):
                act.wait_ge(vector_done, vector_at(*(("gate", 1, 1, 1) if i == 0 else ("out2", 1, 1))))
                for c in range(NT):
                    last = fn(XN[:, c, :], X[:, c, :], ACT.Square, accum_out=SUMSQ[:, c:c + 1])
                link(last)
                rsqrt(RSTD[:], SUMSQ[:], 1.0 / D, 1).then_inc(scalar_done, 1)

            def s_feat(j):
                b = bank_of("feat", j)
                if j in (3, 4):
                    act.wait_ge(vector_done, vector_at("feat", j))
                    for a in range(2):
                        t = 2 * j + a
                        last = fn(Q2[:, t, :], CV2[:, j % 2, a * T:(a + 1) * T], ACT.Silu, bias=v("mlb", t - QT["mq"]))
                    last.then_inc(scalar_done, 1)
                    return
                act.wait_ge(tensor_done, tensor_at("feat", j))
                if j == 5:
                    fn(tiles(Q2, 2 * j, 2), PS[:, b, :], ACT.Sigmoid).then_inc(scalar_done, 1)
                    return
                if j in (6, 7):
                    act.wait_ge(vector_done, vector_at("qn", 0, j - 6))
                slot = SQ_SLOTS[j // 6][j % 3]
                fn(tiles(Q2, 2 * j, 2), PS[:, b, :], ACT.Copy)
                fn(SQ2[:, slot, :], PS[:, b, :], ACT.Square).then_inc(scalar_done, 1)

            def s_qn(i, b):
                act.wait_ge(tensor_done, tensor_at("qn", i, b))
                rsqrt(SQ2[:, SQ_SLOTS[i][b], :], PS[:, b, :], 1.0 / HD, 1).then_inc(scalar_done, 1)

            def s_ga():
                act.wait_ge(vector_done, vector_at("ga"))
                fn(flat(GB), flat(GB), ACT.Exp).then_inc(scalar_done, 1)

            def s_gb():
                act.wait_ge(vector_done, vector_at("gb"))
                fn(flat(GB), flat(GB), ACT.Ln).then_inc(scalar_done, 1)

            def s_val(n, part):
                act.wait_ge(tensor_done, tensor_at("val", n, 1))
                b = bank_of("val", n, 1)
                fn(V2[:, :, n * SLAB:(n + 1) * SLAB], PS[:, b:b + 2, :], ACT.Copy).then_inc(scalar_done, 1)

            def s_gm():
                act.wait_ge(vector_done, vector_at("gm"))
                for h in range(FOX, FOX + ML):
                    for c in range(NT):
                        fn(B2[:, h, rows(c)], B2[:, h, rows(c)], ACT.Exp, bias=MX[:, h, c:c + 1])
                fn(EM, MX[:, FOX:FOX + ML, :], ACT.Exp).then_inc(scalar_done, 1)

            def s_score(h):
                act.wait_ge(vector_done, vector_at("score", h))
                for c in range(NT):
                    last = fn(SC[:, h % 2, rows(c)], SC[:, h % 2, rows(c)], ACT.Exp, bias=MX[:, h, c:c + 1],
                              accum_out=SM[:, h, c:c + 1])
                last.then_inc(scalar_done, 1)

            def s_turn(h):
                act.wait_ge(tensor_done, tensor_at("turn", h))
                if h >= 2:
                    act.wait_ge(tensor_done, tensor_at("pv", h - 2))
                fn(PTT[:, h % 2, :], PS[:, 2, 0:3 * P], ACT.Copy).then_inc(scalar_done, 1)

            def s_pv(h):
                act.wait_ge(tensor_done, tensor_at("pv", h))
                t = h // 2
                if FOX // 2 <= t < (FOX + ML) // 2:
                    a = t - FOX // 2
                    fn(SQ2[:, 0, a * T:(a + 1) * T], PS[:, 3, 0:T], ACT.Square)
                    fn(YML[:, a, :], PS[:, 3, 0:T], ACT.Copy).then_inc(scalar_done, 1)
                    return
                fn(YH[:, t, :], PS[:, 3, 0:T], ACT.Copy).then_inc(scalar_done, 1)

            def s_mln():
                act.wait_ge(tensor_done, tensor_at("mln"))
                rsqrt(SQ2[:, 1, :], PS[:, 0, :], 1.0 / HD, 1).then_inc(scalar_done, 1)

            def s_ff(j):
                act.wait_ge(tensor_done, tensor_at("ff", j))
                if j >= 2:
                    act.wait_ge(vector_done, vector_at("ff", j - 2))
                fn(SG[:, j % 2, :], PS[:, bank_of("ff", j), 0:T], ACT.Silu).then_inc(scalar_done, 1)

            parts = {"setup": s_setup, "c1": s_c1, "split": s_split, "xs": s_xs, "ba1": s_ba1, "ba2": s_ba2, "k": s_conv("k"),
                     "q": s_conv("q"), "v": s_conv("v"), "gc": s_gc, "norm": s_norm, "gv": s_gv, "gs": s_gs,
                     "go": s_go, "gr": s_gr, "zb": s_zb, "ah": s_ah, "az": s_az, "pl": s_pl, "xl": s_xl, "lna": s_lna,
                     "xt": s_xt, "gate": s_gate, "ada": s_ada, "lb": s_lb, "f": s_f, "q1": s_q1,
                     "z1": s_z1, "i": s_i, "hf": s_hf, "hx": s_hx, "hc": s_hc, "ho": s_ho,
                     "hr": s_hr, "rms": s_rms, "feat": s_feat, "qn": s_qn, "ga": s_ga, "gb": s_gb, "val": s_val,
                     "gm": s_gm, "score": s_score, "turn": s_turn, "pv": s_pv, "mln": s_mln, "ff": s_ff}
            mine = 0
            for step in order["S"]:
                if mine:
                    act.wait_ge(scalar_done, mine)
                parts[step.kind](*step.args)
                mine += 1

        @block.vector
        def _(dve):
            links = [0]

            def link(ins):
                links[0] += 1
                ins.then_inc(vector_link, 1)
                dve.wait_ge(vector_link, links[0])

            tt, ts, stt = dve.tensor_tensor, dve.tensor_scalar, dve.scalar_tensor_tensor

            def conv(acc, src, weight, taps):
                for a in range(2):
                    last = ts(acc[:, a, :], src[:, a, :], weight(a, taps - 1), None, ALU.mult)
                for back in range(1, taps):
                    link(last)
                    for a in range(2):
                        last = stt(acc[:, a, back:T], src[:, a, 0:T - back], weight(a, taps - 1 - back),
                                   acc[:, a, back:T], ALU.mult, ALU.add)
                return last

            def newton(x, y, to, scale, eps, gain=1.0):
                link(stt(x, x, eps / scale, y, ALU.add, ALU.mult))
                link(stt(x, x, -0.5 * scale, y, ALU.mult, ALU.mult))
                link(stt(to, x, 1.5, to, ALU.add, ALU.mult))
                return stt(to, to, gain, y, ALU.mult, ALU.mult)

            def refine(x, y, scale, eps):
                link(ts(x, x, scale, eps, ALU.mult, ALU.add))
                link(tt(x, x, y, ALU.mult))
                link(stt(x, x, -0.5, y, ALU.mult, ALU.mult))
                return stt(y, x, 1.5, y, ALU.add, ALU.mult)

            def banks(b, n):
                return PS[:, b:b + n, :].rearrange("p b n -> p (b n)")

            def two(ap):
                return ap.rearrange("p (a t) -> p a t", a=2)

            def v_setup():
                dve.wait_ge(vec_loaded, 16)
                dve.memset(RSTD[:], 0.0).then_inc(vector_done, 1)

            def v_split(k, i):
                dve.wait_ge(scalar_done, scalar_at("split", k, i))
                n = _width(slabs[i])
                tt(WL[:, k % SPLIT_RING, 0:n], RAW[:, i % RAW_RING, 0:n],
                          as_float(WH[:, k % SPLIT_RING, 0:n]), ALU.subtract).then_inc(vector_done, 1)

            def v_xs():
                dve.wait_ge(scalar_done, scalar_at("xs"))
                tt(flat(XTL[:]), flat(XT0), as_float(flat(XTH[:])), ALU.subtract).then_inc(vector_done, 1)

            def split_y(src, t, n=1):
                h, l = tiles(YH, t, n), tiles(YL, t, n)
                link(dve.tensor_copy(h, src))
                return tt(l, src, as_float(h), ALU.subtract)

            def v_ba():
                dve.wait_ge(tensor_done, tensor_at("ba"))
                for g in range(2):
                    for c in range(NT):
                        o = g * 8 + c * HG
                        dve.tensor_copy(TA[:, o:o + HG], PS[:, 0, c * 16 + g * HG:c * 16 + (g + 1) * HG])
                        last = tt(TD[:, o:o + HG], PS[:, 0, c * 16 + 8 + g * HG:c * 16 + 8 + (g + 1) * HG],
                                  v("dt", g * HG, HG), ALU.add)
                link(last)
                stt(TB, TD, -1.0, TD, ALU.mult, ALU.min).then_inc(vector_done, 1)

            def v_ba1():
                dve.wait_ge(scalar_done, scalar_at("ba1"))
                link(ts(flat(BE), flat(BE), 1.0, None, ALU.add))
                dve.reciprocal(flat(BE), flat(BE))
                ts(TB, TB, 1.0, None, ALU.add).then_inc(vector_done, 1)

            def v_ba2():
                dve.wait_ge(scalar_done, scalar_at("ba2"))
                dve.wait_ge(cst_loaded, 16)
                link(stt(TB, TD, 0.0, TB, ALU.max, ALU.add))
                for g in range(2):
                    for c in range(NT):
                        o = g * 8 + c * HG
                        last = stt(GG[:, g, c * HG:(c + 1) * HG], TB[:, o:o + HG], -1.0, TC[:, g * HG:(g + 1) * HG],
                                   ALU.mult, ALU.mult)
                last.then_inc(vector_done, 1)

            def v_c1():
                dve.wait_ge(scalar_done, scalar_at("c1"))
                tt(SC8[:], SC8[:], v("c", 0, 8), ALU.mult).then_inc(vector_done, 1)

            def v_conv(kind, first):
                def part(g, p):
                    dve.wait_ge(tensor_done, tensor_at(kind, g, p))
                    i = conv_units.index((kind, g, p))
                    if i >= 2:
                        dve.wait_ge(scalar_done, scalar_at(*conv_units[i - 2]))
                    tile = first + g * HG + 2 * p
                    conv(two(CV[:, i % 2, :]), two(PS[:, bank_of(kind, g, p), :]),
                                lambda a, j: v("conv_b", (tile + a) * 4 + j), 4).then_inc(vector_done, 1)
                return part

            def v_gc(g):
                dve.wait_ge(tensor_done, tensor_at("gc", g))
                link(dve.tensor_copy(GCOL, PS[:, 2, 0:8]))
                r = PS[:, 0:2, :].rearrange("p b (h j) -> p (b h) j", h=HG)
                link(tt(DU, r, bc(GCOL, P), ALU.subtract))
                ts(flat(DL), flat(DU), 0.0, None, ALU.max)
                link(dve.tensor_copy(KDF, DU[:, 0:HG, P - 1]))
                ts(flat(DU), flat(DU), 0.0, None, ALU.min).then_inc(vector_done, 1)

            def v_gc2(g):
                dve.wait_ge(scalar_done, scalar_at("gc", g))
                tt(DL, DL, bc(BE[:, g, :], P), ALU.mult)
                stt(DU, DU, SCALE128, rep(triu, 8), ALU.mult, ALU.mult)
                tt(BEG, EGC, BE[:, g, :], ALU.mult).then_inc(vector_done, 1)

            def v_norm(kind, g):
                dve.wait_ge(scalar_done, scalar_at("norm", kind, g))
                newton(banks(bank_of("norm", kind, g), 2), flat(SQ), tiles(KT if kind == "k" else QT0, g * HG, HG),
                              1.0, L2_EPS).then_inc(vector_done, 1)

            def heads4(bank):
                return PS[:, bank, :].rearrange("p (h j) -> p h j", h=HG)

            def heads8(bank):
                return PS[:, bank:bank + 2, :].rearrange("p b (h j) -> p (b h) j", h=HG)

            def v_vtr(g):
                dve.wait_ge(tensor_done, tensor_at("vtr", g))
                tt(BV, heads8(0), bc(BE[:, g, :], P), ALU.mult).then_inc(vector_done, 1)

            def v_gk(g):
                dve.wait_ge(tensor_done, tensor_at("gk", g))
                dve.wait_ge(scalar_done, scalar_at("gc", g))
                tt(KD, heads4(2), bc(KDF, P), ALU.mult).then_inc(vector_done, 1)

            def v_gkk(g):
                dve.wait_ge(tensor_done, tensor_at("gkk", g))
                tt(DL, heads8(0), DL, ALU.mult)
                tt(DU, heads8(2), DU, ALU.mult)
                q = QT0[:, g * HG:(g + 1) * HG, P:T]
                stt(q, q, SCALE128, ER, ALU.mult, ALU.mult).then_inc(vector_done, 1)

            def v_gp(g, i, c):
                dve.wait_ge(tensor_done, tensor_at("gp", g, i, c))
                tt(PM[:, c * HG:(c + 1) * HG, :], heads4(c), rep(lvl[i], HG), ALU.mult).then_inc(vector_done, 1)

            def v_gu(g, i, c):
                dve.wait_ge(tensor_done, tensor_at("gu", g, i, c))
                u, xi, pm = (x[:, c * HG:(c + 1) * HG, :] for x in (U, XI, PM))
                if i == 0:
                    tt(u, rep(ident, HG), pm, ALU.subtract)
                    tt(xi, rep(ident, HG), heads4(c), ALU.subtract).then_inc(vector_done, 1)
                    return
                last = tt(u, u, heads4(2 + c), ALU.subtract)
                if i < NL - 1:
                    last = tt(xi, xi, heads4(c), ALU.subtract)
                last.then_inc(vector_done, 1)

            def v_gks(g):
                dve.wait_ge(tensor_done, tensor_at("gks", g))
                link(tt(PM[:, 0:HG, :], heads4(2), bc(BEG[:, HG:2 * HG], P), ALU.mult))
                tt(BV[:, HG:2 * HG, :], BV[:, HG:2 * HG, :], PM[:, 0:HG, :], ALU.subtract).then_inc(vector_done, 1)

            def gated(o, r, gain, z, t):
                link(newton(banks(2, 2), flat(r), flat(o), 1.0 / P, LN_EPS, gain))
                link(tt(flat(o), flat(o), z, ALU.mult))
                return split_y(flat(o), t, HG)

            def v_gr(g):
                dve.wait_ge(scalar_done, scalar_at("gr", g))
                dve.wait_ge(scalar_done, scalar_at("zb", g, 1))
                gated(OT, RO, v("gdn_g"), flat(ZB), KC + g * HG).then_inc(vector_done, 1)

            def v_ac(hf, p):
                dve.wait_ge(tensor_done, tensor_at("ac", hf, p))
                dve.wait_ge(scalar_done, scalar_at("ah", hf, p))
                link(tt(AH, AH, PS[:, bank_of("ac", hf, p), :], ALU.mult))
                conv(two(AC), two(AH), lambda a, j: v("conv_a", (hf * HG + 2 * p + a) * 3 + j), 3).then_inc(vector_done, 1)

            def v_ab(hf, p):
                dve.wait_ge(tensor_done, tensor_at("ab", hf, p))
                dve.wait_ge(scalar_done, scalar_at("az", hf, p))
                link(tt(AC, AC, PS[:, bank_of("ab", hf, p), :], ALU.mult))
                link(tt(AC, AC, AZ, ALU.mult))
                split_y(AC, hf * HG + 2 * p, 2).then_inc(vector_done, 1)

            def v_out(layer, n, part):
                dve.wait_ge(tensor_done, tensor_at("out", layer, n, 3))
                if layer == 0 and n == 0:
                    dve.wait_ge(x_loaded, 32)
                for c in range(NT):
                    x = X[:, c, n * SLAB:(n + 1) * SLAB]
                    last = stt(x, x, ALPHA, PS[:, bank_of("out", layer, n, 3) + c, :], ALU.mult, ALU.add)
                last.then_inc(vector_done, 1)

            def v_lna(layer):
                for c in range(NT):
                    for n in range(2):
                        last = dve.bn_stats(STAT[:, c, n, :], X[:, c, n * SLAB:(n + 1) * SLAB])
                link(last)
                for c in range(NT):
                    last = dve.bn_aggr(AGG[:, c, :], STAT[:, c, :, :])
                last.then_inc(vector_done, 1)

            def v_lnb(layer):
                dve.wait_ge(scalar_done, scalar_at("lna", layer))
                link(refine(AGG[:, :, 1], RSTD[:], 1.0, LN_EPS))
                dve.wait_ge(ln_loaded, 16 * (layer + 1))
                for c in range(NT):
                    last = stt(X[:, c, :], X[:, c, :], AGG[:, c, 0:1], LNW[:, 0, :], ALU.subtract, ALU.mult)
                link(last)
                for c in range(NT):
                    last = stt(X[:, c, :], X[:, c, :], RSTD[:, c:c + 1], LNW[:, 1, :], ALU.mult, ALU.add)
                last.then_inc(vector_done, 1)

            def v_xt(i, half):
                dve.wait_ge(scalar_done, scalar_at("xt", i, half))
                b = bank_of("xt", i, half)
                tt(tiles(XTL, 4 * half, 4), PS[:, b:b + 2, :].rearrange("p b n -> p (b n)"),
                          as_float(tiles(XTH, 4 * half, 4)), ALU.subtract).then_inc(vector_done, 1)

            def v_gate(layer, n, part):
                dve.wait_ge(scalar_done, scalar_at("gate", layer, n, 1))
                dve.wait_ge(scalar_done, scalar_at("pl", layer, n))
                s = slice(n * SLAB, (n + 1) * SLAB)
                link(tt(GT, GT, PLB[:, :, s], ALU.mult))
                tt(X[:, :, s], X[:, :, s], GT, ALU.add).then_inc(vector_done, 1)

            def v_adat(i):
                dve.wait_ge(tensor_done, tensor_at("adat", i))
                b = bank_of("adat", i)
                if MOD_ROW[i] is None:
                    dve.wait_ge(ln_loaded, 48)
                    g = LNW[:, i // 6, (i % 2) * SLAB:(i % 2 + 1) * SLAB]
                    tt(g, g, PS[:, b, :], ALU.add).then_inc(vector_done, 1)
                    return
                r, o = MOD_ROW[i], (i % 2) * 4
                tt(MODT[:, r, o:o + 4], PS[:, b, 0:4], v("bada", r * KC + o, 4), ALU.add).then_inc(vector_done, 1)

            def v_mod(i):
                stt(MODG[:, i, :], MODT[:, 2 * i + 1, :], 1.0, v("n1" if i == 0 else "n2", 0, KC),
                           ALU.add, ALU.mult).then_inc(vector_done, 1)

            def v_lb():
                link(tt(LT2, v("lb", 0, 16), v("lb", 16, 16), ALU.max))
                tt(LT1[:, 0:16], v("lb", 0, 16), LT2, ALU.subtract)
                tt(LT1[:, 16:32], v("lb", 16, 16), LT2, ALU.subtract).then_inc(vector_done, 1)

            def v_lb2():
                dve.wait_ge(scalar_done, scalar_at("lb"))
                link(tt(LT2, LT1[:, 0:16], LT1[:, 16:32], ALU.add))
                link(dve.reciprocal(LT2, LT2))
                link(tt(LBV, LT1[:, 16:32], LT2, ALU.mult))
                ts(OML, LBV, -1.0, 1.0, ALU.mult, ALU.add).then_inc(vector_done, 1)

            def v_f(g, p):
                dve.wait_ge(scalar_done, scalar_at("f", g, p))
                for a in range(2):
                    t, h = g * HG + 2 * p + a, 2 * p + a
                    ts(FS[:, h, :], FS[:, h, :], OML[:, t:t + 1], LBV[:, t:t + 1], ALU.mult, ALU.add)
                    k = HK[:, g % 2 * HG + h, :]
                    last = ts(k, k, OML[:, t:t + 1], None, ALU.mult)
                last.then_inc(vector_done, 1)

            def v_hf(g):
                dve.wait_ge(scalar_done, scalar_at("hf", g))
                for h in range(HG):
                    for c in range(NT):
                        s = slice(c * P, (c + 1) * P)
                        last = dve.tensor_tensor_scan(HB[:, h, s], ONES[:], FS[:, h, s], 0.0,
                                                      ALU.mult, ALU.add)
                last.then_inc(vector_done, 1)

            def v_hd(g):
                dve.wait_ge(tensor_done, tensor_at("hd", g))
                if g:
                    dve.wait_ge(tensor_done, tensor_at("ho", g - 1))
                tt(HA, heads8(0), rep(ident, 8), ALU.mult).then_inc(vector_done, 1)

            def v_hx(g, i):
                if i >= 2:
                    dve.wait_ge(gpsimd_done, gpsimd_at("hy", g, i - 2))
                elif g:
                    dve.wait_ge(gpsimd_done, gpsimd_at("hy", g - 1, NL - 1 + i))
                b = HB
                e = HE[:, i % 2 * HG:(i % 2 + 1) * HG, :]
                if i == NL:
                    tt(e[:, :, 0:P], b[:, :, 0:P], b[:, :, P - 1:P].to_broadcast([P, HG, P]), ALU.subtract).then_inc(vector_done, 1)
                    return
                s = LEVELS[i]
                n = HG * T // (2 * s)
                b3 = flat(b).rearrange("p (b s) -> p b s", s=2 * s)
                e3 = flat(e).rearrange("p (b s) -> p b s", s=2 * s)
                tt(e3, b3, b3[:, :, s - 1:s].to_broadcast([P, n, 2 * s]), ALU.subtract).then_inc(vector_done, 1)

            def v_hy(g, i):
                dve.wait_ge(scalar_done, scalar_at("hx", g, i))
                dve.wait_ge(scalar_done, scalar_at("q1", g, 1))
                if i >= 2:
                    dve.wait_ge(tensor_done, tensor_at("hm", g, i - 2))
                elif i == 0 and g:
                    dve.wait_ge(tensor_done, tensor_at("hm", g - 1, NL - 1))
                r = slice(i % 2 * HG, (i % 2 + 1) * HG)
                q = HQ[:, g % 2 * HG:(g % 2 + 1) * HG, :]
                if i == NL:
                    tt(HX[:, r, P:T], q[:, :, P:T], HE[:, r, P:T], ALU.mult).then_inc(vector_done, 1)
                    return
                s = LEVELS[i]
                x, e, y = (flat(a).rearrange("p (b s) -> p b s", s=2 * s)[:, :, s:2 * s]
                           for a in (HX[:, r, :], HE[:, r, :], q))
                tt(x, y, e, ALU.mult).then_inc(vector_done, 1)

            def v_hp(g, i):
                dve.wait_ge(tensor_done, tensor_at("hm", g, i))
                dve.copy_predicated(HA, rep(lvl[i].bitcast(U32), 8), heads8(script[where[("hm", g, i)]].banks[0])).then_inc(vector_done, 1)

            def v_hr(g):
                dve.wait_ge(scalar_done, scalar_at("hr", g))
                dve.wait_ge(scalar_done, scalar_at("z1", g, 1))
                gated(HOT, HS, v("hgrn_g"), flat(HZ), g * HG).then_inc(vector_done, 1)

            def v_rmsb(i):
                dve.wait_ge(scalar_done, scalar_at("rms", i))
                link(refine(SUMSQ[:], RSTD[:], 1.0 / D, RMS_EPS))
                for c in range(NT):
                    last = ts(XN[:, c, :], X[:, c, :], RSTD[:, c:c + 1], None, ALU.mult)
                last.then_inc(vector_done, 1)

            def v_wg():
                dve.wait_ge(small_loaded, 32)
                h, l = flat(WGH[:]), flat(WGL[:])
                link(dve.tensor_copy(h, WGA[:]))
                tt(l, WGA[:], as_float(h), ALU.subtract).then_inc(vector_done, 1)

            def v_gates(c):
                dve.wait_ge(tensor_done, tensor_at("gates", c))
                tt(GA[:, c, :], PS[:, bank_of("gates", c), 0:NG], v("gate_bias", 0, NG), ALU.add).then_inc(vector_done, 1)

            def v_ga():
                stt(flat(GB), flat(GA), -1.0, flat(GA), ALU.mult, ALU.min).then_inc(vector_done, 1)

            def v_gb():
                dve.wait_ge(scalar_done, scalar_at("ga"))
                ts(flat(GB), flat(GB), 1.0, None, ALU.add).then_inc(vector_done, 1)

            def v_gd():
                dve.wait_ge(scalar_done, scalar_at("gb"))
                link(stt(flat(NLS), flat(GA), 0.0, flat(GB), ALU.min, ALU.subtract))
                ts(flat(NLS), flat(NLS), -1.0, None, ALU.mult).then_inc(vector_done, 1)

            def spread(eng, lnk, c, tmp):
                eng.tensor_tensor(GSP[c][:, 0:FOX, :], rep(triu, FOX), bc(NLS[:, c, 0:FOX], P), ALU.mult)
                eng.tensor_tensor(GSP[c][:, FOX:FOX + ML, :], rep(triu, ML), bc(NLS[:, c, FOX + ML:NG], P), ALU.mult)
                lnk(eng.tensor_tensor(tmp, rep(ident, ML), bc(GA[:, c, FOX:FOX + ML], P), ALU.mult))
                o = GSP[c][:, FOX:FOX + ML, :]
                return eng.tensor_tensor(o, o, tmp, ALU.add)

            def v_gsp():
                spread(dve, link, 1, V2[:, 1, 0:ML * P].rearrange("p (h k) -> p h k", h=ML)).then_inc(vector_done, 1)

            def v_gcol():
                dve.wait_ge(tensor_done, tensor_at("gcol"))
                dve.wait_ge(mask_loaded, 16)
                ts(flat(GCC), PS[:, 3, 0:2 * NG], -1.0, None, ALU.mult).then_inc(vector_done, 1)

            def v_grow(part):
                dve.wait_ge(tensor_done, tensor_at("grow", part))
                for j in range(FOX) if part == 0 else range(FOX, FOX + ML):
                    b, o = (j - (0 if part == 0 else FOX)) // 2, (j % 2) * T
                    for c in range(NT):
                        last = stt(B2[:, j, rows(c)], PS[:, b, o:o + (c + 1) * P], GCC[:, c, gate_of(j):gate_of(j) + 1],
                                   mask3[:, rows(c)], ALU.add, ALU.add)
                last.then_inc(vector_done, 1)

            def v_gm():
                for h in range(FOX, FOX + ML):
                    for c in range(NT):
                        last = dve.tensor_reduce(MX[:, h, c:c + 1], B2[:, h, rows(c)], AX.X, ALU.max)
                link(last)
                for h in range(FOX, FOX + ML):
                    last = tt(MX[:, h, :], MX[:, h, :], GCC[:, :, gate_of(h)], ALU.max)
                link(last)
                ts(MX[:, FOX:FOX + ML, :], MX[:, FOX:FOX + ML, :], -1.0, None, ALU.mult).then_inc(vector_done, 1)

            def v_feat(j):
                dve.wait_ge(tensor_done, tensor_at("feat", j))
                conv(two(CV2[:, j % 2, :]), two(PS[:, bank_of("feat", j), :]),
                            lambda a, k: v("mlw", (2 * j - QT["mq"] + a) * 4 + k), 4).then_inc(vector_done, 1)

            def v_qn(i, b):
                dve.wait_ge(scalar_done, scalar_at("qn", i, b))
                for a in range(2):
                    n = 2 * b + a
                    t = n + (0 if i == 0 else QT["bq"])
                    gain = v((("foxq", "foxk"), ("mobaq", "mobak"))[i][n // 3])
                    last = newton(PS[:, b, a * T:(a + 1) * T], SQ2[:, SQ_SLOTS[i][b], a * T:(a + 1) * T], Q2[:, t, :],
                                  1.0 / HD, L2_EPS, gain)
                last.then_inc(vector_done, 1)

            def v_mb():
                for i in range(MOBA):
                    slope = 2.0 ** (-8.0 * (i + 1) / MOBA)
                    last = stt(B2[:, FOX + ML + i, :], dist3, slope, mask3, ALU.mult, ALU.add)
                last.then_inc(vector_done, 1)

            def v_score(h):
                dve.wait_ge(tensor_done, tensor_at("score", h))
                dve.wait_ge(scalar_done, scalar_at("gm"))
                if h >= 2:
                    dve.wait_ge(tensor_done, tensor_at("turn", h - 2))
                b = PS[:, bank_of("score", h), 0:3 * P]
                s = SC[:, h % 2, :]
                if FOX <= h < FOX + ML:
                    for c in range(NT):
                        last = stt(s[:, rows(c)], b[:, rows(c)], SCALE64, B2[:, h, rows(c)], ALU.mult, ALU.mult,
                                   accum_out=SM[:, h, c:c + 1])
                    last.then_inc(vector_done, 1)
                    return
                link(stt(s, b, SCALE64, B2[:, h, :], ALU.mult, ALU.add))
                for c in range(NT):
                    last = dve.tensor_reduce(MX[:, h, c:c + 1], s[:, rows(c)], AX.X, ALU.max, negate=True)
                last.then_inc(vector_done, 1)

            def v_ratio(h):
                if FOX <= h < FOX + ML:
                    link(stt(RI[:, h, :], SM[:, h, :], -1.0, SM[:, h, :], ALU.mult, ALU.max))
                    link(tt(RI[:, h, :], RI[:, h, :], EM[:, h - FOX, :], ALU.max))
                    link(dve.reciprocal(RI[:, h, :], RI[:, h, :]))
                else:
                    dve.wait_ge(scalar_done, scalar_at("score", h))
                    link(dve.reciprocal(RI[:, h, :], SM[:, h, :]))
                s = SC[:, h % 2, :]
                for c in range(NT):
                    last = ts(s[:, rows(c)], s[:, rows(c)], RI[:, h, c:c + 1], None, ALU.mult)
                last.then_inc(vector_done, 1)

            def v_mln():
                dve.wait_ge(scalar_done, scalar_at("mln"))
                link(newton(PS[:, 0, :], SQ2[:, 1, :], flat(YML), 1.0 / HD, L2_EPS))
                for a in range(2):
                    last = stt(YML[:, a, :], YML[:, a, :], v("mlg", a), Q2[:, QT["mo"] + a, :], ALU.mult, ALU.mult)
                link(last)
                split_y(flat(YML), FOX // 2, 2).then_inc(vector_done, 1)

            def v_pv(h):
                dve.wait_ge(scalar_done, scalar_at("pv", h))
                tt(YL[:, h // 2, :], PS[:, 3, 0:T], as_float(YH[:, h // 2, :]), ALU.subtract).then_inc(vector_done, 1)

            def residual(name, n, gain, tmp):
                b = bank_of(name, n, 0)
                s = slice(n * SLAB, (n + 1) * SLAB)
                for c in range(NT):
                    last = tt(tmp[:, c, s], PS[:, b + c, :], LNW[:, gain, s], ALU.mult)
                link(last)
                return tt(X[:, :, s], X[:, :, s], tmp[:, :, s], ALU.add)

            def v_out2(n, part):
                dve.wait_ge(tensor_done, tensor_at("out2", n, 1))
                residual("out2", n, 0, XN).then_inc(vector_done, 1)

            def v_down(n, part):
                dve.wait_ge(tensor_done, tensor_at("down", n, 5))
                residual("down", n, 1, XR).then_inc(vector_done, 1)

            def v_ff(j):
                dve.wait_ge(scalar_done, scalar_at("ff", j))
                link(tt(HT[:, j % 2, :], SG[:, j % 2, :], PS[:, bank_of("ff", j), T:2 * T], ALU.mult))
                h, l = y_tile(j)
                link(dve.tensor_copy(h, HT[:, j % 2, :]))
                tt(l, HT[:, j % 2, :], as_float(h), ALU.subtract).then_inc(vector_done, 1)

            parts = {"setup": v_setup, "split": v_split, "xs": v_xs, "wg": v_wg, "pv": v_pv, "ba": v_ba, "ba1": v_ba1, "ba2": v_ba2, "c1": v_c1, "k": v_conv("k", 8), "q": v_conv("q", 0),
                     "v": v_conv("v", 16), "gc": v_gc, "gc2": v_gc2, "norm": v_norm, "vtr": v_vtr, "gk": v_gk,
                     "gkk": v_gkk, "gp": v_gp, "gu": v_gu, "gks": v_gks, "gr": v_gr, "ac": v_ac, "ab": v_ab,
                     "out": v_out, "lna": v_lna, "lnb": v_lnb, "xt": v_xt, "gate": v_gate,
                     "adat": v_adat, "mod": v_mod, "lb": v_lb, "lb2": v_lb2, "f": v_f, "hf": v_hf, "hd": v_hd,
                     "hx": v_hx, "hy": v_hy, "hp": v_hp, "hr": v_hr, "rmsb": v_rmsb, "gates": v_gates,
                     "ga": v_ga, "gb": v_gb, "gd": v_gd, "gsp": v_gsp, "gcol": v_gcol, "grow": v_grow, "gm": v_gm,
                     "feat": v_feat, "qn": v_qn, "mb": v_mb, "score": v_score, "ratio": v_ratio, "mln": v_mln,
                     "out2": v_out2, "down": v_down, "ff": v_ff}
            dve.wait_ge(gpsimd_done, gpsimd_at("setup"))
            mine = 0
            for step in order["V"]:
                if mine:
                    dve.wait_ge(vector_done, mine)
                parts[step.kind](*step.args)
                mine += 1

        @block.gpsimd
        def _(pool):
            links = [0]

            def link(ins):
                links[0] += 1
                ins.then_inc(gpsimd_link, 1)
                pool.wait_ge(gpsimd_link, links[0])

            tt = pool.tensor_tensor

            def g_setup():
                pool.memset(ONES[:], 1.0)
                pool.memset(EPS[:, 0:1], LN_EPS)
                pool.memset(EPS[:, 1:2], L2_EPS).then_inc(gpsimd_done, 1)

            def g_gt(g):
                pool.wait_ge(cst_loaded, 16)
                pool.wait_ge(vector_done, vector_at("ba2"))
                if g:
                    pool.wait_ge(vector_done, vector_at("gr", 0))
                tt(PM, rep(triu, 8), bc(GG[:, g, :], P), ALU.mult).then_inc(gpsimd_done, 1)

            def g_hy(g, i):
                pool.wait_ge(scalar_done, scalar_at("hx", g, i))
                if i >= 2:
                    pool.wait_ge(tensor_done, tensor_at("hm", g, i - 2))
                elif g and i:
                    pool.wait_ge(vector_done, vector_at("hr", g - 1))
                elif g:
                    pool.wait_ge(tensor_done, tensor_at("hm", g - 1, NL - 1))
                r = slice(i % 2 * HG, (i % 2 + 1) * HG)
                k = HK[:, g % 2 * HG:(g % 2 + 1) * HG, :]
                if i == NL:
                    tt(HX[:, r, 0:P], k[:, :, 0:P], HE[:, r, 0:P], ALU.mult).then_inc(gpsimd_done, 1)
                    return
                s = LEVELS[i]
                x, e, y = (flat(a).rearrange("p (b s) -> p b s", s=2 * s)[:, :, 0:s]
                           for a in (HX[:, r, :], HE[:, r, :], k))
                tt(x, y, e, ALU.mult).then_inc(gpsimd_done, 1)

            def g_gsp():
                pool.wait_ge(vector_done, vector_at("gd"))
                tmp = V2[:, 0, 0:ML * P].rearrange("p (h k) -> p h k", h=ML)
                tt(GSP[0][:, 0:FOX, :], rep(triu, FOX), bc(NLS[:, 0, 0:FOX], P), ALU.mult)
                tt(GSP[0][:, FOX:FOX + ML, :], rep(triu, ML), bc(NLS[:, 0, FOX + ML:NG], P), ALU.mult)
                link(tt(tmp, rep(ident, ML), bc(GA[:, 0, FOX:FOX + ML], P), ALU.mult))
                o = GSP[0][:, FOX:FOX + ML, :]
                tt(o, o, tmp, ALU.add).then_inc(gpsimd_done, 1)

            parts = {"setup": g_setup, "gt": g_gt, "hy": g_hy, "gsp": g_gsp}
            mine = 0
            for step in order["G"]:
                if mine:
                    pool.wait_ge(gpsimd_done, mine)
                parts[step.kind](*step.args)
                mine += 1


def _blocks(w):
    return w.reshape(w.shape[0] // P, P, w.shape[1]).transpose(1, 0, 2)


def _slab(name, w):
    kind, a = name[0], name[1:]
    narrow = {"q": ("even", 4096), "k": ("even", 5120), "v": ("even", 6144), "zb": ("even", 7168),
              "ah": ("even", 0), "ac": ("even", 1024), "ab": ("even", 2048), "az": ("even", 3072),
              "q1": ("odd", 0), "f": ("odd", 2048), "z1": ("odd", 6144)}
    if kind in narrow:
        which, at = narrow[kind]
        at += a[0] * SLAB + a[1] * 2 * P
        s = _blocks(w[which][:, at:at + 2 * P])
    elif kind in ("feat", "ff"):
        s = _blocks(w[kind][:, a[0] * 2 * P:(a[0] + 1) * 2 * P])
    elif kind == "pl":
        s = _blocks(w["pl"][a[0]])
    else:
        m, n, part = {"i": (w["odd"][:, 4096:6144], a[0], a[-1]), "out": (w["out"][a[0] % 2], a[1 % len(a)], a[-1]),
                      "gate": (w["gate"][a[0] % 2], a[1 % len(a)], a[-1])}.get(kind) or (w[kind], a[0], a[-1])
        s = _blocks(m[part * 4 * P:(part + 1) * 4 * P, n * SLAB:(n + 1) * SLAB])
    s = s.reshape(P, -1)
    return np.pad(s, ((0, 0), (0, HALF - s.shape[1])))


def _width(name):
    return (FF % 4) * SLAB if name[0] == "down" and name[2] == FF // 4 else HALF


def _columns(x):
    return x.reshape(-1, P).T


def _constants():
    i, j = np.arange(P)[:, None], np.arange(P)[None, :]
    parts = [i == j, i <= j, i // HD == j // HD]
    parts += [(i // (2 * s) == j // (2 * s)) & (i // s < j // s) for s in LEVELS]
    k = np.concatenate([np.arange(P), np.arange(T)])[None, :]
    q = i + np.concatenate([np.zeros(P), np.full(T, P)])[None, :]
    return (np.concatenate([np.asarray(x, np.float32) for x in parts], axis=1),
            np.stack([np.where(k <= q, 0.0, NEG), k - q], axis=1).astype(np.float32))


def kernel(**inputs):
    import concourse.bacc as _bacc
    from concourse.bass_utils import run_bass_kernel_spmd as _run

    z = {n: np.asarray(a) for n, a in inputs.items()}
    _, slabs = plan(STAGE)
    w2 = z["w_in_2"][0]
    fx, mw = FOX * HD, ML * HD
    at = np.cumsum([0, fx, fx, fx, FOX, mw, mw, mw, ML, ML, mw, fx, fx, fx])
    fq, fk, fv, ff, mq, mk, mv, mi, mf, mo, bq, bk, bv = (w2[:, a:b] for a, b in zip(at[:-1], at[1:]))
    feat = np.concatenate([fq, fk, mq, mk, mo, bq, bk], axis=1)
    gu = z["w_gate_up_2"][0].reshape(D, 2, FF, P).transpose(0, 2, 1, 3).reshape(D, 2 * D_FF)
    w = {"even": z["w_in_even"][0], "odd": z["w_in_odd"][0], "out": [z["w_out_even"][0], z["w_out_odd"][0]],
         "pl": z["w_pl"], "gate": z["w_pl_gate"], "ada": z["w_ada_2"][0], "feat": feat,
         "val": np.concatenate([fv, mv, bv], axis=1), "out2": z["w_out_2"][0], "ff": gu, "down": z["w_down_2"][0]}
    x, p = z["x"][0], z["p"][:, 0]
    bada = z["b_ada_2"][0].reshape(6, D)
    lane = lambda a: np.broadcast_to(a.reshape(1, -1), (P, a.size))
    twice = lambda a: np.concatenate([a, a]).reshape(P, 1)
    taps = lambda a: a.reshape(a.shape[0], -1, P).transpose(2, 1, 0).reshape(P, -1)
    vec = {"conv_b": taps(z["conv_b_w"][0]), "conv_a": taps(z["conv_a_w"][0]), "gdn_g": _columns(z["gdn_norm_g"][0]),
           "hgrn_g": _columns(z["hgrn_norm_g"][0]), "lb": _columns(z["lower_bounds"].reshape(-1)),
           "n1": _columns(z["norm1_g_2"][0]), "n2": _columns(z["norm2_g_2"][0]), "mlw": taps(z["ml_conv_w_2"][0]),
           "mlb": _columns(z["ml_conv_b_2"][0]), "mlg": _columns(z["ml_h_g_2"][0]),
           "bada": np.concatenate([_columns(bada[i]) for i in (0, 1, 3, 4)], axis=1), "c": _columns(z["c_2"][0]),
           "foxq": twice(z["fox_q_g_2"][0]), "foxk": twice(z["fox_k_g_2"][0]), "mobaq": twice(z["moba_q_g_2"][0]),
           "mobak": twice(z["moba_k_g_2"][0]), "a_log": lane(z["a_log"]), "dt": lane(z["dt_bias"]),
           "gate_bias": lane(np.concatenate([z["fox_f_bias_2"][0], z["ml_i_bias_2"][0], z["ml_f_bias_2"][0]]))}
    arrays = {
        "wst": np.stack([_slab(s, w) for s in slabs]),
        "x": x.reshape(NT, P, D).transpose(1, 0, 2),
        "xt": _blocks(x.T),
        "pt": p.transpose(0, 2, 1).reshape(2, 2, P, T).transpose(2, 0, 1, 3),
        "wba": _blocks(z["w_in_even"][0][:, 8192:8208]),
        "wga": _blocks(np.concatenate([ff, mi, mf], axis=1)).reshape(P, -1),
        "cst": _constants()[0],
        "msk": _constants()[1],
        "vec": np.concatenate([vec[n] for n, _ in _SIZES], axis=1),
        "lnrow": np.stack([np.stack([z["ln_g"][0], z["ln_b"][0]]), np.stack([z["ln_g"][1], z["ln_b"][1]]),
                           np.stack([bada[2], bada[5]])]),
    }
    nc = _bacc.Bacc("TRN2", target_bir_lowering=False, num_devices=1)
    arrays = {n: np.ascontiguousarray(a) for n, a in arrays.items()}
    args = [nc.dram_tensor(n, a.shape, F32, kind="ExternalInput").ap() for n, a in arrays.items()]
    out = nc.dram_tensor("out", (P, NT, D), F32, kind="ExternalOutput").ap()
    build(nc, *args, out)
    got = _run(nc, [arrays], core_ids=[0]).results[0]["out"]
    return np.asarray(got).transpose(1, 0, 2).reshape(1, T, D)
```
